# Optimizing a Trainium2 kernel written in Bass

```python
import math
import jax
import jax.numpy as jnp
from jax import lax
import numpy as np

D_MODEL = 1024
BATCH = 1
SEQ = 256
DEPTH = 2

MEM_LEN = 256
HEAD_DIM = 64
D_MIX = D_MODEL
RET_WIDTH = 3 * D_MIX // 8
SSD_WIDTH = 3 * D_MIX // 8
LRU_WIDTH = D_MIX - RET_WIDTH - SSD_WIDTH
RET_HEADS = RET_WIDTH // HEAD_DIM
SSD_HEADS = SSD_WIDTH // HEAD_DIM
SSD_GROUPS = 2
SSD_HEADS_PER_GROUP = SSD_HEADS // SSD_GROUPS
SSD_STATE = 128
SSD_CONV_DIM = SSD_WIDTH + 2 * SSD_GROUPS * SSD_STATE
LRU_BLOCKS = LRU_WIDTH // HEAD_DIM
LRU_C = 8.0
CONV_WIDTH = 4
CHUNK = 128
ROPE_BASE = 10000.0
CA_HEADS = 4
CA_HEAD_DIM = D_MODEL // CA_HEADS
N_GROUPS = 4
EXPERTS_PER_GROUP = 8
N_EXPERTS = N_GROUPS * EXPERTS_PER_GROUP
TOP_K = 2
D_EXPERT = D_MODEL // 2
MOE_BLOCK = 128
EPS = 1e-6
IN_SPLITS = (RET_WIDTH, RET_WIDTH, RET_WIDTH, RET_WIDTH, SSD_WIDTH, SSD_CONV_DIM, SSD_HEADS, LRU_WIDTH, LRU_WIDTH)
D_IN = sum(IN_SPLITS)
SPLIT_POINTS = tuple(int(p) for p in np.cumsum(IN_SPLITS)[:-1])

kernel_name = 'hybrid_ret_ssd_rglru_xattn_hmoe_encoder'

def rms_norm(x, g):
    xf = x.astype(jnp.float32)
    y = xf * lax.rsqrt(jnp.mean(xf * xf, axis=-1, keepdims=True) + EPS)
    return (y * g.astype(jnp.float32)).astype(x.dtype)

def _rev(t):
    return jnp.flip(t, axis=1)

def centred_dwconv(x, w, b):
    k = w.shape[0]
    left = k // 2
    y = lax.conv_general_dilated(x, w[:, None, :].astype(x.dtype), window_strides=(1,),
                                 padding=[(left, k - 1 - left)],
                                 dimension_numbers=('NWC', 'WIO', 'NWC'),
                                 feature_group_count=x.shape[-1])
    return y + b.astype(y.dtype)

def rotary(x):
    s, dh = x.shape[1], x.shape[-1]
    half = dh // 2
    inv = ROPE_BASE ** (-jnp.arange(half, dtype=jnp.float32) / half)
    ang = jnp.arange(s, dtype=jnp.float32)[:, None] * inv[None, :]
    cos = jnp.cos(ang)[:, None, :]
    sin = jnp.sin(ang)[:, None, :]
    x1 = x[..., :half].astype(jnp.float32)
    x2 = x[..., half:].astype(jnp.float32)
    return jnp.concatenate([x1 * cos - x2 * sin, x1 * sin + x2 * cos], axis=-1)

def _retention_causal(q, k, v, log_gamma, strict):
    b, s, h, dh = q.shape
    n = s // CHUNK
    q = q.reshape(b, n, CHUNK, h, dh)
    k = k.reshape(b, n, CHUNK, h, dh)
    v = v.reshape(b, n, CHUNK, h, v.shape[-1])
    idx = jnp.arange(CHUNK)
    diff = (idx[:, None] - idx[None, :]).astype(jnp.float32)
    mask = diff > 0 if strict else diff >= 0
    decay = jnp.where(mask, jnp.exp(jnp.where(mask, diff, 0.0)[None] * log_gamma[:, None, None]), 0.0)
    scores = jnp.einsum('bnihd,bnjhd->bnhij', q, k) * decay
    inner = jnp.einsum('bnhij,bnjhe->bnihe', scores, v)
    pos = idx.astype(jnp.float32)[:, None]
    zeta = jnp.exp((CHUNK - 1 - pos) * log_gamma)
    xi = jnp.exp((pos + 1) * log_gamma)
    states = jnp.einsum('bnjhd,jh,bnjhe->bnhde', k, zeta, v)
    chunk_decay = jnp.exp(CHUNK * log_gamma)[:, None, None]

    def step(r, st):
        return r * chunk_decay + st, r

    _, r_prev = lax.scan(step, jnp.zeros_like(states[:, 0]), jnp.moveaxis(states, 1, 0))
    r_prev = jnp.moveaxis(r_prev, 0, 1)
    cross = jnp.einsum('bnihd,bnhde->bnihe', q, r_prev) * xi[None, None, :, :, None]
    return (inner + cross).reshape(b, s, h, -1)

def retention_mixer(q, k, v, g):
    b, s, _ = q.shape
    shp = (b, s, RET_HEADS, HEAD_DIM)
    q = rotary(q.reshape(shp))
    k = rotary(k.reshape(shp)) * HEAD_DIM ** -0.5
    v = v.reshape(shp).astype(jnp.float32)
    log_gamma = jnp.log1p(-jnp.exp2(-5.0 - jnp.arange(RET_HEADS, dtype=jnp.float32)))
    o = _retention_causal(q, k, v, log_gamma, strict=False)
    o = o + _rev(_retention_causal(_rev(q), _rev(k), _rev(v), log_gamma, strict=True))
    o = o * lax.rsqrt(jnp.mean(o * o, axis=-1, keepdims=True) + EPS)
    return jax.nn.silu(g.astype(jnp.float32)) * o.reshape(b, s, RET_WIDTH)

def _ssd_causal(x, dt, log_a, bm, cm, strict):
    b, s, g, r, p = x.shape
    n = s // CHUNK
    x = x.reshape(b, n, CHUNK, g, r, p)
    dt = dt.reshape(b, n, CHUNK, g, r)
    log_a = log_a.reshape(b, n, CHUNK, g, r)
    bm = bm.reshape(b, n, CHUNK, g, -1)
    cm = cm.reshape(b, n, CHUNK, g, -1)
    a_cum = jnp.cumsum(log_a, axis=2)
    idx = jnp.arange(CHUNK)
    mask = (idx[:, None] > idx[None, :]) if strict else (idx[:, None] >= idx[None, :])
    mask = mask[None, None, :, :, None, None]
    seg = a_cum[:, :, :, None] - a_cum[:, :, None, :]
    lmat = jnp.where(mask, jnp.exp(jnp.where(mask, seg, 0.0)), 0.0)
    xdt = x * dt[..., None]
    cb = jnp.einsum('bnigs,bnjgs->bnijg', cm, bm)
    y_diag = jnp.einsum('bnijgr,bnjgrp->bnigrp', cb[..., None] * lmat, xdt)
    decay_states = jnp.exp(a_cum[:, :, -1:] - a_cum)
    states = jnp.einsum('bnlgs,bnlgr,bnlgrp->bngrps', bm, decay_states, xdt)
    chunk_decay = jnp.exp(a_cum[:, :, -1])

    def step(hst, inp):
        st, d = inp
        return hst * d[..., None, None] + st, hst

    _, h_prev = lax.scan(step, jnp.zeros_like(states[:, 0]),
                         (jnp.moveaxis(states, 1, 0), jnp.moveaxis(chunk_decay, 1, 0)))
    h_prev = jnp.moveaxis(h_prev, 0, 1)
    y_off = jnp.einsum('bnigs,bngrps,bnigr->bnigrp', cm, h_prev, jnp.exp(a_cum))
    return (y_diag + y_off).reshape(b, s, g, r, p)

def ssd_mixer(z, xbc, dt_raw, conv_w, conv_b, dt_bias, a_log, d_skip, norm_w):
    b, s, _ = z.shape
    f32 = jnp.float32
    xbc = jax.nn.silu(centred_dwconv(xbc, conv_w, conv_b).astype(f32))
    xs, bm, cm = jnp.split(xbc, [SSD_WIDTH, SSD_WIDTH + SSD_GROUPS * SSD_STATE], axis=-1)
    xs = xs.reshape(b, s, SSD_GROUPS, SSD_HEADS_PER_GROUP, HEAD_DIM)
    bm = bm.reshape(b, s, SSD_GROUPS, SSD_STATE)
    cm = cm.reshape(b, s, SSD_GROUPS, SSD_STATE)
    hs = (SSD_GROUPS, SSD_HEADS_PER_GROUP)
    dt_raw = dt_raw.astype(f32)
    dt_f = jax.nn.softplus(dt_raw + dt_bias[0].astype(f32)).reshape(b, s, *hs)
    dt_b = jax.nn.softplus(dt_raw + dt_bias[1].astype(f32)).reshape(b, s, *hs)
    la_f = -dt_f * jnp.exp(a_log[0].astype(f32)).reshape(hs)
    la_b = -dt_b * jnp.exp(a_log[1].astype(f32)).reshape(hs)
    y_f = _ssd_causal(xs, dt_f, la_f, bm, cm, strict=False)
    y_b = _rev(_ssd_causal(_rev(xs), _rev(dt_b), _rev(la_b), _rev(bm), _rev(cm), strict=True))
    y = y_f + y_b + d_skip.astype(f32).reshape(hs)[..., None] * xs
    y = y.reshape(b, s, SSD_WIDTH) * jax.nn.silu(z.astype(f32))
    y = y.reshape(b, s, SSD_GROUPS, SSD_WIDTH // SSD_GROUPS)
    y = y * lax.rsqrt(jnp.mean(y * y, axis=-1, keepdims=True) + EPS)
    return y.reshape(b, s, SSD_WIDTH) * norm_w.astype(f32)

def _linear_scan(a, u, reverse):
    def combine(lhs, rhs):
        a_l, u_l = lhs
        a_r, u_r = rhs
        return a_l * a_r, a_r * u_l + u_r

    _, h = lax.associative_scan(combine, (a, u), axis=1, reverse=reverse)
    return h

def _rglru_direction(xc, lam, wa, ba, wx, bx, reverse):
    b, s, _ = xc.shape
    f32 = jnp.float32
    xh = xc.reshape(b, s, LRU_BLOCKS, HEAD_DIM)
    r_gate = jax.nn.sigmoid(jnp.einsum('bshi,hij->bshj', xh, wa.astype(f32)).reshape(b, s, LRU_WIDTH) + ba.astype(f32))
    i_gate = jax.nn.sigmoid(jnp.einsum('bshi,hij->bshj', xh, wx.astype(f32)).reshape(b, s, LRU_WIDTH) + bx.astype(f32))
    log_a = -LRU_C * r_gate * jax.nn.softplus(-lam.astype(f32))
    a = jnp.exp(log_a)
    u = jnp.sqrt(-jnp.expm1(2.0 * log_a)) * (i_gate * xc)
    return _linear_scan(a, u, reverse)

def lru_mixer(xr, gate, conv_w, conv_b, lam, wa, ba, wx, bx):
    xc = centred_dwconv(xr, conv_w, conv_b).astype(jnp.float32)
    h = _rglru_direction(xc, lam[0], wa[0], ba[0], wx[0], bx[0], reverse=False)
    h = h + _rglru_direction(xc, lam[1], wa[1], ba[1], wx[1], bx[1], reverse=True)
    return h * jax.nn.gelu(gate.astype(jnp.float32))

def hybrid_mixer(xn, w_in, w_out, ssd_conv_w, ssd_conv_b, ssd_dt_bias, ssd_a_log, ssd_d, ssd_norm,
                 lru_conv_w, lru_conv_b, lru_lambda, lru_wa, lru_ba, lru_wx, lru_bx):
    proj = xn @ w_in
    q, k, v, g, z, xbc, dt_raw, xr, gate = jnp.split(proj, SPLIT_POINTS, axis=-1)
    o_ret = retention_mixer(q, k, v, g)
    o_ssd = ssd_mixer(z, xbc, dt_raw, ssd_conv_w, ssd_conv_b, ssd_dt_bias, ssd_a_log, ssd_d, ssd_norm)
    o_lru = lru_mixer(xr, gate, lru_conv_w, lru_conv_b, lru_lambda, lru_wa, lru_ba, lru_wx, lru_bx)
    o = jnp.concatenate([o_ret, o_ssd, o_lru], axis=-1).astype(xn.dtype)
    return o @ w_out

def memory_cross_attention(xn, mn, wq, wkv, wo):
    b, s, d = xn.shape
    m = mn.shape[1]
    q = (xn @ wq).reshape(b, s, CA_HEADS, CA_HEAD_DIM)
    k, v = jnp.split(mn @ wkv, 2, axis=-1)
    k = k.reshape(b, m, CA_HEADS, CA_HEAD_DIM)
    v = v.reshape(b, m, CA_HEADS, CA_HEAD_DIM)
    scores = jnp.einsum('bshd,bmhd->bhsm', q, k).astype(jnp.float32) * CA_HEAD_DIM ** -0.5
    p = jax.nn.softmax(scores, axis=-1).astype(v.dtype)
    o = jnp.einsum('bhsm,bmhd->bshd', p, v).reshape(b, s, d)
    return o @ wo

def _expert_dispatch(xt, expert_id, gates, w1, w3, w2):
    t, d = xt.shape
    n_assign = t * TOP_K
    e = expert_id.reshape(n_assign).astype(jnp.int32)
    tok = jnp.repeat(jnp.arange(t, dtype=jnp.int32), TOP_K)
    wts = gates.reshape(n_assign)
    order = jnp.argsort(e)
    e_s, tok_s, w_s = e[order], tok[order], wts[order]
    counts = jnp.zeros((N_EXPERTS,), jnp.int32).at[e].add(1)
    padded = (counts + MOE_BLOCK - 1) // MOE_BLOCK * MOE_BLOCK
    start = jnp.cumsum(counts) - counts
    pad_end = jnp.cumsum(padded)
    pad_start = pad_end - padded
    dest = pad_start[e_s] + jnp.arange(n_assign, dtype=jnp.int32) - start[e_s]
    n_blocks = -(-n_assign // MOE_BLOCK) + N_EXPERTS
    slots = n_blocks * MOE_BLOCK
    buf_tok = jnp.zeros((slots,), jnp.int32).at[dest].set(tok_s)
    buf_w = jnp.zeros((slots,), wts.dtype).at[dest].set(w_s)
    block_start = jnp.arange(n_blocks, dtype=jnp.int32) * MOE_BLOCK
    block_e = jnp.minimum(jnp.searchsorted(pad_end, block_start, side='right'), N_EXPERTS - 1)
    xb = xt[buf_tok].reshape(n_blocks, MOE_BLOCK, d)

    def expert_block(args):
        xblk, eid = args
        hid = jax.nn.silu(xblk @ w1[eid]) * (xblk @ w3[eid])
        return hid @ w2[eid]

    yb = lax.map(expert_block, (xb, block_e)).reshape(slots, d)
    return jnp.zeros_like(xt).at[buf_tok].add(yb * buf_w[:, None])

def hierarchical_moe(xn, wg, bg, we, be, w1, w3, w2):
    b, s, d = xn.shape
    xt = xn.reshape(b * s, d)
    t = xt.shape[0]
    group_p = jax.nn.softmax((xt @ wg).astype(jnp.float32) + bg.astype(jnp.float32), axis=-1)
    gp, gi = lax.top_k(group_p, 1)
    e_logits = ((xt @ we).astype(jnp.float32) + be.astype(jnp.float32)).reshape(t, N_GROUPS, EXPERTS_PER_GROUP)
    e_logits = jnp.take_along_axis(e_logits, gi[:, :, None], axis=1)[:, 0]
    ep, ei = lax.top_k(jax.nn.softmax(e_logits, axis=-1), TOP_K)
    gates = gp * ep / jnp.sum(ep, axis=-1, keepdims=True)
    expert_id = gi * EXPERTS_PER_GROUP + ei
    y = _expert_dispatch(xt, expert_id, gates.astype(xt.dtype), w1, w3, w2)
    return y.reshape(b, s, d)

def setup_inputs(seed: int = 0) -> dict:
    key = jax.random.key(seed)
    keys = iter(jax.random.split(key, 48))
    f32 = jnp.float32
    L = DEPTH

    def normal(shape, scale):
        return jax.random.normal(next(keys), shape, f32) * scale

    def uniform(shape, lo, hi):
        return jax.random.uniform(next(keys), shape, f32, lo, hi)

    def gain(shape):
        return 1.0 + normal(shape, 0.02)

    x = normal((BATCH, SEQ, D_MODEL), 1.0)
    mem = normal((BATCH, MEM_LEN, D_MODEL), 1.0)
    g_mix = gain((L, D_MODEL))
    w_in = normal((L, D_MODEL, D_IN), D_MODEL ** -0.5)
    w_out = normal((L, D_MIX, D_MODEL), D_MIX ** -0.5)
    ssd_conv_w = normal((L, CONV_WIDTH, SSD_CONV_DIM), CONV_WIDTH ** -0.5)
    ssd_conv_b = normal((L, SSD_CONV_DIM), 0.02)
    dt0 = jnp.exp(uniform((L, 2, SSD_HEADS), math.log(1e-3), math.log(1e-1)))
    ssd_dt_bias = dt0 + jnp.log(-jnp.expm1(-dt0))
    ssd_a_log = jnp.log(uniform((L, 2, SSD_HEADS), 1.0, 16.0))
    ssd_d = 1.0 + normal((L, SSD_HEADS), 0.1)
    ssd_norm = gain((L, SSD_WIDTH))
    lru_conv_w = normal((L, CONV_WIDTH, LRU_WIDTH), CONV_WIDTH ** -0.5)
    lru_conv_b = normal((L, LRU_WIDTH), 0.02)
    a_root = uniform((L, 2, LRU_WIDTH), 0.9, 0.999) ** (1.0 / LRU_C)
    lru_lambda = jnp.log(a_root) - jnp.log1p(-a_root)
    lru_wa = normal((L, 2, LRU_BLOCKS, HEAD_DIM, HEAD_DIM), HEAD_DIM ** -0.5)
    lru_ba = normal((L, 2, LRU_WIDTH), 0.02)
    lru_wx = normal((L, 2, LRU_BLOCKS, HEAD_DIM, HEAD_DIM), HEAD_DIM ** -0.5)
    lru_bx = normal((L, 2, LRU_WIDTH), 0.02)
    g_ca = gain((L, D_MODEL))
    g_mem = gain((L, D_MODEL))
    ca_wq = normal((L, D_MODEL, D_MODEL), D_MODEL ** -0.5)
    ca_wkv = normal((L, D_MODEL, 2 * D_MODEL), D_MODEL ** -0.5)
    ca_wo = normal((L, D_MODEL, D_MODEL), D_MODEL ** -0.5)
    g_moe = gain((L, D_MODEL))
    moe_wg = normal((L, D_MODEL, N_GROUPS), D_MODEL ** -0.5)
    moe_bg = normal((L, N_GROUPS), 0.01)
    moe_we = normal((L, D_MODEL, N_EXPERTS), D_MODEL ** -0.5)
    moe_be = normal((L, N_EXPERTS), 0.01)
    moe_w1 = normal((L, N_EXPERTS, D_MODEL, D_EXPERT), D_MODEL ** -0.5)
    moe_w3 = normal((L, N_EXPERTS, D_MODEL, D_EXPERT), D_MODEL ** -0.5)
    moe_w2 = normal((L, N_EXPERTS, D_EXPERT, D_MODEL), D_EXPERT ** -0.5)
    g_final = gain((D_MODEL,))
    return {'x': x, 'mem': mem, 'g_mix': g_mix, 'w_in': w_in, 'w_out': w_out,
            'ssd_conv_w': ssd_conv_w, 'ssd_conv_b': ssd_conv_b, 'ssd_dt_bias': ssd_dt_bias,
            'ssd_a_log': ssd_a_log, 'ssd_d': ssd_d, 'ssd_norm': ssd_norm,
            'lru_conv_w': lru_conv_w, 'lru_conv_b': lru_conv_b, 'lru_lambda': lru_lambda,
            'lru_wa': lru_wa, 'lru_ba': lru_ba, 'lru_wx': lru_wx, 'lru_bx': lru_bx,
            'g_ca': g_ca, 'g_mem': g_mem, 'ca_wq': ca_wq, 'ca_wkv': ca_wkv, 'ca_wo': ca_wo,
            'g_moe': g_moe, 'moe_wg': moe_wg, 'moe_bg': moe_bg, 'moe_we': moe_we, 'moe_be': moe_be,
            'moe_w1': moe_w1, 'moe_w3': moe_w3, 'moe_w2': moe_w2, 'g_final': g_final}

def reference(x, mem, g_mix, w_in, w_out, ssd_conv_w, ssd_conv_b, ssd_dt_bias, ssd_a_log, ssd_d, ssd_norm,
              lru_conv_w, lru_conv_b, lru_lambda, lru_wa, lru_ba, lru_wx, lru_bx,
              g_ca, g_mem, ca_wq, ca_wkv, ca_wo,
              g_moe, moe_wg, moe_bg, moe_we, moe_be, moe_w1, moe_w3, moe_w2, g_final):
    h = x
    for l in range(DEPTH):
        h = h + hybrid_mixer(rms_norm(h, g_mix[l]), w_in[l], w_out[l],
                             ssd_conv_w[l], ssd_conv_b[l], ssd_dt_bias[l], ssd_a_log[l], ssd_d[l], ssd_norm[l],
                             lru_conv_w[l], lru_conv_b[l], lru_lambda[l], lru_wa[l], lru_ba[l], lru_wx[l], lru_bx[l])
        h = h + memory_cross_attention(rms_norm(h, g_ca[l]), rms_norm(mem, g_mem[l]), ca_wq[l], ca_wkv[l], ca_wo[l])
        h = h + hierarchical_moe(rms_norm(h, g_moe[l]), moe_wg[l], moe_bg[l], moe_we[l], moe_be[l],
                                 moe_w1[l], moe_w3[l], moe_w2[l])
    return rms_norm(h, g_final)


_drawn_inputs = setup_inputs


def setup_inputs(seed=0):
    import zlib

    import numpy as np

    out = dict(_drawn_inputs(seed))
    spreads = {}
    factors = {'lru_ba': 5.433,
     'lru_bx': 3.018,
     'g_ca': 2.842,
     'g_mem': 4.572,
     'g_final': 8.337,
     'g_moe': 4.96,
     'moe_bg': 7.939,
     'moe_be': 6.221}
    for name, (base, spread) in spreads.items():
        noise = np.random.default_rng([zlib.crc32(name.encode()), seed]).standard_normal(out[name].shape)
        drawn = base * np.exp(spread * noise) if base else spread * noise
        out[name] = jnp.asarray(drawn.astype(out[name].dtype))
    for name, factor in factors.items():
        out[name] = (out[name] * factor).astype(out[name].dtype)
    return out
```

```python
import math
from contextlib import ExitStack

import numpy as np
import concourse.bass as bass
from concourse import mybir

F32 = mybir.dt.float32
I32 = mybir.dt.int32
ALU = mybir.AluOpType
ACT = mybir.ActivationFunctionType
AX_X = mybir.AxisListType.X

P = 128
D = 1024
T = 256
NT = T // P
NK = D // P
DEPTH = 2
EPS = 1e-6
RET_W, SSD_W, LRU_W = 384, 384, 256
MISC = 16 * 20
HEADS = 6
HD = 64
XBC = SSD_W + 2 * 2 * 128
D_IN = 4 * RET_W + SSD_W + XBC + HEADS + 2 * LRU_W
NCONV = (XBC + LRU_W) // P
CW = 4
PAD = 2
CA_HEADS = 4
GROUPS, PER_GROUP = 4, 8
NE = GROUPS * PER_GROUP
F = 512
CAP = 32
QUAD = P // CAP
OV_BLOCKS = 16
SLOTS = NE * CAP
RING = 6
UNIT = 4096

CONST = {}
_at = 0
for _name, _n in (("ident", P), ("rot", P), ("cos", T), ("sin", T), ("decay", HEADS * 3 * P), ("causal", NT * T),
                  ("head_mean", P), ("group_mean", P), ("before", P), ("ones", P), ("iota", F), ("part", 1),
                  ("first_slot", NE), ("pick_head", HEADS * P)):
    CONST[_name] = (_at, _at + _n)
    _at += _n
N_CONST = _at

ROWS = {}
_at = 0
for _name, _n in (("conv_w", CW * 7), ("conv_b", 7), ("lru_conv_w", CW * 2), ("lru_conv_b", 2), ("lam", 4),
                  ("ba", 4), ("bx", 4), ("ssd_norm", 3)):
    ROWS[_name] = (_at, _n)
    _at += _n
N_ROWS = _at

O_Q, O_K, O_V, O_G, O_Z, O_X = 0, 384, 768, 1152, 1536, 1920
O_DT = O_X + XBC
O_XR = O_DT + HEADS
W_IN_UNITS = ((O_X, 512), (O_X + 512, 390), (O_XR, 512), (O_Q, 512), (512, 512), (1024, 512), (O_Z, 384))
JOBS = ((0, 0, 2, P), (0, 256, 2, P), (1, 0, 2, P), (1, 256, 2, HEADS), (2, 0, 2, P), (2, 256, 2, P),
        (3, 0, 2, P), (3, 256, 2, P), (4, 0, 2, P), None, None, (5, 128, 2, P), (5, 384, 1, P),
        (6, 0, 2, P), (6, 256, 1, P))
PRE_SLOT = (0, 1, 2, 3, 0, 1, 2, 3, 0, 1, 2, 3, 4, 5, 0, 1, 2)
EXPERT_SLOT0 = 3


def constants():
    c = np.zeros((P, N_CONST), np.float64)

    def put(name, a):
        lo, hi = CONST[name]
        c[:a.shape[0], lo:hi] = a

    p = np.arange(P)
    put("ident", np.eye(P))
    rot = np.zeros((P, P))
    for b in (0, HD):
        for d in range(HD // 2):
            rot[b + HD // 2 + d, b + d] = -1.0
            rot[b + d, b + HD // 2 + d] = 1.0
    put("rot", rot)
    inv = (10000.0 ** (-np.arange(HD // 2, dtype=np.float32) / np.float32(HD // 2))).astype(np.float32)
    ang = (np.arange(T, dtype=np.float32)[None, :] * inv[p % (HD // 2)][:, None]).astype(np.float32)
    put("cos", np.cos(ang.astype(np.float64)))
    put("sin", np.sin(ang.astype(np.float64)))
    band = np.arange(3 * P)[None, :] - P - p[:, None]
    put("decay", np.concatenate([HD ** -0.5 * (1.0 - 2.0 ** (-5.0 - h)) ** np.abs(band) for h in range(HEADS)], 1))
    t = np.arange(T)
    put("causal", np.concatenate([(t[None, :] >= P * j + p[:, None]).astype(float) for j in range(NT)], 1))
    put("head_mean", (p[:, None] // HD == p[None, :] // HD) / float(HD))
    put("group_mean", np.full((P, P), 1.0 / (SSD_W // 2)))
    put("before", (p[:, None] < p[None, :]).astype(float))
    put("ones", np.ones((P, P)))
    put("iota", np.tile(np.arange(F), (P, 1)))
    put("part", p[:, None])
    put("first_slot", np.tile(np.arange(NE) * CAP, (P, 1)))
    put("pick_head", np.concatenate([np.tile((np.arange(HEADS) == h)[:, None], (1, P)) for h in range(HEADS)], 1))
    return c.astype(np.float32)


SEMS = """params rows_turned params_cols params_misc x_in mem_in
squared variance deviation inverse normed_act normed_vec turned turned_act turned_vec
proj proj_evac dt_raw conv tanh_conv silu xs_turned xs_tok
soft_abs soft_exp soft_ln dt_rows cum_rows dt_cols cols_sb cb cb_sb
lru_gates gate_tanh lru_coef lru_decay lru_open lru_ratio lru_root lru_state
seg_rows seg_fwd seg_arg seg_exp dt_mix cb_dt head_mat ssd_y ssd_sum z_tanh z_gate ssd_sq ssd_mean ssd_sd
rot rotated score decayed ret_done ret_copy g_tanh ret_sq ret_mean ret_sd mix_ready lru_gelu_a lru_gelu_t
mixed mixed_added kv kv_evac kv_evac_vec q_proj q_evac q_evac_vec att_score att_max att_exp att_prob att_turned att_pt att_pt_vec att_o att_oevac att_oevac_vec
att_out att_added logits logits_sb group_exp gate_exp rank_mm routed diag diag_mm bcast sel gather gather_act gather_vec route_mem
act_step vec_step pool_step ov_w ov_step
x_hidden x_tanh x_gated x_h x_hT x_hTsb x_y x_yact x_yvec x_selT x_scat x_added x_vec x_stage att_step route_step ov_sel ov_x ov_xT""".split()


def build_trunk(nc, a, out):
    ctx = ExitStack()
    consts_in = ctx.enter_context(nc.semaphore("consts_in"))
    S = {n: ctx.enter_context(nc.semaphore(n)) for n in SEMS}
    full = [ctx.enter_context(nc.semaphore(f"unit_landed_{s}")) for s in range(RING)]
    xfull = [ctx.enter_context(nc.semaphore(f"expert_landed_{s}")) for s in range(RING)]
    last_sem = ctx.enter_context(nc.semaphore("last_of_a_layer"))
    layer_sems = range(S["params"].num, last_sem.num + 1)
    assert len(layer_sems) == len(SEMS) + 2 * RING + 1

    def sb(name, shape, dt=F32):
        return ctx.enter_context(nc.sbuf_tensor(name, shape, dt))

    ring = sb("ring", [P, RING, UNIT])
    h = sb("h", [P, NT, D])
    xn = sb("xn", [P, NT, D])
    xnT = sb("xnT", [P, NK, T])
    K = sb("const", [P, N_CONST])
    gains = sb("gains", [P, 4, NK])
    prow = sb("prow", [N_ROWS, P])
    pcol = sb("pcol", [P, N_ROWS])
    dtp = sb("dtp", [HEADS, 2, 3])
    dskip = sb("dskip", [P, 3])
    lruw = sb("lruw", [P, 2, 2, 2, P])
    lrup = sb("lrup", [P, 4, 4])
    halfb = sb("halfb", [P, 8])
    wge = sb("wge", [P, NK, GROUPS + NE])
    bge = sb("bge", [P, GROUPS + NE])
    stat = sb("stat", [P, 4, NT, 4])
    ov_table = sb("ov_table", [P, 3 * NE])
    ov_int = sb("ov_int", [P, 2], I32)
    ov_at = sb("ov_at", [P, 4])
    slotc = sb("slotc", [P, NT, 8])
    slot_id = sb("slot_id", [P, 1])
    eps = sb("eps", [P, 1])
    arena = sb("arena", [P, 14848])
    ps = ctx.enter_context(nc.psum_tensor("ps", [P, 8, 512], F32))

    def C(name, lo=0, n=None):
        b, e = CONST[name]
        return K[:, b + lo:(b + lo + n) if n else e]

    ident = C("ident")

    def col(name, i):
        return pcol[:, ROWS[name][0] + i:ROWS[name][0] + i + 1]

    class Carve:
        def __init__(self):
            self.used = 0

        def __call__(self, *shape):
            n = math.prod(shape)
            lo, self.used = self.used, self.used + n
            assert self.used <= 14848, self.used
            v = arena[:, lo:lo + n]
            names = "abc"[:len(shape)]
            if len(shape) == 1:
                return v
            return v.rearrange(f"p ({' '.join(names)}) -> p {' '.join(names)}", **dict(zip(names, shape)))

    mx = Carve()
    spare = ring[:, 4:6, :].rearrange("p s n -> p (s n)")
    xc = mx(NCONV, 260)
    th = mx(7, T)
    qk = mx(6, T)
    qkr = mx(6, T)
    vtok = mx(NT, RET_W)
    gz = mx(6, T)
    gt = mx(2, T)
    cbs = mx(2, 2 * T)
    yc = spare[:, 0:NCONV * T].rearrange("p (a b) -> p a b", b=T)
    o1 = NCONV * T
    headm = spare[:, o1:o1 + 1024].rearrange("p (a b) -> p a b", a=2)
    cbd = spare[:, o1 + 1024:o1 + 2048].rearrange("p (a b) -> p a b", a=2)
    o2 = o1 + 2048
    lru = spare[:, o2:o2 + 3072].rearrange("p (a b) -> p a b", b=T)
    o3 = o2 + 3072
    xstok = spare[:, o3:o3 + NT * SSD_W].rearrange("p (a b) -> p a b", a=NT)
    assert o3 + NT * SSD_W <= 2 * UNIT
    lru_a = mx(4, T)
    dtr = mx(5, 2, T)
    cols = mx(8, HEADS)
    dt_diff = mx(NT, HEADS)
    oT = xn.rearrange("p a b -> p (a b)").rearrange("p (a b) -> p a b", b=T)
    xcf = xc.rearrange("p a b -> p (a b)")
    seg_f = xcf[:, 0:1024].rearrange("p (a b) -> p a b", a=2)
    seg_b = xcf[:, 1024:2048].rearrange("p (a b) -> p a b", a=2)
    seg_e = th.rearrange("p a b -> p (a b)")[:, 0:1024].rearrange("p (a b) -> p a b", a=2)

    sq = xcf[:, 0:768].rearrange("p (a b) -> p a b", b=T)
    sd = xcf[:, 768:1536].rearrange("p (a b) -> p a b", b=T)
    means = ps[:, 0:2, :].rearrange("p a b -> p (a b)")[:, 0:768].rearrange("p (a b) -> p a b", b=T)

    def nrm(c):
        return means[:, c, :]

    at = Carve()
    memT = at(NK, T)
    kT = at(NK, T)
    vm = at(NT, D)
    qT = at(NK, T)
    prob = at(CA_HEADS, NT, T)
    probT = at(CA_HEADS, NT, T)
    attT = at(NK, T)
    mem_sb = prob.rearrange("p a b c -> p (a b c)").rearrange("p (a b) -> p a b", a=NT)
    att_stat = at(3, CA_HEADS, NT)
    memn = probT.rearrange("p a b c -> p (a b c)").rearrange("p (a b) -> p a b", a=NT)

    mo = Carve()
    xselT = mo(NK, SLOTS)
    rows4 = mo(4, T)
    ysb = mo(2, D)
    gated = mo(2, T)
    hsb = mo(2, T)
    hTs = mo(2, 2, 2 * CAP)
    selT = mo(2, T)
    diag = ysb.rearrange("p a b -> p (a b)")[:, 0:2 * 4 * P].rearrange("p (a q s) -> p a q s", a=NT, q=4)
    rt = ysb.rearrange("p a b -> p (a b)")[:, 2 * 4 * P:]
    r_used = [0]

    def small(*shape):
        n = math.prod(shape)
        v = rt[:, r_used[0]:r_used[0] + n]
        r_used[0] += n
        return v if len(shape) == 1 else v.rearrange("p (a b) -> p a b", a=shape[0])

    r_lg, r_iota = small(NT, GROUPS + NE), small(PER_GROUP)
    r_gm, r_min, r_m1, r_m2 = small(NT), small(NT), small(NT), small(NT)
    r_og, r_ge, r_o1, r_o2, r_el = small(NT, GROUPS), small(NT, GROUPS), small(NT, 8), small(NT, 8), small(NT, 8)
    r_t4 = small(NT, NE).rearrange("p t (g e) -> p t g e", g=GROUPS)
    r_e1, r_e2, r_ea, r_sv = small(NT, NE), small(NT, NE), small(NT, NE), small(NT, NE)
    r_cnt, r_nov = small(NE), small(NE)
    rows_t = mo(T)
    ov_x = xselT[:, 0, 0:NK * CAP].rearrange("p (k s) -> p k s", k=NK)
    ov_f, ov_s = xselT[:, 1, 0:NE], xselT[:, 1, NE:NE + CAP]
    ov_sel = xselT[:, 2, 0:NT * CAP].rearrange("p (t s) -> p t s", t=NT)
    sel = xnT.rearrange("p a b -> p (a b)").rearrange("p (a b) -> p a b", a=4)
    stage = xnT.rearrange("p a b -> p (a b)").rearrange("p (q k s) -> p q k s", q=2, k=NK)

    x_v = a["x"].rearrange("b (tt p) d -> p (b tt) d", p=P)
    mem_v = a["mem"].rearrange("b (tt p) d -> p (b tt) d", p=P)
    out_v = out.rearrange("b (tt p) d -> p (b tt) d", p=P)


    def chained(eng, sem):
        count = [0]

        def mark(ins):
            count[0] += 1
            ins.then_inc(sem, 1)
            return count[0]

        def link(ins):
            eng.wait_ge(sem, mark(ins))

        return mark, link

    def norm_act(act, n, src, dst, dstT, bank0):
        for tt in range(NT):
            act.activation(dst[:, tt, :], src[:, tt, :], ACT.Square,
                           accum_out=stat[:, n, tt, 0:1]).then_inc(S["squared"], 1)
        act.wait_ge(S["variance"], n + 1)
        act.activation(stat[:, n, :, 2], stat[:, n, :, 1], ACT.Sqrt).then_inc(S["deviation"], 1)
        act.wait_ge(S["inverse"], n + 1)
        act.activation(dst[:, 0, :], src[:, 0, :], ACT.Copy, scale=stat[:, n, 0, 3:4]).then_inc(S["normed_act"], 1)
        for k in (0, 1, 4, 5):
            act.wait_ge(S["turned"], 4 * n + k // 2 + 1)
            act.activation(dstT[:, k, :], ps[:, bank0 + k // 2, (k % 2) * T:(k % 2 + 1) * T], ACT.Copy,
                           scale=gains[:, n, k:k + 1]).then_inc(S["turned_act"], 1)

    def norm_vec(vec, n, src, dst, dstT, bank0):
        vec.wait_ge(S["squared"], 2 * (n + 1))
        vec.tensor_scalar(stat[:, n, :, 1], stat[:, n, :, 0], 1.0 / D, EPS, ALU.mult, ALU.add).then_inc(S["variance"], 1)
        vec.wait_ge(S["deviation"], n + 1)
        vec.reciprocal(stat[:, n, :, 3], stat[:, n, :, 2]).then_inc(S["inverse"], 1)
        vec.wait_ge(S["inverse"], n + 1)
        vec.tensor_scalar(dst[:, 1, :], src[:, 1, :], stat[:, n, 1, 3:4], None, ALU.mult).then_inc(S["normed_vec"], 1)
        for k in (2, 3, 6, 7):
            vec.wait_ge(S["turned"], 4 * n + k // 2 + 1)
            vec.tensor_scalar(dstT[:, k, :], ps[:, bank0 + k // 2, (k % 2) * T:(k % 2 + 1) * T], gains[:, n, k:k + 1], None,
                              ALU.mult).then_inc(S["turned_vec"], 1)

    def norm_pe(pe, n, dst, bank0):
        pe.wait_ge(S["normed_act"], n + 1)
        pe.wait_ge(S["normed_vec"], n + 1)
        for k in range(NK):
            for tt in range(NT):
                o = (k % 2) * T + tt * P
                ins = pe.transpose(ps[:, bank0 + k // 2, o:o + P], dst[:, tt, k::NK], ident)
            if k % 2:
                ins.then_inc(S["turned"], 1)

    def normed_T_ready(pe, n):
        pe.wait_ge(S["turned_act"], 4 * (n + 1))
        pe.wait_ge(S["turned_vec"], 4 * (n + 1))

    with nc.Block() as block:
        @block.sync
        def _(sp):
            sp.dma_start(h[:, :, :], x_v).then_inc(consts_in, 16)
            sp.dma_start(K[:, :], a["const"]).then_inc(consts_in, 16)
            sp.wait_ge(consts_in, 32)

        @block.gpsimd
        def _(pool):
            pool.memset(lruw[:, :, :, :, :], 0.0)
            pool.memset(eps[:, :], EPS)

    def mixer(layer):
        def of(name):
            return a[name][bass.ds(layer, 1)]

        w_in_v = a["w_in"].rearrange("l (p k) n -> l p k n", k=NK)
        w_out_v = a["w_out"].rearrange("l (c p) n -> l p c n", p=P)
        with nc.Block() as block:
            @block.sync
            def _(sp):
                free = {4: (S["proj"], 2), 5: (S["proj"], 4), 6: (S["proj"], 6), 7: (S["proj"], 8), 8: (S["proj"], 11)}
                for u in range(9):
                    if u in free:
                        sp.wait_ge(*free[u])
                    s = PRE_SLOT[u]
                    if u < 7:
                        c0, n = W_IN_UNITS[u]
                        dst = ring[:, s, :].rearrange("p (k n) -> p k n", k=NK)[:, :, 0:n]
                        src = w_in_v[bass.ds(layer, 1), :, :, c0:c0 + n].rearrange("l p k n -> p (l k) n")
                    else:
                        c = 4 * (u - 7)
                        dst = ring[:, s, :].rearrange("p (c n) -> p c n", c=4)
                        src = w_out_v[bass.ds(layer, 1), :, c:c + 4, :].rearrange("l p c n -> p (l c) n")
                    sp.dma_start(dst, src).then_inc(full[s], 16)

            @block.gpsimd
            def _(pool):
                for hh in range(HEADS):
                    b = hh % 2
                    pool.wait_ge(S["cols_sb"], 1)
                    if hh >= 2:
                        pool.wait_ge(S["head_mat"], hh - 1)
                    for j in range(NT):
                        pool.tensor_scalar(cbd[:, b, j * T:(j + 1) * T], C("causal", j * T, T),
                                           dt_diff[:, j, hh:hh + 1], cols[:, 6 + j, hh:hh + 1],
                                           ALU.mult, ALU.add).then_inc(S["dt_mix"], 1)
                    pool.wait_ge(S["dt_mix"], 2 * hh + 2)
                    pool.wait_ge(S["cb_sb"], hh // 3 + 1)
                    pool.tensor_tensor(cbd[:, b, :], cbd[:, b, :], cbs[:, hh // 3, :], ALU.mult).then_inc(S["cb_dt"], 1)

            @block.scalar
            def _(act):
                def rows(name, src):
                    r, n = ROWS[name]
                    act.dma_start(prow[r:r + n, :], src).then_inc(S["params"], 16)

                rows("conv_w", of("ssd_conv_w").rearrange("l i (c p) -> (l i c) p", p=P))
                rows("conv_b", of("ssd_conv_b").rearrange("l (c p) -> (l c) p", p=P))
                rows("lru_conv_w", of("lru_conv_w").rearrange("l i (c p) -> (l i c) p", p=P))
                rows("lru_conv_b", of("lru_conv_b").rearrange("l (c p) -> (l c) p", p=P))
                rows("lam", of("lru_lambda").rearrange("l r (c p) -> (l r c) p", p=P))
                rows("ba", of("lru_ba").rearrange("l r (c p) -> (l r c) p", p=P))
                rows("bx", of("lru_bx").rearrange("l r (c p) -> (l r c) p", p=P))
                rows("ssd_norm", of("ssd_norm").rearrange("l (c p) -> (l c) p", p=P))

                def misc(dst, src):
                    act.dma_start(dst, src).then_inc(S["params_misc"], 16)

                with nc.allow_non_contiguous_dma(reason="a few bytes"):
                    for n, g in enumerate(("g_mix", "g_mem", "g_ca", "g_moe")):
                        misc(gains[:, n, :], of(g).rearrange("l (p k) -> p (l k)", k=NK))
                    misc(dtp[:, :, 0], of("ssd_dt_bias").rearrange("l r h -> h (l r)"))
                    misc(dtp[:, :, 1], of("ssd_a_log").rearrange("l r h -> h (l r)"))
                    for half in range(2):
                        src = of("ssd_d").rearrange("l (c two) -> (l two) c", two=2)[half:half + 1, :]
                        misc(dskip[half * HD:(half + 1) * HD, :], src.to_broadcast([HD, 3]))
                        for gate, name in enumerate(("lru_wa", "lru_wx")):
                            for r in range(2):
                                src = of(name)[:, r].rearrange("l (c two) i j -> (l two) i c j", two=2)[half]
                                misc(lruw[half * HD:(half + 1) * HD, r, gate, :, half * HD:(half + 1) * HD], src)
                    misc(wge[:, :, 0:GROUPS], of("moe_wg").rearrange("l (p k) n -> p (l k) n", k=NK))
                    misc(wge[:, :, GROUPS:], of("moe_we").rearrange("l (p k) n -> p (l k) n", k=NK))
                    misc(bge[:, 0:GROUPS], of("moe_bg").to_broadcast([P, GROUPS]))
                    misc(bge[:, GROUPS:], of("moe_be").to_broadcast([P, NE]))
                act.wait_ge(S["params_misc"], MISC)
                norm_act(act, 0, h, xn, xnT, 0)

                def evac(n, dst):
                    act.wait_ge(S["proj"], n + 1)
                    blocks = 1 if len(dst.shape) == 2 else dst.shape[1]
                    src = ps[:, 4 + n % 2, 0:math.prod(dst.shape[1:])]
                    if blocks > 1:
                        src = src.rearrange("p (a b) -> p a b", a=blocks)
                    act.activation(dst, src, ACT.Copy).then_inc(S["proj_evac"], 1)

                def tanh_conv(b):
                    act.wait_ge(S["conv"], b + 1)
                    act.activation(th[:, b, :], yc[:, b, :], ACT.Tanh, scale=0.5).then_inc(S["tanh_conv"], 1)

                act.wait_ge(S["params_cols"], 1)
                act.activation(dtp[:, :, 2], dtp[:, :, 1], ACT.Exp).then_inc(S["act_step"], 1)
                act.wait_ge(S["soft_abs"], 1)
                act.activation(lrup[:, :, 1], lrup[:, :, 0], ACT.Exp, scale=-1.0).then_inc(S["soft_exp"], 1)
                act.wait_ge(S["soft_exp"], 1)
                act.activation(lrup[:, :, 2], lrup[:, :, 1], ACT.Ln, bias=1.0).then_inc(S["soft_ln"], 1)
                for n in range(4):
                    if n == 3:
                        act.wait_ge(S["proj"], 4)
                        act.activation(xc[:, 6, PAD:PAD + T], ps[:, 5, 0:T], ACT.Copy).then_inc(S["proj_evac"], 1)
                    else:
                        evac(n, xc[:, 2 * n:2 * n + 2, PAD:PAD + T])
                evac(4, xc[:, 7:9, PAD:PAD + T])
                act.wait_ge(S["soft_abs"], 2)
                act.activation(dtr[0:HEADS, 2], dtr[0:HEADS, 1], ACT.Exp, scale=-1.0).then_inc(S["soft_exp"], 1)
                act.wait_ge(S["soft_exp"], 2)
                act.activation(dtr[0:HEADS, 3], dtr[0:HEADS, 2], ACT.Ln, bias=1.0).then_inc(S["soft_ln"], 1)
                for b in range(7):
                    tanh_conv(b)
                for tt in range(NT):
                    act.wait_ge(S["xs_turned"], tt + 1)
                    act.activation(xstok[:, tt, :], ps[:, tt, 0:SSD_W], ACT.Copy).then_inc(S["xs_tok"], 1)
                evac(5, gt)
                evac(6, qk[:, 0:2, :])
                for n in range(4):
                    act.wait_ge(S["lru_gates"], n + 1)
                    act.wait_ge(S["lru_coef"], 1)
                    for gate in range(2):
                        act.activation(lru[:, 4 * gate + n, :], ps[:, n % 2, gate * T:(gate + 1) * T], ACT.Tanh,
                                       scale=0.5, bias=halfb[:, 4 * gate + n:4 * gate + n + 1]
                                       ).then_inc(S["gate_tanh"], 1)
                evac(7, qk[:, 2:4, :])
                for n in range(4):
                    act.wait_ge(S["gate_tanh"], 2 * n + 2)
                    act.activation(lru_a[:, n, :], lru[:, n, :], ACT.Exp, scale=lrup[:, n, 3:4],
                                   bias=lrup[:, n, 3:4]).then_inc(S["lru_decay"], 1)
                for n in range(4):
                    act.wait_ge(S["lru_decay"], n + 1)
                    act.activation(lru[:, n, :], lru[:, n, :], ACT.Tanh, scale=lrup[:, n, 0:1],
                                   bias=lrup[:, n, 0:1]).then_inc(S["lru_open"], 1)
                evac(8, qk[:, 4:6, :])

                def head(hh):
                    b = hh % 2
                    act.wait_ge(S["seg_rows"], hh + 1)
                    act.wait_ge(S["cols_sb"], 1)
                    act.wait_ge(S["conv"], NCONV)
                    if hh >= 2:
                        act.wait_ge(S["seg_arg"], hh - 1)
                    for j in range(NT):
                        act.activation(seg_f[:, b, j * T:(j + 1) * T], ps[:, 6 + b, 0:T], ACT.Relu, scale=-1.0,
                                       bias=cols[:, j, hh:hh + 1]).then_inc(S["seg_fwd"], 1)
                    act.wait_ge(S["seg_arg"], hh + 1)
                    act.wait_ge(S["silu"], 7)
                    if hh >= 2:
                        act.wait_ge(S["head_mat"], hh - 1)
                    act.activation(seg_e[:, b, :], seg_b[:, b, :], ACT.Exp).then_inc(S["seg_exp"], 1)

                head(0)
                evac(9, vtok[:, 0, :])
                head(1)
                evac(10, vtok[:, 1, :])
                head(2)
                evac(11, gz[:, 0:2, :])
                head(3)
                evac(12, gz[:, 2, :])
                head(4)
                evac(13, gz[:, 3:5, :])
                head(5)
                evac(14, gz[:, 5, :])
                act.wait_ge(S["lru_ratio"], 1)
                act.activation(lru[:, 8:12, :], lru[:, 8:12, :], ACT.Sqrt, scale=0.5).then_inc(S["lru_root"], 1)
                act.wait_ge(S["proj_evac"], 15)
                act.wait_ge(S["head_mat"], HEADS)
                act.activation(th[:, 0:6, :], gz[:, :, :], ACT.Tanh, scale=0.5).then_inc(S["z_tanh"], 1)
                act.wait_ge(S["lru_gelu_a"], 1)
                act.activation(lru[:, 0:2, :], lru[:, 0:2, :], ACT.Tanh, scale=math.sqrt(2.0 / math.pi)
                               ).then_inc(S["lru_gelu_t"], 1)
                act.wait_ge(S["ssd_sum"], 1)
                act.activation(sq, oT[:, 3:6, :], ACT.Square).then_inc(S["ssd_sq"], 1)
                act.wait_ge(S["ssd_mean"], 1)
                act.activation(sd, means, ACT.Sqrt, bias=eps[:, 0:1]).then_inc(S["ssd_sd"], 1)
                for c in range(3):
                    act.wait_ge(S["ret_done"], 2 * c + 2)
                    act.activation(oT[:, c, :], ps[:, 2 + c % 2, 0:T], ACT.Copy).then_inc(S["ret_copy"], 1)
                act.wait_ge(S["ret_copy"], 3)
                act.wait_ge(S["mix_ready"], 4)
                act.activation(sq, oT[:, 0:3, :], ACT.Square).then_inc(S["ret_sq"], 1)
                act.wait_ge(S["ret_mean"], 1)
                act.activation(sd, means, ACT.Sqrt, bias=eps[:, 0:1]).then_inc(S["ret_sd"], 1)

            @block.vector
            def _(vec):
                mark, link = chained(vec, S["vec_step"])
                mark(vec.memset(xc[:, :, 0:PAD], 0.0))
                link(vec.memset(xc[:, :, PAD + T:260], 0.0))
                vec.wait_ge(S["params_misc"], MISC)
                norm_vec(vec, 0, h, xn, xnT, 0)
                vec.wait_ge(S["rows_turned"], 1)
                vec.tensor_copy(pcol[:, :], ps[:, 4, 0:N_ROWS]).then_inc(S["params_cols"], 1)
                vec.wait_ge(S["params_cols"], 1)
                lam = pcol[:, ROWS["lam"][0]:ROWS["lam"][0] + 4]
                vec.scalar_tensor_tensor(lrup[:, :, 0], lam, -1.0, lam, ALU.mult, ALU.max).then_inc(S["soft_abs"], 1)
                b0 = ROWS["ba"][0]
                mark(vec.tensor_scalar(halfb[:, :], pcol[:, b0:b0 + 8], 0.5, None, ALU.mult))
                vec.wait_ge(S["soft_ln"], 1)
                link(vec.tensor_scalar(lrup[:, :, 1], lam, -1.0, 0.0, ALU.mult, ALU.max))
                link(vec.tensor_tensor(lrup[:, :, 2], lrup[:, :, 1], lrup[:, :, 2], ALU.add))
                mark(vec.tensor_scalar(lrup[:, :, 0], lrup[:, :, 2], 4.0, None, ALU.mult))
                vec.tensor_scalar(lrup[:, :, 3], lrup[:, :, 2], -4.0, None, ALU.mult).then_inc(S["lru_coef"], 1)

                def conv(b):
                    w, bias = ("conv_w", col("conv_b", b)) if b < 7 else ("lru_conv_w", col("lru_conv_b", b - 7))
                    nb, i = (7, b) if b < 7 else (2, b - 7)
                    vec.wait_ge(S["proj_evac"], (b // 2 + 1) if b < 7 else 5)
                    link(vec.tensor_scalar(yc[:, b, :], xc[:, b, 0:T], col(w, i), bias, ALU.mult, ALU.add))
                    for tap in range(1, CW):
                        ins = vec.scalar_tensor_tensor(yc[:, b, :], xc[:, b, tap:tap + T], col(w, tap * nb + i),
                                                       yc[:, b, :], ALU.mult, ALU.add)
                        if tap < CW - 1:
                            link(ins)
                    ins.then_inc(S["conv"], 1)

                def silu(b):
                    vec.wait_ge(S["tanh_conv"], b + 1)
                    vec.scalar_tensor_tensor(yc[:, b, :], th[:, b, :], 1.0, yc[:, b, :], ALU.add, ALU.mult
                                             ).then_inc(S["silu"], 1)

                for b in range(7):
                    conv(b)
                vec.wait_ge(S["proj"], 4)
                for r in range(2):
                    vec.tensor_scalar(dtr[0:HEADS, 0, r, :], ps[0:HEADS, 5, T:2 * T], dtp[:, r, 0:1], None,
                                      ALU.add).then_inc(S["dt_raw"], 1)
                vec.wait_ge(S["dt_raw"], 2)
                vec.scalar_tensor_tensor(dtr[0:HEADS, 1], dtr[0:HEADS, 0], -1.0, dtr[0:HEADS, 0], ALU.mult, ALU.max
                                         ).then_inc(S["soft_abs"], 1)
                for b in range(7):
                    silu(b)
                conv(7)
                conv(8)
                vec.wait_ge(S["soft_ln"], 2)
                vec.wait_ge(S["act_step"], 1)
                link(vec.scalar_tensor_tensor(dtr[0:HEADS, 4], dtr[0:HEADS, 0], 0.0, dtr[0:HEADS, 3], ALU.max,
                                              ALU.add))
                for r in range(2):
                    n = mark(vec.tensor_scalar(dtr[0:HEADS, 1, r, :], dtr[0:HEADS, 4, r, :], dtp[:, r, 2:3], -1.0,
                                               ALU.mult, ALU.mult))
                vec.tensor_scalar(dtr[0:HEADS, 3], dtr[0:HEADS, 4], 0.0625, None, ALU.mult).then_inc(S["dt_rows"], 1)
                vec.wait_ge(S["vec_step"], n)
                one = C("ones", 0, 1)[0:HEADS].to_broadcast([HEADS, T])
                vec.tensor_tensor_scan(dtr[0:HEADS, 2, 0, :], one, dtr[0:HEADS, 1, 0, :], 0.0, ALU.mult, ALU.add
                                       ).then_inc(S["cum_rows"], 1)
                vec.tensor_tensor_scan(dtr[0:HEADS, 2, 1, ::-1], one, dtr[0:HEADS, 1, 1, ::-1], 0.0,
                                       ALU.mult, ALU.add).then_inc(S["cum_rows"], 1)
                for g in range(2):
                    vec.wait_ge(S["cb"], g + 1)
                    vec.tensor_copy(cbs[:, g, :], ps[:, 2 + g, :]).then_inc(S["cb_sb"], 1)
                vec.wait_ge(S["dt_cols"], 1)
                link(vec.tensor_copy(cols[:, :, :], ps[:, 6, 0:8 * HEADS].rearrange("p (a b) -> p a b", a=8)))
                vec.tensor_tensor(dt_diff, cols[:, 4:6, :], cols[:, 6:8, :], ALU.subtract).then_inc(S["cols_sb"], 1)

                def seg(hh):
                    b = hh % 2
                    vec.wait_ge(S["seg_fwd"], 2 * hh + 2)
                    if hh >= 2:
                        vec.wait_ge(S["seg_exp"], hh - 1)
                    for j in range(NT):
                        n = mark(vec.tensor_scalar(seg_b[:, b, j * T:(j + 1) * T], ps[:, 6 + b, T:2 * T],
                                                   cols[:, 2 + j, hh:hh + 1], 0.0, ALU.subtract, ALU.min))
                    vec.wait_ge(S["vec_step"], n)
                    vec.tensor_tensor(seg_b[:, b, :], seg_b[:, b, :], seg_f[:, b, :], ALU.subtract
                                      ).then_inc(S["seg_arg"], 1)

                def head_mat(hh):
                    b = hh % 2
                    vec.wait_ge(S["seg_exp"], hh + 1)
                    vec.wait_ge(S["cb_dt"], hh + 1)
                    if hh >= 2:
                        vec.wait_ge(S["ssd_y"], hh - 1)
                    vec.tensor_tensor(headm[:, b, :], seg_e[:, b, :], cbd[:, b, :], ALU.mult).then_inc(S["head_mat"], 1)

                def lru_inputs():
                    vec.wait_ge(S["lru_open"], 4)
                    link(vec.tensor_scalar(lru[:, 8:12, :], lru[:, 0:4, :], 1.0, None, ALU.add))
                    link(vec.reciprocal(lru[:, 8:12, :], lru[:, 8:12, :]))
                    vec.tensor_tensor(lru[:, 8:12, :], lru[:, 8:12, :], lru[:, 0:4, :], ALU.mult
                                      ).then_inc(S["lru_ratio"], 1)
                    vec.wait_ge(S["lru_ratio"], 1)
                    link(vec.tensor_tensor(lru[:, 0:2, :], gt[:, :, :], gt[:, :, :], ALU.mult))
                    link(vec.tensor_scalar(lru[:, 0:2, :], lru[:, 0:2, :], 0.044715, 1.0, ALU.mult, ALU.add))
                    vec.tensor_tensor(lru[:, 0:2, :], lru[:, 0:2, :], gt[:, :, :], ALU.mult
                                      ).then_inc(S["lru_gelu_a"], 1)
                    for r in range(2):
                        n = mark(vec.scalar_tensor_tensor(lru[:, 4 + 2 * r:6 + 2 * r, :],
                                                          lru[:, 4 + 2 * r:6 + 2 * r, :], 1.0, yc[:, 7:9, :],
                                                          ALU.add, ALU.mult))
                    return n

                seg(0)
                seg(1)
                head_mat(0)
                n = lru_inputs()
                for hh in range(2, HEADS):
                    seg(hh)
                    head_mat(hh - 1)
                head_mat(HEADS - 1)
                vec.wait_ge(S["vec_step"], n)
                vec.wait_ge(S["lru_root"], 1)
                link(vec.tensor_tensor(lru[:, 4:8, :], lru[:, 4:8, :], lru[:, 8:12, :], ALU.mult))
                for c in range(2):
                    mark(vec.tensor_tensor_scan(lru[:, 8 + c, :], lru_a[:, c, :], lru[:, 4 + c, :], 0.0,
                                                ALU.mult, ALU.add))
                    n = mark(vec.tensor_tensor_scan(lru[:, 10 + c, ::-1], lru_a[:, 2 + c, ::-1],
                                                    lru[:, 6 + c, ::-1], 0.0, ALU.mult, ALU.add))
                vec.wait_ge(S["lru_gelu_t"], 1)
                n2 = mark(vec.scalar_tensor_tensor(lru[:, 0:2, :], lru[:, 0:2, :], 1.0, gt[:, :, :], ALU.add,
                                                   ALU.mult))
                vec.wait_ge(S["vec_step"], n)
                link(vec.tensor_tensor(lru[:, 8:10, :], lru[:, 8:10, :], lru[:, 10:12, :], ALU.add))
                vec.scalar_tensor_tensor(oT[:, 6:8, :], lru[:, 8:10, :], 0.5, lru[:, 0:2, :], ALU.mult, ALU.mult
                                         ).then_inc(S["mix_ready"], 1)
                vec.wait_ge(S["z_tanh"], 1)
                link(vec.scalar_tensor_tensor(gz[:, :, :], th[:, 0:6, :], 1.0, gz[:, :, :], ALU.add, ALU.mult))
                link(vec.tensor_scalar(dskip[:, :], dskip[:, :], 0.25, None, ALU.mult))
                for c in range(3):
                    vec.wait_ge(S["ssd_y"], 2 * c + 2)
                    link(vec.scalar_tensor_tensor(oT[:, 3 + c, :], yc[:, c, :], dskip[:, c:c + 1],
                                                  ps[:, c % 2, 0:T], ALU.mult, ALU.add))
                    vec.sem_inc(S["z_gate"], 1)
                vec.tensor_tensor(oT[:, 3:6, :], oT[:, 3:6, :], gz[:, 3:6, :], ALU.mult).then_inc(S["ssd_sum"], 1)

                def rotate(c):
                    x, y = qk[:, 2 * c:2 * c + 2, :], qkr[:, 2 * c:2 * c + 2, :]
                    vec.wait_ge(S["rot"], c + 1)
                    cs = C("cos").unsqueeze(1).to_broadcast([P, 2, T])
                    sn = C("sin").unsqueeze(1).to_broadcast([P, 2, T])
                    n = mark(vec.tensor_tensor(x, x, cs, ALU.mult))
                    link(vec.tensor_tensor(y, ps[:, 2 + c % 2, :].rearrange("p (a b) -> p a b", a=2), sn, ALU.mult))
                    vec.tensor_tensor(y, y, x, ALU.add).then_inc(S["rotated"], 1)

                for c in range(3):
                    rotate(c)
                vec.wait_ge(S["ssd_sd"], 1)
                link(vec.reciprocal(sd, sd))
                for c in range(3):
                    vec.scalar_tensor_tensor(oT[:, 3 + c, :], oT[:, 3 + c, :], col("ssd_norm", c), sd[:, c, :],
                                             ALU.mult, ALU.mult).then_inc(S["mix_ready"], 1)
                for hh in range(HEADS):
                    b = hh % 2
                    vec.wait_ge(S["score"], hh + 1)
                    if hh >= 2:
                        vec.wait_ge(S["ret_done"], hh - 1)
                    dec = C("decay", hh * 3 * P, 3 * P)
                    for j in range(NT):
                        vec.tensor_tensor(headm[:, b, j * T:(j + 1) * T], ps[:, 6 + b, j * T:(j + 1) * T],
                                          dec[:, (1 - j) * P:(1 - j) * P + T], ALU.mult).then_inc(S["decayed"], 1)
                vec.wait_ge(S["ret_sd"], 1)
                link(vec.reciprocal(sd, sd))
                link(vec.scalar_tensor_tensor(sd, sd, 0.5, gz[:, 0:3, :], ALU.mult, ALU.mult))
                vec.tensor_tensor(oT[:, 0:3, :], oT[:, 0:3, :], sd, ALU.mult).then_inc(S["mix_ready"], 1)
                for n in range(4):
                    vec.wait_ge(S["mixed"], n + 1)
                    tt, half = n // 2, n % 2
                    hs = h[:, tt, half * 512:(half + 1) * 512]
                    vec.tensor_tensor(hs, hs, ps[:, 4 + n, :], ALU.add).then_inc(S["mixed_added"], 1)

            @block.tensor
            def _(pe):
                pe.wait_ge(S["params"], 16 * 8)
                pe.transpose(ps[:, 4, 0:N_ROWS], prow[:, :], ident[0:N_ROWS, 0:N_ROWS]).then_inc(S["rows_turned"], 1)
                norm_pe(pe, 0, xn, 0)
                normed_T_ready(pe, 0)
                pe.wait_ge(S["params_cols"], 1)
                landed = set()

                def unit(u):
                    if u not in landed:
                        landed.add(u)
                        pe.wait_ge(full[PRE_SLOT[u]], 16 * sum(PRE_SLOT[v] == PRE_SLOT[u] for v in range(u + 1)))
                    return ring[:, PRE_SLOT[u], :].rearrange("p (k n) -> p k n", k=NK)

                def bank_free(n):
                    if n >= 2:
                        pe.wait_ge(S["proj_evac"], n - 1)
                    if n == 5:
                        pe.wait_ge(S["dt_raw"], 2)

                def job(n):
                    u, c0, blocks, rows = JOBS[n]
                    w = unit(u)
                    bank_free(n)
                    for b in range(blocks):
                        m = rows if b == blocks - 1 else P
                        for k in range(NK):
                            ins = pe.matmul(ps[0:m, 4 + n % 2, b * T:(b + 1) * T], w[:, k, c0 + b * P:c0 + b * P + m],
                                            xnT[:, k, :], start=(k == 0), stop=(k == NK - 1))
                    ins.then_inc(S["proj"], 1)

                def job_v(tt):
                    n = 9 + tt
                    bank_free(n)
                    for u, c0, m, o in ((4, 256, 256, 0), (5, 0, 128, 256)):
                        w = unit(u)
                        for k in range(NK):
                            ins = pe.matmul(ps[:, 4 + n % 2, o:o + m], xnT[:, k, tt * P:(tt + 1) * P],
                                            w[:, k, c0:c0 + m], start=(k == 0), stop=(k == NK - 1))
                    ins.then_inc(S["proj"], 1)

                def seg_rows(hh):
                    if hh >= 2:
                        pe.wait_ge(S["seg_arg"], hh - 1)
                    elif hh == 0:
                        pe.wait_ge(S["cols_sb"], 1)
                    pe.matmul(ps[:, 6 + hh % 2, :], C("pick_head", hh * P, P)[0:HEADS],
                              dtr[0:HEADS, 2].rearrange("p a b -> p (a b)"), start=True, stop=True
                              ).then_inc(S["seg_rows"], 1)

                def ssd_y(hh):
                    c, lo = hh // 2, (hh % 2) * HD
                    pe.wait_ge(S["head_mat"], hh + 1)
                    if hh == 0:
                        pe.wait_ge(S["gate_tanh"], 8)
                    if hh == 4:
                        pe.wait_ge(S["z_gate"], 1)
                    for j in range(NT):
                        ins = pe.matmul(ps[lo:lo + HD, c % 2, 0:T], xstok[:, j, hh * HD:(hh + 1) * HD],
                                        headm[:, hh % 2, j * T:(j + 1) * T], start=(j == 0), stop=(j == NT - 1))
                    ins.then_inc(S["ssd_y"], 1)

                for n in range(5):
                    job(n)
                pe.wait_ge(S["silu"], 3)
                for tt in range(NT):
                    for c in range(3):
                        ins = pe.transpose(ps[:, tt, c * P:(c + 1) * P], yc[:, c, tt * P:(tt + 1) * P], ident)
                    ins.then_inc(S["xs_turned"], 1)
                job(5)
                pe.wait_ge(S["silu"], 7)
                for g in range(2):
                    for j in range(NT):
                        ins = pe.matmul(ps[:, 2 + g, j * T:(j + 1) * T], yc[:, 3 + g, j * P:(j + 1) * P],
                                        yc[:, 5 + g, :], start=True, stop=True)
                    ins.then_inc(S["cb"], 1)
                job(6)
                pe.wait_ge(S["conv"], 9)
                for n in range(4):
                    r, c = n // 2, n % 2
                    pe.wait_ge(S["xs_tok"], 2) if n < 2 else pe.wait_ge(S["gate_tanh"], 2 * (n - 1))
                    for gate in range(2):
                        ins = pe.matmul(ps[:, n % 2, gate * T:(gate + 1) * T], lruw[:, r, gate, c, :],
                                        yc[:, 7 + c, :], start=True, stop=True)
                    ins.then_inc(S["lru_gates"], 1)
                pe.wait_ge(S["cum_rows"], 2)
                pe.wait_ge(S["dt_rows"], 1)
                for q in range(4):
                    for tt in range(NT):
                        ins = pe.transpose(ps[:, 6, (2 * q + tt) * HEADS:(2 * q + tt + 1) * HEADS],
                                           dtr[0:HEADS, 2 + q // 2, q % 2, tt * P:(tt + 1) * P],
                                           ident[0:HEADS, 0:HEADS])
                ins.then_inc(S["dt_cols"], 1)
                job(7)
                seg_rows(0)
                seg_rows(1)
                job(8)
                job_v(0)
                ssd_y(0)
                seg_rows(2)
                job_v(1)
                ssd_y(1)
                seg_rows(3)
                job(11)
                ssd_y(2)
                seg_rows(4)
                job(12)
                ssd_y(3)
                seg_rows(5)
                job(13)
                job(14)

                def rot(c):
                    if c == 0:
                        pe.wait_ge(S["cb_sb"], 2)
                    if c == 2:
                        pe.wait_ge(S["rotated"], 1)
                    for b in range(2):
                        ins = pe.matmul(ps[:, 2 + c % 2, b * T:(b + 1) * T], C("rot"), qk[:, 2 * c + b, :],
                                        start=True, stop=True)
                    ins.then_inc(S["rot"], 1)

                pe.wait_ge(S["proj_evac"], 9)
                rot(0)
                rot(1)
                ssd_y(4)
                ssd_y(5)
                rot(2)
                pe.wait_ge(S["ssd_sq"], 1)
                pe.wait_ge(S["z_gate"], 3)
                gm = C("group_mean")
                lo, hi = slice(0, HD), slice(HD, P)
                nlo = [nrm(c) for c in range(3)]
                pe.matmul(nlo[0], gm, sq[:, 0, :], start=True, stop=False)
                pe.matmul(nlo[0], gm[lo], sq[lo, 1, :], start=False, stop=True)
                pe.matmul(nlo[1][lo], gm[:, lo], sq[:, 0, :], start=True, stop=False)
                pe.matmul(nlo[1][lo], gm[lo, lo], sq[lo, 1, :], start=False, stop=True)
                pe.matmul(nlo[1][hi], gm[:, lo], sq[:, 2, :], start=True, stop=False)
                pe.matmul(nlo[1][hi], gm[hi, lo], sq[hi, 1, :], start=False, stop=True)
                pe.matmul(nlo[2], gm, sq[:, 2, :], start=True, stop=False)
                pe.matmul(nlo[2], gm[hi], sq[hi, 1, :], start=False, stop=True).then_inc(S["ssd_mean"], 1)

                def score(hh):
                    c, lo = hh // 2, (hh % 2) * HD
                    if hh == 0:
                        pe.wait_ge(S["rotated"], 3)
                        pe.wait_ge(S["seg_arg"], HEADS)
                    if hh >= 2:
                        pe.wait_ge(S["decayed"], 2 * (hh - 1))
                    for j in range(NT):
                        ins = pe.matmul(ps[:, 6 + hh % 2, j * T:(j + 1) * T], qkr[lo:lo + HD, 3 + c, j * P:(j + 1) * P],
                                        qkr[lo:lo + HD, c, :], start=True, stop=True)
                    ins.then_inc(S["score"], 1)

                def ret_sum(hh):
                    c, lo = hh // 2, (hh % 2) * HD
                    pe.wait_ge(S["decayed"], 2 * hh + 2)
                    if hh == 4:
                        pe.wait_ge(S["ret_copy"], 1)
                    for j in range(NT):
                        ins = pe.matmul(ps[lo:lo + HD, 2 + c % 2, 0:T], vtok[:, j, hh * HD:(hh + 1) * HD],
                                        headm[:, hh % 2, j * T:(j + 1) * T], start=(j == 0), stop=(j == NT - 1))
                    ins.then_inc(S["ret_done"], 1)

                score(0)
                score(1)
                for hh in range(HEADS):
                    ret_sum(hh)
                    if hh + 2 < HEADS:
                        score(hh + 2)
                pe.wait_ge(S["ret_sq"], 1)
                for c in range(3):
                    ins = pe.matmul(nrm(c), C("head_mean"), sq[:, c, :], start=True, stop=True)
                ins.then_inc(S["ret_mean"], 1)
                pe.wait_ge(S["proj_evac"], 15)
                for n in range(4):
                    tt, half = n // 2, n % 2
                    order = (4, 5, 6, 7, 3, 0, 1, 2)
                    for i, c in enumerate(order):
                        w = ring[:, PRE_SLOT[7 + c // 4], :].rearrange("p (c n) -> p c n", c=4)
                        unit(7 + c // 4)
                        if n == 0 and i == 0:
                            pe.wait_ge(S["mix_ready"], 4)
                        if n == 0 and i == 5:
                            pe.wait_ge(S["mix_ready"], 5)
                        ins = pe.matmul(ps[:, 4 + n, :], oT[:, c, tt * P:(tt + 1) * P],
                                        w[:, c % 4, half * 512:(half + 1) * 512], start=(i == 0), stop=(i == NK - 1))
                    ins.then_inc(S["mixed"], 1)

    def attention(layer):
        wkv_v = a["ca_wkv"].rearrange("l (p k) n -> l p k n", k=NK)
        wq_v = a["ca_wq"].rearrange("l (p k) n -> l p k n", k=NK)
        wo_v = a["ca_wo"].rearrange("l (c p) n -> l p c n", p=P)
        with nc.Block() as block:
            @block.sync
            def _(sp):
                sp.dma_start(mem_sb, mem_v).then_inc(S["mem_in"], 16)
                free = {15: (S["kv"], 2), 16: (S["kv"], 4)}
                for u in range(9, 17):
                    if u in free:
                        sp.wait_ge(*free[u])
                    s = PRE_SLOT[u]
                    if u < 15:
                        w, c = (wkv_v, 512 * (u - 9)) if u < 13 else (wq_v, 512 * (u - 13))
                        dst = ring[:, s, :].rearrange("p (k n) -> p k n", k=NK)
                        src = w[bass.ds(layer, 1), :, :, c:c + 512].rearrange("l p k n -> p (l k) n")
                    else:
                        c = 4 * (u - 15)
                        dst = ring[:, s, :].rearrange("p (c n) -> p c n", c=4)
                        src = wo_v[bass.ds(layer, 1), :, c:c + 4, :].rearrange("l p c n -> p (l c) n")
                    sp.dma_start(dst, src).then_inc(full[s], 16)
                ready = ((S["kv"], 6), (S["kv"], 8), (S["q_proj"], 2), (S["q_proj"], 4), (S["att_out"], 4), (S["att_out"], 4))
                for e in range(2):
                    expert_loads(sp, layer * NE + e, e, lambda i: sp.wait_ge(*ready[3 * e + i]))

            @block.scalar
            def _(act):
                act.wait_ge(S["mem_in"], 16)
                norm_act(act, 1, mem_sb, memn, memT, 4)
                norm_act(act, 2, h, xn, xnT, 4)
                for n in range(0, 8, 2):
                    act.wait_ge(S["kv"], n + 1)
                    dst = kT[:, 2 * n:2 * n + 2, :] if n < 4 else vm[:, n % 2, (n // 2 - 2) * 512:(n // 2 - 1) * 512]
                    src = ps[:, n % 4, :]
                    if n < 4:
                        src = src.rearrange("p (a b) -> p a b", a=2)
                    act.activation(dst, src, ACT.Copy).then_inc(S["kv_evac"], 1)
                for n in range(0, 4, 2):
                    act.wait_ge(S["q_proj"], n + 1)
                    act.activation(qT[:, 2 * n:2 * n + 2, :], ps[:, n, :].rearrange("p (a b) -> p a b", a=2),
                                   ACT.Copy, scale=1.0 / 16.0).then_inc(S["q_evac"], 1)
                for hd in range(CA_HEADS):
                    act.wait_ge(S["att_max"], hd + 1)
                    for st in range(NT):
                        act.activation(prob[:, hd, st, :], ps[:, 4 + hd, st * T:(st + 1) * T], ACT.Exp,
                                       bias=att_stat[:, 0, hd, st:st + 1],
                                       accum_out=att_stat[:, 1, hd, st:st + 1]).then_inc(S["att_exp"], 1)
                for hd in range(0, CA_HEADS, 2):
                    act.wait_ge(S["att_turned"], hd + 1)
                    act.activation(probT[:, hd], ps[:, hd, :].rearrange("p (a b) -> p a b", a=2), ACT.Copy
                                   ).then_inc(S["att_pt"], 1)
                for hd in range(0, CA_HEADS, 2):
                    act.wait_ge(S["att_o"], hd + 1)
                    act.activation(attT[:, 2 * hd:2 * hd + 2, :], ps[:, 4 + hd, :].rearrange("p (a b) -> p a b", a=2),
                                   ACT.Copy).then_inc(S["att_oevac"], 1)

            @block.vector
            def _(vec):
                vec.wait_ge(S["mem_in"], 16)
                norm_vec(vec, 1, mem_sb, memn, memT, 4)
                norm_vec(vec, 2, h, xn, xnT, 4)
                for n in range(1, 8, 2):
                    vec.wait_ge(S["kv"], n + 1)
                    dst = kT[:, 2 * n:2 * n + 2, :] if n < 4 else vm[:, n % 2, (n // 2 - 2) * 512:(n // 2 - 1) * 512]
                    src = ps[:, n % 4, :]
                    if n < 4:
                        src = src.rearrange("p (a b) -> p a b", a=2)
                    vec.tensor_copy(dst, src).then_inc(S["kv_evac_vec"], 1)
                for n in range(1, 4, 2):
                    vec.wait_ge(S["q_proj"], n + 1)
                    vec.tensor_scalar(qT[:, 2 * n:2 * n + 2, :], ps[:, n, :].rearrange("p (a b) -> p a b", a=2),
                                      1.0 / 16.0, None, ALU.mult).then_inc(S["q_evac_vec"], 1)
                for hd in range(CA_HEADS):
                    vec.wait_ge(S["att_score"], hd + 1)
                    vec.tensor_reduce(att_stat[:, 0, hd, :], ps[:, 4 + hd, :].rearrange("p (a b) -> p a b", a=2),
                                      AX_X, ALU.max, negate=True).then_inc(S["att_max"], 1)
                mark, link = chained(vec, S["att_step"])
                for hd in range(CA_HEADS):
                    vec.wait_ge(S["att_exp"], 2 * hd + 2)
                    link(vec.reciprocal(att_stat[:, 2, hd, :], att_stat[:, 1, hd, :]))
                    for st in range(NT):
                        vec.tensor_scalar(prob[:, hd, st, :], prob[:, hd, st, :], att_stat[:, 2, hd, st:st + 1],
                                          None, ALU.mult).then_inc(S["att_prob"], 1)
                for hd in range(1, CA_HEADS, 2):
                    vec.wait_ge(S["att_turned"], hd + 1)
                    vec.tensor_copy(probT[:, hd], ps[:, hd, :].rearrange("p (a b) -> p a b", a=2)
                                    ).then_inc(S["att_pt_vec"], 1)
                for hd in range(1, CA_HEADS, 2):
                    vec.wait_ge(S["att_o"], hd + 1)
                    vec.tensor_copy(attT[:, 2 * hd:2 * hd + 2, :],
                                    ps[:, 4 + hd, :].rearrange("p (a b) -> p a b", a=2)).then_inc(S["att_oevac_vec"], 1)
                for n in range(4):
                    vec.wait_ge(S["att_out"], n + 1)
                    hs = h[:, n // 2, (n % 2) * 512:(n % 2 + 1) * 512]
                    vec.tensor_tensor(hs, hs, ps[:, n, :], ALU.add).then_inc(S["att_added"], 1)

            @block.tensor
            def _(pe):
                def unit(u):
                    pe.wait_ge(full[PRE_SLOT[u]], 16 * sum(PRE_SLOT[v] == PRE_SLOT[u] for v in range(u + 1)))
                    return ring[:, PRE_SLOT[u], :]

                norm_pe(pe, 1, memn, 4)
                normed_T_ready(pe, 1)
                norm_pe(pe, 2, xn, 4)
                for n in range(4):
                    w = unit(9 + n // 2).rearrange("p (k n) -> p k n", k=NK)
                    for b in range(2):
                        c0 = ((2 * n + b) % 4) * P
                        for k in range(NK):
                            ins = pe.matmul(ps[:, n, b * T:(b + 1) * T], w[:, k, c0:c0 + P], memT[:, k, :],
                                            start=(k == 0), stop=(k == NK - 1))
                    ins.then_inc(S["kv"], 1)
                for n in range(4, 8):
                    w = unit(9 + n // 2).rearrange("p (k n) -> p k n", k=NK)
                    pe.wait_ge(S["kv_evac"] if n % 2 == 0 else S["kv_evac_vec"], n // 2 - 1)
                    for k in range(NK):
                        ins = pe.matmul(ps[:, n % 4, :], memT[:, k, (n % 2) * P:(n % 2 + 1) * P], w[:, k, :],
                                        start=(k == 0), stop=(k == NK - 1))
                    ins.then_inc(S["kv"], 1)
                normed_T_ready(pe, 2)
                for n in range(4):
                    w = unit(13 + n // 2).rearrange("p (k n) -> p k n", k=NK)
                    pe.wait_ge(S["kv_evac"] if n % 2 == 0 else S["kv_evac_vec"], n // 2 + 3)
                    for b in range(2):
                        c0 = ((2 * n + b) % 4) * P
                        for k in range(NK):
                            ins = pe.matmul(ps[:, n, b * T:(b + 1) * T], w[:, k, c0:c0 + P], xnT[:, k, :],
                                            start=(k == 0), stop=(k == NK - 1))
                    ins.then_inc(S["q_proj"], 1)
                for hd in range(CA_HEADS):
                    pe.wait_ge(S["q_evac"] if hd % 2 == 0 else S["q_evac_vec"], hd // 2 + 1)
                    for st in range(NT):
                        for c in range(2):
                            ins = pe.matmul(ps[:, 4 + hd, st * T:(st + 1) * T],
                                            qT[:, 2 * hd + c, st * P:(st + 1) * P], kT[:, 2 * hd + c, :],
                                            start=(c == 0), stop=(c == 1))
                    ins.then_inc(S["att_score"], 1)
                for hd in range(CA_HEADS):
                    pe.wait_ge(S["att_prob"], 2 * hd + 2)
                    for mt in range(NT):
                        for st in range(NT):
                            ins = pe.transpose(ps[:, hd, mt * T + st * P:mt * T + (st + 1) * P],
                                               prob[:, hd, st, mt * P:(mt + 1) * P], ident)
                    ins.then_inc(S["att_turned"], 1)
                for hd in range(CA_HEADS):
                    pe.wait_ge(S["att_pt"] if hd % 2 == 0 else S["att_pt_vec"], hd // 2 + 1)
                    for c in range(2):
                        for mt in range(NT):
                            o = hd * 2 * P + c * P
                            ins = pe.matmul(ps[:, 4 + hd, c * T:(c + 1) * T], vm[:, mt, o:o + P],
                                            probT[:, hd, mt, :], start=(mt == 0), stop=(mt == 1))
                    ins.then_inc(S["att_o"], 1)
                pe.wait_ge(S["att_oevac"], 2)
                pe.wait_ge(S["att_oevac_vec"], 2)
                wo = [unit(15 + i).rearrange("p (c n) -> p c n", c=4) for i in range(2)]
                for n in range(4):
                    for c in range(NK):
                        ins = pe.matmul(ps[:, n, :], attT[:, c, (n // 2) * P:(n // 2 + 1) * P],
                                        wo[c // 4][:, c % 4, (n % 2) * 512:(n % 2 + 1) * 512],
                                        start=(c == 0), stop=(c == NK - 1))
                    ins.then_inc(S["att_out"], 1)

    w1_v = a["moe_w1"].rearrange("l e (p k) f -> (l e) p k f", k=NK)
    w3_v = a["moe_w3"].rearrange("l e (p k) f -> (l e) p k f", k=NK)
    w2_v = a["moe_w2"].rearrange("l e (half p b) d -> (l e) p half b d", half=2, b=2)

    def expert_unit(par, i):
        return (EXPERT_SLOT0 + 3 * par + i) % RING

    def expert_loads(sp, which, par, wait_free):
        for i in range(3):
            wait_free(i)
            s = expert_unit(par, i)
            if i < 2:
                dst = ring[:, s, :].rearrange("p (w k n) -> p w k n", w=2, k=4)
                for w, v in enumerate((w1_v, w3_v)):
                    src = v[bass.ds(which, 1), :, 4 * i:4 * i + 4, :].rearrange("e p k f -> p (e k) f")
                    sp.dma_start(dst[:, w], src).then_inc(xfull[s], 16)
            else:
                dst = ring[:, s, :].rearrange("p (half b d) -> p half b d", half=2, b=2)
                for half in range(2):
                    src = w2_v[bass.ds(which, 1), :, half, :, :].rearrange("e p b d -> p (e b) d")
                    sp.dma_start(dst[:, half], src).then_inc(xfull[s], 16)

    def hidden_matmuls(pe, par, i, lhs, bank):
        w = ring[:, expert_unit(par, i), :].rearrange("p (w k n) -> p w k n", w=2, k=4)
        for k in range(4):
            for j in range(4):
                ins = pe.matmul(ps[CAP * j:CAP * (j + 1), bank, 0:T], lhs(4 * i + k),
                                w[:, j // 2, k, (j % 2) * T:(j % 2 + 1) * T], start=(i == 0 and k == 0),
                                stop=(i == 1 and k == 3))
        return ins

    def down_matmuls(pe, par, hT, bank):
        w = ring[:, expert_unit(par, 2), :].rearrange("p (f d) -> p f d", f=4)
        for f in range(4):
            for j in range(4):
                ins = pe.matmul(ps[CAP * j:CAP * (j + 1), bank, 0:T], hT[:, f % 2, (f // 2) * CAP:(f // 2 + 1) * CAP],
                                w[:, f, j * T:(j + 1) * T], start=(f == 0), stop=(f == 3))
        return ins

    def router(layer):
        with nc.Block() as block:
            @block.scalar
            def _(act):
                norm_act(act, 3, h, xn, xnT, 0)
                act.wait_ge(S["logits_sb"], 1)
                act.activation(r_ge, r_ge, ACT.Exp).then_inc(S["group_exp"], 1)
                act.wait_ge(S["gate_exp"], 1)
                act.activation(r_m2, r_m2, ACT.Exp).then_inc(S["gate_exp"], 1)
                for n in range(0, 16, 2):
                    act.wait_ge(S["gather"], n + 1)
                    act.activation(xselT[:, n % NK, (n // NK) * 512:(n // NK + 1) * 512], ps[:, n % 4, :], ACT.Copy,
                                   scale=gains[:, 3, n % NK:n % NK + 1]).then_inc(S["gather_act"], 1)

            @block.vector
            def _(vec):
                norm_vec(vec, 3, h, xn, xnT, 0)
                mark, link = chained(vec, S["route_step"])
                vec.wait_ge(S["logits"], 1)
                lg = r_lg
                for tt in range(NT):
                    n = mark(vec.tensor_tensor(lg[:, tt, :], ps[:, 4 + tt, 0:GROUPS + NE], bge[:, :], ALU.add))
                link(vec.tensor_scalar(r_iota, C("iota", 0, PER_GROUP), -64.0, None, ALU.add))

                def over(x, n):
                    return x.unsqueeze(2).to_broadcast([P, NT, n])

                def first_max(x, mx_, one, n):
                    iota = r_iota[:, 0:n].unsqueeze(1).to_broadcast([P, NT, n])
                    link(vec.tensor_reduce(mx_, x, AX_X, ALU.max))
                    link(vec.tensor_tensor(one, x, over(mx_, n), ALU.is_equal))
                    link(vec.tensor_tensor(one, one, iota, ALU.mult))
                    link(vec.tensor_reduce(r_min, one, AX_X, ALU.min))
                    link(vec.tensor_tensor(one, iota, over(r_min, n), ALU.is_equal))

                first_max(lg[:, :, 0:GROUPS], r_gm, r_og, GROUPS)
                vec.tensor_tensor(r_ge, lg[:, :, 0:GROUPS], over(r_gm, GROUPS), ALU.subtract).then_inc(S["logits_sb"], 1)
                l4 = lg[:, :, GROUPS:].rearrange("p t (g e) -> p t g e", g=GROUPS)
                for tt in range(NT):
                    og = r_og[:, tt, :].unsqueeze(2).to_broadcast([P, GROUPS, PER_GROUP])
                    link(vec.tensor_tensor(r_t4[:, tt], l4[:, tt], og, ALU.mult))
                    link(vec.tensor_reduce(r_el[:, tt, :], r_t4[:, tt].rearrange("p g e -> p e g"), AX_X, ALU.add))
                first_max(r_el, r_m1, r_o1, PER_GROUP)
                link(vec.scalar_tensor_tensor(r_el, r_o1, -1e30, r_el, ALU.mult, ALU.add))
                first_max(r_el, r_m2, r_o2, PER_GROUP)
                vec.tensor_tensor(r_m2, r_m2, r_m1, ALU.subtract).then_inc(S["gate_exp"], 1)
                vec.wait_ge(S["group_exp"], 1)
                link(vec.tensor_reduce(r_gm, r_ge, AX_X, ALU.add))
                vec.wait_ge(S["gate_exp"], 2)
                link(vec.tensor_scalar(r_m1, r_m2, 1.0, None, ALU.add))
                link(vec.tensor_tensor(r_gm, r_gm, r_m1, ALU.mult))
                link(vec.reciprocal(slotc[:, :, 2], r_gm))
                link(vec.tensor_tensor(slotc[:, :, 3], slotc[:, :, 2], r_m2, ALU.mult))
                for tt in range(NT):
                    og = r_og[:, tt, :].unsqueeze(2).to_broadcast([P, GROUPS, PER_GROUP])
                    for o, e in ((r_o1, r_e1), (r_o2, r_e2)):
                        ob = o[:, tt, :].unsqueeze(1).to_broadcast([P, GROUPS, PER_GROUP])
                        link(vec.tensor_tensor(e[:, tt].rearrange("p (g e) -> p g e", g=GROUPS), og, ob, ALU.mult))
                vec.tensor_tensor(r_ea, r_e1, r_e2, ALU.add).then_inc(S["routed"], 1)
                vec.wait_ge(S["rank_mm"], 1)
                link(vec.tensor_copy(r_cnt, ps[:, 6, 2 * NE:3 * NE]))
                link(vec.tensor_scalar(r_nov, r_cnt, float(CAP), None, ALU.is_gt))
                for m in range(2, T // CAP):
                    link(vec.scalar_tensor_tensor(r_nov, r_cnt, float(CAP * m), r_nov, ALU.is_gt, ALU.add))
                one = C("ones", 0, NE)
                link(vec.tensor_tensor_scan(ov_table[:, 0:NE], one, r_nov, 0.0, ALU.mult, ALU.add))
                link(vec.tensor_copy(ov_int[:, 0:1], ov_table[:, NE - 1:NE]))
                link(vec.tensor_tensor(r_nov, ov_table[:, 0:NE], r_nov, ALU.subtract))
                link(vec.scalar_tensor_tensor(r_nov, r_nov, float(CAP), C("first_slot"), ALU.mult, ALU.subtract))
                link(vec.tensor_scalar(r_nov, r_nov, float(SLOTS - CAP), None, ALU.add))
                rank = ps[:, 6, 0:2 * NE].rearrange("p (t e) -> p t e", t=NT)
                for tt in range(NT):
                    link(vec.scalar_tensor_tensor(r_sv[:, tt, :], rank[:, tt, :], float(CAP), r_nov, ALU.is_ge,
                                                  ALU.mult))
                    link(vec.tensor_tensor(r_sv[:, tt, :], r_sv[:, tt, :], rank[:, tt, :], ALU.add))
                    link(vec.tensor_tensor(r_sv[:, tt, :], r_sv[:, tt, :], C("first_slot"), ALU.add))
                for i, e in enumerate((r_e1, r_e2)):
                    link(vec.tensor_tensor(e, e, r_sv, ALU.mult))
                    link(vec.tensor_reduce(slotc[:, :, i], e, AX_X, ALU.add))
                link(vec.tensor_scalar(slotc[:, :, 4:6], slotc[:, :, 0:2], -512.0, None, ALU.add))
                for tt in range(NT):
                    for q in range(4):
                        ins = vec.tensor_scalar(diag[:, tt, q, :], ident, slotc[:, tt, q:q + 1], None, ALU.mult)
                        ins.then_inc(S["diag"], 1)
                for half in range(2):
                    for tt in range(NT):
                        o = 4 if half else 0
                        link(vec.tensor_scalar(sel[:, 2 * half + tt, :], C("iota"), slotc[:, tt, o:o + 1], None,
                                               ALU.is_equal))
                        vec.scalar_tensor_tensor(sel[:, 2 * half + tt, :], C("iota"), slotc[:, tt, o + 1:o + 2],
                                                 sel[:, 2 * half + tt, :], ALU.is_equal, ALU.add).then_inc(S["sel"], 1)
                for tt in range(NT):
                    vec.wait_ge(S["diag_mm"], tt + 1)
                    vec.tensor_copy(rows4[:, :, tt * P:(tt + 1) * P], ps[:, 4 + tt, :].rearrange("p (q s) -> p q s", q=4)
                                    ).then_inc(S["bcast"], 1)
                vec.tensor_copy(slot_id[:, :], C("part")).then_inc(S["bcast"], 1)
                vec.memset(ov_at[:, 0:1], float(SLOTS)).then_inc(S["bcast"], 1)
                vec.memset(ov_at[:, 1:2], 0.0).then_inc(S["bcast"], 1)
                for n in range(1, 16, 2):
                    vec.wait_ge(S["gather"], n + 1)
                    vec.tensor_scalar(xselT[:, n % NK, (n // NK) * 512:(n // NK + 1) * 512], ps[:, n % 4, :],
                                      gains[:, 3, n % NK:n % NK + 1], None, ALU.mult).then_inc(S["gather_vec"], 1)

            @block.tensor
            def _(pe):
                norm_pe(pe, 3, xn, 0)
                normed_T_ready(pe, 3)
                for tt in range(NT):
                    for k in range(NK):
                        ins = pe.matmul(ps[:, 4 + tt, 0:GROUPS + NE], xnT[:, k, tt * P:(tt + 1) * P], wge[:, k, :],
                                        start=(k == 0), stop=(k == NK - 1))
                ins.then_inc(S["logits"], 1)
                pe.wait_ge(S["routed"], 1)
                pe.matmul(ps[:, 6, 0:NE], C("before"), r_ea[:, 0, :], start=True, stop=True)
                pe.matmul(ps[:, 6, NE:2 * NE], C("ones"), r_ea[:, 0, :], start=True, stop=False)
                pe.matmul(ps[:, 6, NE:2 * NE], C("before"), r_ea[:, 1, :], start=False, stop=True)
                pe.matmul(ps[:, 6, 2 * NE:3 * NE], C("ones"), r_ea[:, 0, :], start=True, stop=False)
                pe.matmul(ps[:, 6, 2 * NE:3 * NE], C("ones"), r_ea[:, 1, :], start=False, stop=True
                          ).then_inc(S["rank_mm"], 1)
                for tt in range(NT):
                    pe.wait_ge(S["diag"], 4 * tt + 4)
                    pe.matmul(ps[:, 4 + tt, :], C("ones"), diag[:, tt].rearrange("p q s -> p (q s)"), start=True,
                              stop=True).then_inc(S["diag_mm"], 1)
                for n in range(16):
                    half, k = n // NK, n % NK
                    if k == 0:
                        pe.wait_ge(S["sel"], 2 * half + 2)
                    if n >= 4:
                        pe.wait_ge(S["gather_act"] if n % 2 == 0 else S["gather_vec"], n // 2 - 1)
                    for tt in range(NT):
                        ins = pe.matmul(ps[:, n % 4, :], xn[:, tt, k::NK], sel[:, 2 * half + tt, :], start=(tt == 0),
                                        stop=(tt == NT - 1))
                    ins.then_inc(S["gather"], 1)

    def experts(layer):
        H0, C0, A0 = 16, 8, 2
        turns = NE // 8
        with nc.Block() as block:
            @block.sync
            def _(sp):
                with sp.Fori(0, NE // 2 - 1) as it:
                    for par in range(2):
                        e = 2 * it + par

                        def wait_free(i):
                            if i < 2:
                                sp.wait_ge(S["x_hidden"], sp.snap(2 * e + i + 1 + H0))
                            else:
                                sp.wait_ge(S["x_y"], sp.snap(e + 1))

                        expert_loads(sp, layer * NE + e + 2, par, wait_free)

            @block.gpsimd
            def _(pool):
                with pool.Fori(0, turns) as it:
                    for q in range(2):
                        pool.wait_ge(S["x_hidden"], pool.snap(16 * it + 8 * q + 8 + H0 - 16))
                        pool.tensor_copy(stage[:, q], xselT[:, :, bass.ds(it * 256 + q * P, P)]).then_inc(S["x_stage"], 1)

            @block.scalar
            def _(act):
                act.sem_inc(S["x_yact"], A0)
                with act.Fori(0, turns) as it:
                    for r in range(8):
                        q, b = r // 4, r % 2
                        act.wait_ge(S["x_hidden"], act.snap(16 * it + 2 * r + 2 + H0))
                        act.activation(gated[0:64, b, :], ps[0:64, b, 0:T], ACT.Tanh, scale=0.5).then_inc(S["x_tanh"], 1)
                        act.wait_ge(S["x_hT"], act.snap(8 * it + r + 1))
                        act.activation(hTs[:, b], ps[:, 2 + b, 0:4 * CAP].rearrange("p (a b) -> p a b", a=2), ACT.Copy
                                       ).then_inc(S["x_hTsb"], 1)
                        act.wait_ge(S["x_y"], act.snap(8 * it + r + 1))
                        if r % 4 == 0:
                            act.wait_ge(S["x_scat"], act.snap(8 * it + 4 * q + 4))
                        lo = CAP * (r % 4)
                        for j in range(2):
                            ins = act.activation(ysb[lo:lo + CAP, q, j * T:(j + 1) * T],
                                                 ps[CAP * j:CAP * (j + 1), 4 + b, 0:T], ACT.Copy)
                        ins.then_inc(S["x_yact"], 1)

            @block.vector
            def _(vec):
                vec.sem_inc(S["x_h"], A0)
                vec.sem_inc(S["x_yvec"], A0)
                vec.sem_inc(S["x_added"], A0)
                with vec.Fori(0, turns) as it:
                    for r in range(8):
                        q, b = r // 4, r % 2
                        if r % 4 == 0:
                            vec.wait_ge(S["x_scat"], vec.snap(8 * it + 4 * q + 4))
                            step = 4 * q
                            vec.scalar_tensor_tensor(selT[:, q, :], rows4[:, 0, :], slot_id[:, 0:1], rows4[:, 2, :],
                                                     ALU.is_equal, ALU.mult).then_inc(S["x_vec"], 1)
                            vec.scalar_tensor_tensor(rows_t, rows4[:, 1, :], slot_id[:, 0:1], rows4[:, 3, :],
                                                     ALU.is_equal, ALU.mult).then_inc(S["x_vec"], 1)
                            vec.wait_ge(S["x_vec"], vec.snap(6 * it + 3 * q + 2))
                            vec.tensor_tensor(selT[:, q, :], selT[:, q, :], rows_t, ALU.add).then_inc(S["x_selT"], 1)
                            vec.tensor_scalar(slot_id[:, :], slot_id[:, :], float(P), None, ALU.add
                                              ).then_inc(S["x_vec"], 1)
                            vec.wait_ge(S["x_vec"], vec.snap(6 * it + 3 * q + 3))
                            vec.wait_ge(S["x_selT"], vec.snap(2 * it + q + 1))
                        vec.wait_ge(S["x_tanh"], vec.snap(8 * it + r + 1))
                        vec.scalar_tensor_tensor(gated[64:128, b, :], gated[0:64, b, :], 1.0, ps[0:64, b, 0:T],
                                                 ALU.add, ALU.mult).then_inc(S["x_gated"], 1)
                        vec.wait_ge(S["x_gated"], vec.snap(8 * it + r + 1))
                        vec.scalar_tensor_tensor(hsb[64:128, b, :], gated[64:128, b, :], 0.5, ps[64:128, b, 0:T],
                                                 ALU.mult, ALU.mult).then_inc(S["x_h"], 1)
                        vec.wait_ge(S["x_y"], vec.snap(8 * it + r + 1))
                        lo = CAP * (r % 4)
                        for j in range(2, 4):
                            ins = vec.tensor_copy(ysb[lo:lo + CAP, q, j * T:(j + 1) * T],
                                                  ps[CAP * j:CAP * (j + 1), 4 + b, 0:T])
                        ins.then_inc(S["x_yvec"], 1)
                        if r % 4 == 3:
                            for n in range(4):
                                vec.wait_ge(S["x_scat"], vec.snap(8 * it + 4 * q + n + 1 + C0))
                                hs = h[:, n // 2, (n % 2) * 512:(n % 2 + 1) * 512]
                                vec.tensor_tensor(hs, hs, ps[:, 6 + n % 2, :], ALU.add).then_inc(S["x_added"], 1)

            @block.tensor
            def _(pe):
                pe.sem_inc(S["x_hidden"], H0)
                pe.sem_inc(S["x_scat"], C0)
                with pe.Fori(0, turns) as it:
                    for r in range(8):
                        q, b, par = r // 4, r % 2, r % 2
                        if r % 4 == 0:
                            pe.wait_ge(S["x_stage"], pe.snap(2 * it + q + 1))
                        pe.wait_ge(S["x_h"], pe.snap(8 * it + r + A0 - 1))
                        for i in range(2):
                            pe.wait_ge(xfull[expert_unit(par, i)], pe.snap(128 * it + 32 * (r // 2 + 1)))
                            hidden_matmuls(pe, par, i, lambda k: stage[:, q, k, CAP * (r % 4):CAP * (r % 4 + 1)], b
                                           ).then_inc(S["x_hidden"], 1)
                        pe.wait_ge(S["x_h"], pe.snap(8 * it + r + A0 + 1))
                        for f in range(2):
                            ins = pe.matmul(ps[:, 2 + b, f * 64:(f + 1) * 64], hsb[64:128, b, f::2],
                                            ident[64:128, 64:128], start=True, stop=True)
                        ins.then_inc(S["x_hT"], 1)
                        pe.wait_ge(S["x_hTsb"], pe.snap(8 * it + r + 1))
                        pe.wait_ge(S["x_yact"], pe.snap(8 * it + r + A0 - 1))
                        pe.wait_ge(S["x_yvec"], pe.snap(8 * it + r + A0 - 1))
                        pe.wait_ge(xfull[expert_unit(par, 2)], pe.snap(128 * it + 32 * (r // 2 + 1)))
                        down_matmuls(pe, par, hTs[:, b], 4 + b).then_inc(S["x_y"], 1)
                        if r % 4 == 3:
                            pe.wait_ge(S["x_yact"], pe.snap(8 * it + r + A0 + 1))
                            pe.wait_ge(S["x_yvec"], pe.snap(8 * it + r + A0 + 1))
                            pe.wait_ge(S["x_selT"], pe.snap(2 * it + q + 1))
                            for n in range(4):
                                tt, half = n // 2, n % 2
                                pe.wait_ge(S["x_added"], pe.snap(8 * it + 4 * q + n + A0 - 1))
                                pe.matmul(ps[:, 6 + n % 2, :], selT[:, q, tt * P:(tt + 1) * P],
                                          ysb[:, q, half * 512:(half + 1) * 512], start=True, stop=True
                                          ).then_inc(S["x_scat"], 1)

    def overflow(layer):
        with nc.Block() as block:
            @block.sync
            def _(sp):
                sp.wait_ge(S["ov_w"], 1)
                e = sp.value_load(ov_int[0:1, 1:2], min_val=0, max_val=NE - 1)
                expert_loads(sp, layer * NE + e, 0, lambda i: None)

            @block.scalar
            def _(act):
                act.wait_ge(S["x_hidden"], 2)
                act.activation(gated[0:64, 0, :], ps[0:64, 1, 0:T], ACT.Tanh, scale=0.5).then_inc(S["x_tanh"], 1)
                act.wait_ge(S["x_hT"], 1)
                act.activation(hTs[:, 0], ps[:, 2, 0:4 * CAP].rearrange("p (a b) -> p a b", a=2), ACT.Copy
                               ).then_inc(S["x_hTsb"], 1)

            @block.vector
            def _(vec):
                mark, link = chained(vec, S["ov_step"])
                link(vec.tensor_scalar(ov_f, ov_table[:, 0:NE], ov_at[:, 1:2], None, ALU.is_le))
                link(vec.tensor_reduce(ov_at[:, 2:3], ov_f, AX_X, ALU.add))
                vec.tensor_copy(ov_int[:, 1:2], ov_at[:, 2:3]).then_inc(S["ov_w"], 1)
                for tt in range(NT):
                    link(vec.tensor_scalar(ov_s, C("iota", 0, CAP), ov_at[:, 0:1], slotc[:, tt, 0:1], ALU.add,
                                           ALU.is_equal))
                    link(vec.tensor_scalar(ov_sel[:, tt, :], C("iota", 0, CAP), ov_at[:, 0:1], slotc[:, tt, 1:2],
                                           ALU.add, ALU.is_equal))
                    vec.tensor_tensor(ov_sel[:, tt, :], ov_sel[:, tt, :], ov_s, ALU.add).then_inc(S["ov_sel"], 1)
                    vec.wait_ge(S["ov_sel"], tt + 1)
                link(vec.tensor_tensor(ov_at[:, 3:4], C("part"), ov_at[:, 0:1], ALU.add))
                link(vec.scalar_tensor_tensor(selT[:, 0, :], rows4[:, 0, :], ov_at[:, 3:4], rows4[:, 2, :],
                                              ALU.is_equal, ALU.mult))
                link(vec.scalar_tensor_tensor(rows_t, rows4[:, 1, :], ov_at[:, 3:4], rows4[:, 3, :],
                                              ALU.is_equal, ALU.mult))
                vec.tensor_tensor(selT[:, 0, :], selT[:, 0, :], rows_t, ALU.add).then_inc(S["x_selT"], 1)
                vec.wait_ge(S["ov_x"], 1)
                vec.tensor_tensor(ov_x, ps[:, 0, 0:NK * CAP].rearrange("p (k s) -> p k s", k=NK),
                                  gains[:, 3, :].unsqueeze(2).to_broadcast([P, NK, CAP]), ALU.mult
                                  ).then_inc(S["ov_xT"], 1)
                vec.wait_ge(S["x_tanh"], 1)
                vec.scalar_tensor_tensor(gated[64:128, 0, :], gated[0:64, 0, :], 1.0, ps[0:64, 1, 0:T],
                                         ALU.add, ALU.mult).then_inc(S["x_gated"], 1)
                vec.wait_ge(S["x_gated"], 1)
                vec.scalar_tensor_tensor(hsb[64:128, 0, :], gated[64:128, 0, :], 0.5, ps[64:128, 1, 0:T],
                                         ALU.mult, ALU.mult).then_inc(S["x_h"], 1)
                vec.wait_ge(S["x_y"], 1)
                for j in range(4):
                    vec.tensor_copy(ysb[0:CAP, 0, j * T:(j + 1) * T], ps[CAP * j:CAP * (j + 1), 4, 0:T]
                                    ).then_inc(S["x_yvec"], 1)
                for n in range(4):
                    vec.wait_ge(S["x_scat"], n + 1)
                    hs = h[:, n // 2, (n % 2) * 512:(n % 2 + 1) * 512]
                    vec.tensor_tensor(hs, hs, ps[:, 6 + n % 2, :], ALU.add).then_inc(S["x_added"], 1)
                link(vec.tensor_scalar(ov_at[:, 0:1], ov_at[:, 0:1], float(CAP), None, ALU.add))
                link(vec.tensor_scalar(ov_at[:, 1:2], ov_at[:, 1:2], 1.0, None, ALU.add))

            @block.tensor
            def _(pe):
                pe.wait_ge(S["ov_sel"], 2)
                for k in range(NK):
                    for tt in range(NT):
                        ins = pe.matmul(ps[:, 0, k * CAP:(k + 1) * CAP], xn[:, tt, k::NK], ov_sel[:, tt, :],
                                        start=(tt == 0), stop=(tt == NT - 1))
                ins.then_inc(S["ov_x"], 1)
                pe.wait_ge(S["ov_xT"], 1)
                for i in range(2):
                    pe.wait_ge(xfull[expert_unit(0, i)], 32)
                    hidden_matmuls(pe, 0, i, lambda k: ov_x[:, k, :], 1).then_inc(S["x_hidden"], 1)
                pe.wait_ge(S["x_h"], 1)
                for f in range(2):
                    ins = pe.matmul(ps[:, 2, f * 64:(f + 1) * 64], hsb[64:128, 0, f::2], ident[64:128, 64:128],
                                    start=True, stop=True)
                ins.then_inc(S["x_hT"], 1)
                pe.wait_ge(S["x_hTsb"], 1)
                pe.wait_ge(xfull[expert_unit(0, 2)], 32)
                down_matmuls(pe, 0, hTs[:, 0], 4).then_inc(S["x_y"], 1)
                pe.wait_ge(S["x_yvec"], 4)
                pe.wait_ge(S["x_selT"], 1)
                for n in range(4):
                    tt, half = n // 2, n % 2
                    if n >= 2:
                        pe.wait_ge(S["x_added"], n - 1)
                    pe.matmul(ps[:, 6 + n % 2, :], selT[0:CAP, 0, tt * P:(tt + 1) * P],
                              ysb[0:CAP, 0, half * 512:(half + 1) * 512], start=True, stop=True).then_inc(S["x_scat"], 1)

    with nc.Fori(0, DEPTH) as layer:
        mixer(layer)
        attention(layer)
        router(layer)
        experts(layer)
        nc.sync.sem_clear(layer_sems)
        nc.all_engine_barrier()
        overflow_blocks = nc.values_load(ov_int[0:1, 0:1], min_val=0, max_val=OV_BLOCKS)
        with nc.If(overflow_blocks > 0):
            with nc.Fori(0, overflow_blocks):
                overflow(layer)
                nc.sync.sem_clear(layer_sems)
                nc.all_engine_barrier()
        with nc.Else():
            pass

    with nc.Block() as block:
        @block.sync
        def _(sp):
            sp.dma_start(ysb[:, 0, :], a["g_final"].rearrange("(o d) -> o d", o=1).to_broadcast([P, D])
                         ).then_inc(consts_in, 16)
            sp.wait_ge(S["mixed"], NT)
            sp.dma_start(out_v, xn[:, :, :]).then_inc(consts_in, 16)
            sp.wait_ge(consts_in, 64)

        @block.scalar
        def _(act):
            for tt in range(NT):
                act.activation(xn[:, tt, :], h[:, tt, :], ACT.Square, accum_out=stat[:, 0, tt, 0:1]
                               ).then_inc(S["squared"], 1)
            act.wait_ge(S["variance"], 1)
            act.activation(stat[:, 0, :, 2], stat[:, 0, :, 1], ACT.Sqrt).then_inc(S["deviation"], 1)

        @block.vector
        def _(vec):
            vec.wait_ge(S["squared"], NT)
            vec.tensor_scalar(stat[:, 0, :, 1], stat[:, 0, :, 0], 1.0 / D, EPS, ALU.mult, ALU.add
                              ).then_inc(S["variance"], 1)
            vec.wait_ge(S["deviation"], 1)
            vec.reciprocal(stat[:, 0, :, 3], stat[:, 0, :, 2]).then_inc(S["inverse"], 1)
            vec.wait_ge(S["inverse"], 1)
            vec.wait_ge(consts_in, 48)
            for tt in range(NT):
                vec.scalar_tensor_tensor(xn[:, tt, :], h[:, tt, :], stat[:, 0, tt, 3:4], ysb[:, 0, :], ALU.mult,
                                         ALU.mult).then_inc(S["mixed"], 1)
    ctx.close()


INPUTS = ("x mem g_mix w_in w_out ssd_conv_w ssd_conv_b ssd_dt_bias ssd_a_log ssd_d ssd_norm lru_conv_w lru_conv_b "
          "lru_lambda lru_wa lru_ba lru_wx lru_bx g_ca g_mem ca_wq ca_wkv ca_wo g_moe moe_wg moe_bg moe_we moe_be "
          "moe_w1 moe_w3 moe_w2 g_final").split()


def kernel(**inputs):
    import concourse.bacc as bacc
    from concourse.bass_utils import run_bass_kernel_spmd

    nc = bacc.Bacc("TRN2", target_bir_lowering=False, num_devices=1)
    arrays = {f"in_{n}": np.ascontiguousarray(inputs[n]) for n in INPUTS}
    arrays["in_const"] = constants()
    aps = {n[3:]: nc.dram_tensor(n, v.shape, mybir.dt.from_np(v.dtype), kind="ExternalInput").ap()
           for n, v in arrays.items()}
    out = nc.dram_tensor("out_0", inputs["x"].shape, F32, kind="ExternalOutput").ap()
    build_trunk(nc, aps, out)
    r = run_bass_kernel_spmd(nc, [arrays], core_ids=[0])
    return r.results[0]["out_0"]
```

```python
import math
from contextlib import ExitStack

import numpy as np
import concourse.bass as bass
from concourse import mybir

F32 = mybir.dt.float32
I32 = mybir.dt.int32
ALU = mybir.AluOpType
ACT = mybir.ActivationFunctionType
AX_X = mybir.AxisListType.X

P = 128
D = 1024
T = 256
NT = T // P
NK = D // P
DEPTH = 2
EPS = 1e-6
RET_W, SSD_W, LRU_W = 384, 384, 256
EARLY = 3
MIX_PARAMS = 16 * 21
HEADS = 6
HD = 64
XBC = SSD_W + 2 * 2 * 128
D_IN = 4 * RET_W + SSD_W + XBC + HEADS + 2 * LRU_W
NCONV = (XBC + LRU_W) // P
CW = 4
PAD = 2
CA_HEADS = 4
GROUPS, PER_GROUP = 4, 8
NE = GROUPS * PER_GROUP
F = 512
CAP = 32
QUAD = P // CAP
OV_BLOCKS = 16
SLOTS = NE * CAP
TURN = 2 * P
RING = 6
UNIT = 4096

CONST = {}
_at = 0
for _name, _n in (("ident", P), ("rot", P), ("cos", T), ("sin", T), ("decay", HEADS * 3 * P), ("causal", NT * T),
                  ("head_mean", P), ("group_mean", P), ("before", P), ("ones", P), ("iota", F), ("part", 1),
                  ("first_slot", NE), ("pick_head", HEADS * P)):
    CONST[_name] = (_at, _at + _n)
    _at += _n
N_CONST = _at

ROWS = {}
_at = 0
for _name, _n in (("conv_w", CW * 7), ("conv_b", 7), ("lru_conv_w", CW * 2), ("lru_conv_b", 2), ("lam", 4),
                  ("ba", 4), ("bx", 4), ("ssd_norm", 3)):
    ROWS[_name] = (_at, _n)
    _at += _n
N_ROWS = _at

O_Q, O_K, O_V, O_G, O_Z, O_X = 0, 384, 768, 1152, 1536, 1920
O_DT = O_X + XBC
O_XR = O_DT + HEADS
W_IN_UNITS = ((O_X, 512), (O_X + 512, 390), (O_XR, 512), (O_Q, 512), (512, 512), (1024, 512), (O_Z, 384))
JOBS = ((0, 0, 2, P), (0, 256, 2, P), (1, 0, 2, P), (1, 256, 2, HEADS), (2, 0, 2, P), (2, 256, 2, P),
        (3, 0, 2, P), (3, 256, 2, P), (4, 0, 2, P), None, None, (5, 128, 2, P), (5, 384, 1, P),
        (6, 0, 2, P), (6, 256, 1, P))
PRE_SLOT = (0, 1, 2, 3, 0, 1, 2, 3, 0, 1, 2, 3, 4, 5, 0, 1, 2)
EXPERT_SLOT0 = 3


def constants():
    c = np.zeros((P, N_CONST), np.float64)

    def put(name, a):
        lo, hi = CONST[name]
        c[:a.shape[0], lo:hi] = a

    p = np.arange(P)
    put("ident", np.eye(P))
    rot = np.zeros((P, P))
    for b in (0, HD):
        for d in range(HD // 2):
            rot[b + HD // 2 + d, b + d] = -1.0
            rot[b + d, b + HD // 2 + d] = 1.0
    put("rot", rot)
    inv = (10000.0 ** (-np.arange(HD // 2, dtype=np.float32) / np.float32(HD // 2))).astype(np.float32)
    ang = (np.arange(T, dtype=np.float32)[None, :] * inv[p % (HD // 2)][:, None]).astype(np.float32)
    put("cos", np.cos(ang.astype(np.float64)))
    put("sin", np.sin(ang.astype(np.float64)))
    band = np.arange(3 * P)[None, :] - P - p[:, None]
    put("decay", np.concatenate([HD ** -0.5 * (1.0 - 2.0 ** (-5.0 - h)) ** np.abs(band) for h in range(HEADS)], 1))
    t = np.arange(T)
    put("causal", np.concatenate([(t[None, :] >= P * j + p[:, None]).astype(float) for j in range(NT)], 1))
    put("head_mean", (p[:, None] // HD == p[None, :] // HD) / float(HD))
    put("group_mean", np.full((P, P), 1.0 / (SSD_W // 2)))
    put("before", (p[:, None] < p[None, :]).astype(float))
    put("ones", np.ones((P, P)))
    put("iota", np.tile(np.arange(F), (P, 1)))
    put("part", p[:, None])
    put("first_slot", np.tile(np.arange(NE) * CAP, (P, 1)))
    put("pick_head", np.concatenate([np.tile((np.arange(HEADS) == h)[:, None], (1, P)) for h in range(HEADS)], 1))
    return c.astype(np.float32)


SEMS = """params rows_turned params_cols mem_in
squared variance deviation inverse normed_act normed_vec turned turned_act turned_vec
proj proj_evac dt_raw conv tanh_conv silu xs_turned xs_tok
soft_abs soft_exp soft_ln dt_rows cum_rows dt_cols cols_sb cb cb_sb
lru_gates gate_tanh lru_coef lru_decay lru_open lru_ratio lru_root lru_state
seg_rows seg_fwd seg_arg seg_exp dt_mix cb_dt head_mat ssd_y ssd_sum z_tanh z_gate ssd_sq ssd_mean ssd_sd
rot rotated score decayed ret_done ret_copy g_tanh ret_sq ret_mean ret_sd mix_ready lru_gelu_a lru_gelu_t
mixed mixed_added kv kv_evac kv_evac_vec q_proj q_evac q_evac_vec att_score att_max att_exp att_prob att_turned att_pt att_pt_vec att_o att_oevac att_oevac_vec
att_out att_added logits logits_sb group_exp gate_exp rank_mm routed diag diag_mm bcast sel gather gather_act gather_vec route_mem
act_step vec_step pool_step ov_w ov_step
x_hidden x_tanh x_gated x_h x_hT x_hTsb x_y x_yact x_yvec x_selT x_scat x_added x_vec x_stage_free x_stage x_sel x_gather x_gather_act att_step route_step ov_sel ov_x ov_xT""".split()


def build_trunk(nc, a, out):
    ctx = ExitStack()
    consts_in = ctx.enter_context(nc.semaphore("consts_in"))
    next_params = ctx.enter_context(nc.semaphore("next_params"))
    next_unit = [ctx.enter_context(nc.semaphore(f"next_unit_{u}")) for u in range(EARLY)]
    S = {n: ctx.enter_context(nc.semaphore(n)) for n in SEMS}
    full = [ctx.enter_context(nc.semaphore(f"unit_landed_{s}")) for s in range(RING)]
    xfull = [ctx.enter_context(nc.semaphore(f"expert_landed_{s}")) for s in range(RING)]
    last_sem = ctx.enter_context(nc.semaphore("last_of_a_layer"))
    layer_sems = range(S["params"].num, last_sem.num + 1)
    assert len(layer_sems) == len(SEMS) + 2 * RING + 1

    def sb(name, shape, dt=F32):
        return ctx.enter_context(nc.sbuf_tensor(name, shape, dt))

    ring = sb("ring", [P, RING, UNIT])
    h = sb("h", [P, NT, D])
    xn = sb("xn", [P, NT, D])
    xnT = sb("xnT", [P, NK, T])
    K = sb("const", [P, N_CONST])
    gains = sb("gains", [P, 4, NK])
    prow = sb("prow", [N_ROWS, P])
    pcol = sb("pcol", [P, N_ROWS])
    dtp = sb("dtp", [HEADS, 2, 3])
    dskip = sb("dskip", [P, 3])
    lruw = sb("lruw", [P, 2, 2, 2, P])
    lrup = sb("lrup", [P, 4, 4])
    halfb = sb("halfb", [P, 8])
    wge = sb("wge", [P, NK, GROUPS + NE])
    bge = sb("bge", [P, GROUPS + NE])
    stat = sb("stat", [P, 4, NT, 4])
    ov_table = sb("ov_table", [P, 3 * NE])
    ov_int = sb("ov_int", [P, 2], I32)
    ov_at = sb("ov_at", [P, 4])
    slotc = sb("slotc", [P, NT, 4])
    slot_id = sb("slot_id", [P, 1])
    eps = sb("eps", [P, 1])
    arena = sb("arena", [P, 14848])
    ps = ctx.enter_context(nc.psum_tensor("ps", [P, 8, 512], F32))

    def C(name, lo=0, n=None):
        b, e = CONST[name]
        return K[:, b + lo:(b + lo + n) if n else e]

    ident = C("ident")

    def col(name, i):
        return pcol[:, ROWS[name][0] + i:ROWS[name][0] + i + 1]

    class Carve:
        def __init__(self):
            self.used = 0

        def __call__(self, *shape):
            n = math.prod(shape)
            lo, self.used = self.used, self.used + n
            assert self.used <= 14848, self.used
            v = arena[:, lo:lo + n]
            names = "abc"[:len(shape)]
            if len(shape) == 1:
                return v
            return v.rearrange(f"p ({' '.join(names)}) -> p {' '.join(names)}", **dict(zip(names, shape)))

    mx = Carve()
    spare = ring[:, 4:6, :].rearrange("p s n -> p (s n)")
    xc = mx(NCONV, 260)
    th = mx(7, T)
    qk = mx(6, T)
    qkr = mx(6, T)
    vtok = mx(NT, RET_W)
    gz = mx(6, T)
    gt = mx(2, T)
    cbs = mx(2, 2 * T)
    yc = spare[:, 0:NCONV * T].rearrange("p (a b) -> p a b", b=T)
    o1 = NCONV * T
    headm = spare[:, o1:o1 + 1024].rearrange("p (a b) -> p a b", a=2)
    cbd = spare[:, o1 + 1024:o1 + 2048].rearrange("p (a b) -> p a b", a=2)
    o2 = o1 + 2048
    lru = spare[:, o2:o2 + 3072].rearrange("p (a b) -> p a b", b=T)
    o3 = o2 + 3072
    xstok = spare[:, o3:o3 + NT * SSD_W].rearrange("p (a b) -> p a b", a=NT)
    assert o3 + NT * SSD_W <= 2 * UNIT
    lru_a = mx(4, T)
    dtr = mx(5, 2, T)
    cols = mx(8, HEADS)
    dt_diff = mx(NT, HEADS)
    oT = xn.rearrange("p a b -> p (a b)").rearrange("p (a b) -> p a b", b=T)
    xcf = xc.rearrange("p a b -> p (a b)")
    seg_f = xcf[:, 0:1024].rearrange("p (a b) -> p a b", a=2)
    seg_b = xcf[:, 1024:2048].rearrange("p (a b) -> p a b", a=2)
    seg_e = th.rearrange("p a b -> p (a b)")[:, 0:1024].rearrange("p (a b) -> p a b", a=2)

    sq = xcf[:, 0:768].rearrange("p (a b) -> p a b", b=T)
    sd = xcf[:, 768:1536].rearrange("p (a b) -> p a b", b=T)
    ssq = spare[:, o3:o3 + 768].rearrange("p (a b) -> p a b", b=T)
    ssd = spare[:, o1 + 1024:o1 + 1792].rearrange("p (a b) -> p a b", b=T)

    def means(bank):
        return ps[:, bank:bank + 2, :].rearrange("p a b -> p (a b)")[:, 0:768].rearrange("p (a b) -> p a b", b=T)

    ret_means, ssd_means = means(0), means(2)

    at = Carve()
    memT = at(NK, T)
    kT = at(NK, T)
    vm = at(NT, D)
    qT = at(NK, T)
    prob = at(CA_HEADS, NT, T)
    probT = at(CA_HEADS, NT, T)
    attT = at(NK, T)
    mem_sb = prob.rearrange("p a b c -> p (a b c)").rearrange("p (a b) -> p a b", a=NT)
    att_stat = at(3, CA_HEADS, NT)
    memn = probT.rearrange("p a b c -> p (a b c)").rearrange("p (a b) -> p a b", a=NT)

    mo = Carve()
    nextT = mo(NK, TURN)
    sel = mo(NT, TURN)
    slot_left = mo(NT, 2)
    rows4 = mo(4, T)
    ysb = mo(2, D)
    gated = mo(2, T)
    hsb = mo(2, T)
    hTs = mo(2, 2, 2 * CAP)
    selT = mo(2, T)
    diag = ysb.rearrange("p a b -> p (a b)")[:, 0:2 * 4 * P].rearrange("p (a q s) -> p a q s", a=NT, q=4)
    rt = ysb.rearrange("p a b -> p (a b)")[:, 2 * 4 * P:]
    r_used = [0]

    def small(*shape):
        n = math.prod(shape)
        v = rt[:, r_used[0]:r_used[0] + n]
        r_used[0] += n
        return v if len(shape) == 1 else v.rearrange("p (a b) -> p a b", a=shape[0])

    r_lg, r_iota = small(NT, GROUPS + NE), small(PER_GROUP)
    r_gm, r_min, r_m1, r_m2 = small(NT), small(NT), small(NT), small(NT)
    r_og, r_ge, r_o1, r_o2, r_el = small(NT, GROUPS), small(NT, GROUPS), small(NT, 8), small(NT, 8), small(NT, 8)
    r_t4 = small(NT, NE).rearrange("p t (g e) -> p t g e", g=GROUPS)
    r_e1, r_e2, r_ea, r_sv = small(NT, NE), small(NT, NE), small(NT, NE), small(NT, NE)
    r_cnt, r_nov = small(NE), small(NE)
    rows_t = mo(T)
    ov_x = nextT[:, 0, 0:NK * CAP].rearrange("p (k s) -> p k s", k=NK)
    ov_f, ov_s = nextT[:, 1, 0:NE], nextT[:, 1, NE:NE + CAP]
    ov_sel = nextT[:, 2, 0:NT * CAP].rearrange("p (t s) -> p t s", t=NT)
    stage = xnT.rearrange("p a b -> p (a b)").rearrange("p (q k s) -> p q k s", q=2, k=NK)

    x_v = a["x"].rearrange("b (tt p) d -> p (b tt) d", p=P)
    mem_v = a["mem"].rearrange("b (tt p) d -> p (b tt) d", p=P)
    out_v = out.rearrange("b (tt p) d -> p (b tt) d", p=P)


    def chained(eng, sem):
        count = [0]

        def mark(ins):
            count[0] += 1
            ins.then_inc(sem, 1)
            return count[0]

        def link(ins):
            eng.wait_ge(sem, mark(ins))

        return mark, link

    def norm_act(act, n, src, dst, dstT, bank0):
        for tt in range(NT):
            act.activation(dst[:, tt, :], src[:, tt, :], ACT.Square,
                           accum_out=stat[:, n, tt, 0:1]).then_inc(S["squared"], 1)
        act.wait_ge(S["variance"], n + 1)
        act.activation(stat[:, n, :, 2], stat[:, n, :, 1], ACT.Sqrt).then_inc(S["deviation"], 1)
        act.wait_ge(S["inverse"], n + 1)
        act.activation(dst[:, 0, :], src[:, 0, :], ACT.Copy, scale=stat[:, n, 0, 3:4]).then_inc(S["normed_act"], 1)
        for k in (0, 1, 4, 5):
            act.wait_ge(S["turned"], 4 * n + k // 2 + 1)
            act.activation(dstT[:, k, :], ps[:, bank0 + k // 2, (k % 2) * T:(k % 2 + 1) * T], ACT.Copy,
                           scale=gains[:, n, k:k + 1]).then_inc(S["turned_act"], 1)

    def norm_vec(vec, n, src, dst, dstT, bank0):
        vec.wait_ge(S["squared"], 2 * (n + 1))
        vec.tensor_scalar(stat[:, n, :, 1], stat[:, n, :, 0], 1.0 / D, EPS, ALU.mult, ALU.add).then_inc(S["variance"], 1)
        vec.wait_ge(S["deviation"], n + 1)
        vec.reciprocal(stat[:, n, :, 3], stat[:, n, :, 2]).then_inc(S["inverse"], 1)
        vec.wait_ge(S["inverse"], n + 1)
        vec.tensor_scalar(dst[:, 1, :], src[:, 1, :], stat[:, n, 1, 3:4], None, ALU.mult).then_inc(S["normed_vec"], 1)
        for k in (2, 3, 6, 7):
            vec.wait_ge(S["turned"], 4 * n + k // 2 + 1)
            vec.tensor_scalar(dstT[:, k, :], ps[:, bank0 + k // 2, (k % 2) * T:(k % 2 + 1) * T], gains[:, n, k:k + 1], None,
                              ALU.mult).then_inc(S["turned_vec"], 1)

    def norm_pe(pe, n, dst, bank0):
        pe.wait_ge(S["normed_act"], n + 1)
        pe.wait_ge(S["normed_vec"], n + 1)
        for k in range(NK):
            for tt in range(NT):
                o = (k % 2) * T + tt * P
                ins = pe.transpose(ps[:, bank0 + k // 2, o:o + P], dst[:, tt, k::NK], ident)
            if k % 2:
                ins.then_inc(S["turned"], 1)

    def normed_T_ready(pe, n):
        pe.wait_ge(S["turned_act"], 4 * (n + 1))
        pe.wait_ge(S["turned_vec"], 4 * (n + 1))

    w_in_v = a["w_in"].rearrange("l (p k) n -> l p k n", k=NK)

    def mixer_param_loads(layer):
        def of(name):
            return a[name][bass.ds(layer, 1)]

        def rows(name, src):
            r, n = ROWS[name]
            return prow[r:r + n, :], src

        loads = [(gains[:, 0, :], of("g_mix").rearrange("l (p k) -> p (l k)", k=NK)),
                 rows("conv_w", of("ssd_conv_w").rearrange("l i (c p) -> (l i c) p", p=P)),
                 rows("conv_b", of("ssd_conv_b").rearrange("l (c p) -> (l c) p", p=P)),
                 rows("lru_conv_w", of("lru_conv_w").rearrange("l i (c p) -> (l i c) p", p=P)),
                 rows("lru_conv_b", of("lru_conv_b").rearrange("l (c p) -> (l c) p", p=P)),
                 rows("lam", of("lru_lambda").rearrange("l r (c p) -> (l r c) p", p=P)),
                 rows("ba", of("lru_ba").rearrange("l r (c p) -> (l r c) p", p=P)),
                 rows("bx", of("lru_bx").rearrange("l r (c p) -> (l r c) p", p=P)),
                 rows("ssd_norm", of("ssd_norm").rearrange("l (c p) -> (l c) p", p=P)),
                 (dtp[:, :, 0], of("ssd_dt_bias").rearrange("l r h -> h (l r)")),
                 (dtp[:, :, 1], of("ssd_a_log").rearrange("l r h -> h (l r)"))]
        for half in range(2):
            src = of("ssd_d").rearrange("l (c two) -> (l two) c", two=2)[half:half + 1, :]
            loads.append((dskip[half * HD:(half + 1) * HD, :], src.to_broadcast([HD, 3])))
            for gate, name in enumerate(("lru_wa", "lru_wx")):
                for r in range(2):
                    src = of(name)[:, r].rearrange("l (c two) i j -> (l two) i c j", two=2)[half]
                    loads.append((lruw[half * HD:(half + 1) * HD, r, gate, :, half * HD:(half + 1) * HD], src))
        assert 16 * len(loads) == MIX_PARAMS
        return loads

    def w_in_load(sp, layer, u, sem):
        c0, n = W_IN_UNITS[u]
        dst = ring[:, PRE_SLOT[u], :].rearrange("p (k n) -> p k n", k=NK)[:, :, 0:n]
        sp.dma_start(dst, w_in_v[bass.ds(layer, 1), :, :, c0:c0 + n].rearrange("l p k n -> p (l k) n")
                     ).then_inc(sem, 16)

    with nc.Block() as block:
        @block.gpsimd
        def _(pool):
            pool.memset(lruw[:, :, :, :, :], 0.0).then_inc(S["pool_step"], 1)
            pool.memset(eps[:, :], EPS).then_inc(S["pool_step"], 1)

        @block.sync
        def _(sp):
            sp.dma_start(h[:, :, :], x_v).then_inc(consts_in, 16)
            with nc.allow_non_contiguous_dma(reason="a few bytes"):
                sp.dma_start(ident, a["const"][:, 0:P]).then_inc(consts_in, 16)
                for dst, src in mixer_param_loads(0)[0:11]:
                    sp.dma_start(dst, src).then_inc(next_params, 16)
            w_in_load(sp, 0, 0, next_unit[0])
            sp.dma_start(K[:, P:], a["const"][:, P:]).then_inc(consts_in, 16)
            for u in range(1, EARLY):
                w_in_load(sp, 0, u, next_unit[u])
            sp.wait_ge(consts_in, 32)
            sp.wait_ge(next_params, MIX_PARAMS)

        @block.scalar
        def _(act):
            act.wait_ge(S["pool_step"], 1)
            with nc.allow_non_contiguous_dma(reason="a few bytes"):
                for dst, src in mixer_param_loads(0)[11:]:
                    act.dma_start(dst, src).then_inc(next_params, 16)

    def mixer(layer):
        def of(name):
            return a[name][bass.ds(layer, 1)]

        w_out_v = a["w_out"].rearrange("l (c p) n -> l p c n", p=P)
        with nc.Block() as block:
            @block.sync
            def _(sp):
                w_in_load(sp, layer, EARLY, full[PRE_SLOT[EARLY]])
                for u in range(EARLY):
                    sp.wait_ge(next_unit[u], sp.snap(16 * layer + 16))
                    sp.sem_inc(full[PRE_SLOT[u]], 16)

                def param(dst, src):
                    sp.dma_start(dst, src).then_inc(S["params"], 16)

                with nc.allow_non_contiguous_dma(reason="a few bytes"):
                    for n, g in ((1, "g_mem"), (2, "g_ca"), (3, "g_moe")):
                        param(gains[:, n, :], of(g).rearrange("l (p k) -> p (l k)", k=NK))
                    param(wge[:, :, 0:GROUPS], of("moe_wg").rearrange("l (p k) n -> p (l k) n", k=NK))
                    param(wge[:, :, GROUPS:], of("moe_we").rearrange("l (p k) n -> p (l k) n", k=NK))
                    param(bge[:, 0:GROUPS], of("moe_bg").to_broadcast([P, GROUPS]))
                    param(bge[:, GROUPS:], of("moe_be").to_broadcast([P, NE]))
                free = {4: (S["proj"], 2), 5: (S["proj"], 4), 6: (S["proj"], 6), 7: (S["proj"], 8), 8: (S["proj"], 11)}
                for u in range(EARLY + 1, 9):
                    sp.wait_ge(*free[u])
                    s = PRE_SLOT[u]
                    if u < 7:
                        w_in_load(sp, layer, u, full[s])
                    else:
                        c = 4 * (u - 7)
                        dst = ring[:, s, :].rearrange("p (c n) -> p c n", c=4)
                        src = w_out_v[bass.ds(layer, 1), :, c:c + 4, :].rearrange("l p c n -> p (l c) n")
                        sp.dma_start(dst, src).then_inc(full[s], 16)
                sp.wait_ge(S["params"], 16 * 7)

            @block.gpsimd
            def _(pool):
                pool.wait_ge(consts_in, 48)
                for hh in range(HEADS):
                    b = hh % 2
                    pool.wait_ge(S["cols_sb"], 1)
                    if hh >= 2:
                        pool.wait_ge(S["head_mat"], hh - 1)
                    for j in range(NT):
                        pool.tensor_scalar(cbd[:, b, j * T:(j + 1) * T], C("causal", j * T, T),
                                           dt_diff[:, j, hh:hh + 1], cols[:, 6 + j, hh:hh + 1],
                                           ALU.mult, ALU.add).then_inc(S["dt_mix"], 1)
                    pool.wait_ge(S["dt_mix"], 2 * hh + 2)
                    pool.wait_ge(S["cb_sb"], hh // 3 + 1)
                    pool.tensor_tensor(cbd[:, b, :], cbd[:, b, :], cbs[:, hh // 3, :], ALU.mult).then_inc(S["cb_dt"], 1)

            @block.scalar
            def _(act):
                norm_act(act, 0, h, xn, xnT, 0)

                def evac(n, dst):
                    act.wait_ge(S["proj"], n + 1)
                    blocks = 1 if len(dst.shape) == 2 else dst.shape[1]
                    src = ps[:, 4 + n % 2, 0:math.prod(dst.shape[1:])]
                    if blocks > 1:
                        src = src.rearrange("p (a b) -> p a b", a=blocks)
                    act.activation(dst, src, ACT.Copy).then_inc(S["proj_evac"], 1)

                def tanh_conv(b):
                    act.wait_ge(S["conv"], b + 1)
                    act.activation(th[:, b, :], yc[:, b, :], ACT.Tanh, scale=0.5).then_inc(S["tanh_conv"], 1)

                act.wait_ge(S["params_cols"], 1)
                act.activation(dtp[:, :, 2], dtp[:, :, 1], ACT.Exp).then_inc(S["act_step"], 1)
                act.wait_ge(S["soft_abs"], 1)
                act.activation(lrup[:, :, 1], lrup[:, :, 0], ACT.Exp, scale=-1.0).then_inc(S["soft_exp"], 1)
                act.wait_ge(S["soft_exp"], 1)
                act.activation(lrup[:, :, 2], lrup[:, :, 1], ACT.Ln, bias=1.0).then_inc(S["soft_ln"], 1)
                for n in range(4):
                    if n == 3:
                        act.wait_ge(S["proj"], 4)
                        act.activation(xc[:, 6, PAD:PAD + T], ps[:, 5, 0:T], ACT.Copy).then_inc(S["proj_evac"], 1)
                    else:
                        evac(n, xc[:, 2 * n:2 * n + 2, PAD:PAD + T])
                    if n:
                        tanh_conv(2 * n - 2)
                        tanh_conv(2 * n - 1)
                evac(4, xc[:, 7:9, PAD:PAD + T])
                tanh_conv(6)
                act.wait_ge(S["soft_abs"], 2)
                act.activation(dtr[0:HEADS, 2], dtr[0:HEADS, 1], ACT.Exp, scale=-1.0).then_inc(S["soft_exp"], 1)
                act.wait_ge(S["soft_exp"], 2)
                act.activation(dtr[0:HEADS, 3], dtr[0:HEADS, 2], ACT.Ln, bias=1.0).then_inc(S["soft_ln"], 1)
                for tt in range(NT):
                    act.wait_ge(S["xs_turned"], tt + 1)
                    act.activation(xstok[:, tt, :], ps[:, tt, 0:SSD_W], ACT.Copy).then_inc(S["xs_tok"], 1)
                evac(5, gt)

                def gate_tanh(n):
                    act.wait_ge(S["lru_gates"], n + 1)
                    act.wait_ge(S["lru_coef"], 1)
                    for gate in range(2):
                        act.activation(lru[:, 4 * gate + n, :], ps[:, n % 2, gate * T:(gate + 1) * T], ACT.Tanh,
                                       scale=0.5, bias=halfb[:, 4 * gate + n:4 * gate + n + 1]
                                       ).then_inc(S["gate_tanh"], 1)

                def seg_fwd(hh):
                    b = hh % 2
                    act.wait_ge(S["seg_rows"], hh + 1)
                    act.wait_ge(S["cols_sb"], 1)
                    act.wait_ge(S["conv"], NCONV)
                    if hh >= 2:
                        act.wait_ge(S["seg_arg"], hh - 1)
                    for j in range(NT):
                        act.activation(seg_f[:, b, j * T:(j + 1) * T], ps[:, 6 + b, 0:T], ACT.Relu, scale=-1.0,
                                       bias=cols[:, j, hh:hh + 1]).then_inc(S["seg_fwd"], 1)

                def seg_exp(hh):
                    b = hh % 2
                    act.wait_ge(S["seg_arg"], hh + 1)
                    act.wait_ge(S["silu"], 7)
                    if hh >= 2:
                        act.wait_ge(S["head_mat"], hh - 1)
                    act.activation(seg_e[:, b, :], seg_b[:, b, :], ACT.Exp).then_inc(S["seg_exp"], 1)

                gate_tanh(0)
                gate_tanh(1)
                seg_fwd(0)
                seg_fwd(1)
                seg_exp(0)
                seg_exp(1)
                evac(6, qk[:, 0:2, :])
                gate_tanh(2)
                gate_tanh(3)
                seg_fwd(2)
                for n in range(4):
                    act.wait_ge(S["gate_tanh"], 2 * n + 2)
                    act.activation(lru_a[:, n, :], lru[:, n, :], ACT.Exp, scale=lrup[:, n, 3:4],
                                   bias=lrup[:, n, 3:4]).then_inc(S["lru_decay"], 1)
                seg_exp(2)
                for n in range(4):
                    act.wait_ge(S["lru_decay"], n + 1)
                    act.activation(lru[:, n, :], lru[:, n, :], ACT.Tanh, scale=lrup[:, n, 0:1],
                                   bias=lrup[:, n, 0:1]).then_inc(S["lru_open"], 1)
                evac(7, qk[:, 2:4, :])
                seg_fwd(3)
                seg_exp(3)
                evac(8, qk[:, 4:6, :])
                seg_fwd(4)
                seg_exp(4)
                evac(9, vtok[:, 0, :])
                seg_fwd(5)
                seg_exp(5)
                act.wait_ge(S["lru_ratio"], 1)
                act.activation(lru[:, 8:12, :], lru[:, 8:12, :], ACT.Sqrt, scale=0.5).then_inc(S["lru_root"], 1)
                act.wait_ge(S["lru_gelu_a"], 1)
                act.activation(lru[:, 0:2, :], lru[:, 0:2, :], ACT.Tanh, scale=math.sqrt(2.0 / math.pi)
                               ).then_inc(S["lru_gelu_t"], 1)
                evac(10, vtok[:, 1, :])
                evac(11, gz[:, 0:2, :])
                evac(12, gz[:, 2, :])
                act.wait_ge(S["proj_evac"], 13)
                act.activation(th[:, 4:7, :], gz[:, 0:3, :], ACT.Tanh, scale=0.5).then_inc(S["g_tanh"], 1)
                evac(13, gz[:, 3:5, :])

                def ret_copy(c):
                    act.wait_ge(S["ret_done"], 2 * c + 2)
                    act.activation(oT[:, c, :], ps[:, 2 + c % 2, 0:T], ACT.Copy).then_inc(S["ret_copy"], 1)

                for c in range(3):
                    ret_copy(c)
                act.wait_ge(S["ret_copy"], 3)
                act.activation(sq, oT[:, 0:3, :], ACT.Square).then_inc(S["ret_sq"], 1)
                evac(14, gz[:, 5, :])
                act.wait_ge(S["proj_evac"], 15)
                act.wait_ge(S["head_mat"], HEADS)
                act.activation(th[:, 0:3, :], gz[:, 3:6, :], ACT.Tanh, scale=0.5).then_inc(S["z_tanh"], 1)
                act.wait_ge(S["ret_mean"], 1)
                act.activation(sd, ret_means, ACT.Sqrt, bias=eps[:, 0:1]).then_inc(S["ret_sd"], 1)
                act.wait_ge(S["ssd_sum"], 1)
                act.activation(ssq, oT[:, 3:6, :], ACT.Square).then_inc(S["ssd_sq"], 1)
                act.wait_ge(S["ssd_mean"], 1)
                act.activation(ssd, ssd_means, ACT.Sqrt, bias=eps[:, 0:1]).then_inc(S["ssd_sd"], 1)

            @block.vector
            def _(vec):
                mark, link = chained(vec, S["vec_step"])
                mark(vec.memset(xc[:, :, 0:PAD], 0.0))
                link(vec.memset(xc[:, :, PAD + T:260], 0.0))
                norm_vec(vec, 0, h, xn, xnT, 0)
                vec.wait_ge(S["rows_turned"], 1)
                vec.tensor_copy(pcol[:, :], ps[:, 4, 0:N_ROWS]).then_inc(S["params_cols"], 1)
                vec.wait_ge(S["params_cols"], 1)
                lam = pcol[:, ROWS["lam"][0]:ROWS["lam"][0] + 4]
                vec.scalar_tensor_tensor(lrup[:, :, 0], lam, -1.0, lam, ALU.mult, ALU.max).then_inc(S["soft_abs"], 1)
                b0 = ROWS["ba"][0]
                mark(vec.tensor_scalar(halfb[:, :], pcol[:, b0:b0 + 8], 0.5, None, ALU.mult))
                vec.wait_ge(S["soft_ln"], 1)
                link(vec.tensor_scalar(lrup[:, :, 1], lam, -1.0, 0.0, ALU.mult, ALU.max))
                link(vec.tensor_tensor(lrup[:, :, 2], lrup[:, :, 1], lrup[:, :, 2], ALU.add))
                mark(vec.tensor_scalar(lrup[:, :, 0], lrup[:, :, 2], 4.0, None, ALU.mult))
                vec.tensor_scalar(lrup[:, :, 3], lrup[:, :, 2], -4.0, None, ALU.mult).then_inc(S["lru_coef"], 1)

                def conv(b):
                    w, bias = ("conv_w", col("conv_b", b)) if b < 7 else ("lru_conv_w", col("lru_conv_b", b - 7))
                    nb, i = (7, b) if b < 7 else (2, b - 7)
                    vec.wait_ge(S["proj_evac"], (b // 2 + 1) if b < 7 else 5)
                    link(vec.tensor_scalar(yc[:, b, :], xc[:, b, 0:T], col(w, i), bias, ALU.mult, ALU.add))
                    for tap in range(1, CW):
                        ins = vec.scalar_tensor_tensor(yc[:, b, :], xc[:, b, tap:tap + T], col(w, tap * nb + i),
                                                       yc[:, b, :], ALU.mult, ALU.add)
                        if tap < CW - 1:
                            link(ins)
                    ins.then_inc(S["conv"], 1)

                def silu(b):
                    vec.wait_ge(S["tanh_conv"], b + 1)
                    vec.scalar_tensor_tensor(yc[:, b, :], th[:, b, :], 1.0, yc[:, b, :], ALU.add, ALU.mult
                                             ).then_inc(S["silu"], 1)

                for b in range(7):
                    conv(b)
                    if b % 2 and b >= 3:
                        silu(b - 3)
                        silu(b - 2)
                vec.wait_ge(S["proj"], 4)
                for r in range(2):
                    vec.tensor_scalar(dtr[0:HEADS, 0, r, :], ps[0:HEADS, 5, T:2 * T], dtp[:, r, 0:1], None,
                                      ALU.add).then_inc(S["dt_raw"], 1)
                vec.wait_ge(S["dt_raw"], 2)
                vec.scalar_tensor_tensor(dtr[0:HEADS, 1], dtr[0:HEADS, 0], -1.0, dtr[0:HEADS, 0], ALU.mult, ALU.max
                                         ).then_inc(S["soft_abs"], 1)
                silu(4)
                silu(5)
                conv(7)
                conv(8)
                silu(6)
                vec.wait_ge(S["soft_ln"], 2)
                vec.wait_ge(S["act_step"], 1)
                link(vec.scalar_tensor_tensor(dtr[0:HEADS, 4], dtr[0:HEADS, 0], 0.0, dtr[0:HEADS, 3], ALU.max,
                                              ALU.add))
                for r in range(2):
                    n = mark(vec.tensor_scalar(dtr[0:HEADS, 1, r, :], dtr[0:HEADS, 4, r, :], dtp[:, r, 2:3], -1.0,
                                               ALU.mult, ALU.mult))
                vec.tensor_scalar(dtr[0:HEADS, 3], dtr[0:HEADS, 4], 0.0625, None, ALU.mult).then_inc(S["dt_rows"], 1)
                vec.wait_ge(S["vec_step"], n)
                vec.wait_ge(consts_in, 48)
                one = C("ones", 0, 1)[0:HEADS].to_broadcast([HEADS, T])
                vec.tensor_tensor_scan(dtr[0:HEADS, 2, 0, :], one, dtr[0:HEADS, 1, 0, :], 0.0, ALU.mult, ALU.add
                                       ).then_inc(S["cum_rows"], 1)
                vec.tensor_tensor_scan(dtr[0:HEADS, 2, 1, ::-1], one, dtr[0:HEADS, 1, 1, ::-1], 0.0,
                                       ALU.mult, ALU.add).then_inc(S["cum_rows"], 1)
                for g in range(2):
                    vec.wait_ge(S["cb"], g + 1)
                    vec.tensor_copy(cbs[:, g, :], ps[:, 2 + g, :]).then_inc(S["cb_sb"], 1)
                vec.wait_ge(S["dt_cols"], 1)
                link(vec.tensor_copy(cols[:, :, :], ps[:, 6, 0:8 * HEADS].rearrange("p (a b) -> p a b", a=8)))
                vec.tensor_tensor(dt_diff, cols[:, 4:6, :], cols[:, 6:8, :], ALU.subtract).then_inc(S["cols_sb"], 1)

                def seg(hh):
                    b = hh % 2
                    vec.wait_ge(S["seg_fwd"], 2 * hh + 2)
                    if hh >= 2:
                        vec.wait_ge(S["seg_exp"], hh - 1)
                    for j in range(NT):
                        n = mark(vec.tensor_scalar(seg_b[:, b, j * T:(j + 1) * T], ps[:, 6 + b, T:2 * T],
                                                   cols[:, 2 + j, hh:hh + 1], 0.0, ALU.subtract, ALU.min))
                    vec.wait_ge(S["vec_step"], n)
                    vec.tensor_tensor(seg_b[:, b, :], seg_b[:, b, :], seg_f[:, b, :], ALU.subtract
                                      ).then_inc(S["seg_arg"], 1)

                def head_mat(hh):
                    b = hh % 2
                    vec.wait_ge(S["seg_exp"], hh + 1)
                    vec.wait_ge(S["cb_dt"], hh + 1)
                    if hh >= 2:
                        vec.wait_ge(S["ssd_y"], hh - 1)
                    vec.tensor_tensor(headm[:, b, :], seg_e[:, b, :], cbd[:, b, :], ALU.mult).then_inc(S["head_mat"], 1)

                def ratio():
                    vec.wait_ge(S["lru_open"], 4)
                    link(vec.tensor_scalar(lru[:, 8:12, :], lru[:, 0:4, :], 1.0, None, ALU.add))
                    link(vec.reciprocal(lru[:, 8:12, :], lru[:, 8:12, :]))
                    vec.tensor_tensor(lru[:, 8:12, :], lru[:, 8:12, :], lru[:, 0:4, :], ALU.mult
                                      ).then_inc(S["lru_ratio"], 1)
                    vec.wait_ge(S["lru_ratio"], 1)

                def gelu_and_inputs():
                    link(vec.tensor_tensor(lru[:, 0:2, :], gt[:, :, :], gt[:, :, :], ALU.mult))
                    link(vec.tensor_scalar(lru[:, 0:2, :], lru[:, 0:2, :], 0.044715, 1.0, ALU.mult, ALU.add))
                    vec.tensor_tensor(lru[:, 0:2, :], lru[:, 0:2, :], gt[:, :, :], ALU.mult
                                      ).then_inc(S["lru_gelu_a"], 1)
                    for r in range(2):
                        n = mark(vec.scalar_tensor_tensor(lru[:, 4 + 2 * r:6 + 2 * r, :],
                                                          lru[:, 4 + 2 * r:6 + 2 * r, :], 1.0, yc[:, 7:9, :],
                                                          ALU.add, ALU.mult))
                    return n

                def recurrences(n):
                    vec.wait_ge(S["vec_step"], n)
                    vec.wait_ge(S["lru_root"], 1)
                    link(vec.tensor_tensor(lru[:, 4:8, :], lru[:, 4:8, :], lru[:, 8:12, :], ALU.mult))
                    for c in range(2):
                        mark(vec.tensor_tensor_scan(lru[:, 8 + c, :], lru_a[:, c, :], lru[:, 4 + c, :], 0.0,
                                                    ALU.mult, ALU.add))
                        n = mark(vec.tensor_tensor_scan(lru[:, 10 + c, ::-1], lru_a[:, 2 + c, ::-1],
                                                        lru[:, 6 + c, ::-1], 0.0, ALU.mult, ALU.add))
                    vec.wait_ge(S["lru_gelu_t"], 1)
                    mark(vec.scalar_tensor_tensor(lru[:, 0:2, :], lru[:, 0:2, :], 1.0, gt[:, :, :], ALU.add, ALU.mult))
                    vec.wait_ge(S["vec_step"], n)
                    link(vec.tensor_tensor(lru[:, 8:10, :], lru[:, 8:10, :], lru[:, 10:12, :], ALU.add))
                    vec.scalar_tensor_tensor(oT[:, 6:8, :], lru[:, 8:10, :], 0.5, lru[:, 0:2, :], ALU.mult, ALU.mult
                                             ).then_inc(S["mix_ready"], 1)

                def ssd_sum(c):
                    vec.wait_ge(S["ssd_y"], 2 * c + 2)
                    link(vec.scalar_tensor_tensor(oT[:, 3 + c, :], yc[:, c, :], dskip[:, c:c + 1],
                                                  ps[:, c % 2, 0:T], ALU.mult, ALU.add))
                    vec.sem_inc(S["z_gate"], 1)

                def rotate(c):
                    x, y = qk[:, 2 * c:2 * c + 2, :], qkr[:, 2 * c:2 * c + 2, :]
                    vec.wait_ge(S["rot"], c + 1)
                    cs = C("cos").unsqueeze(1).to_broadcast([P, 2, T])
                    sn = C("sin").unsqueeze(1).to_broadcast([P, 2, T])
                    mark(vec.tensor_tensor(x, x, cs, ALU.mult))
                    link(vec.tensor_tensor(y, ps[:, 2 + c % 2, :].rearrange("p (a b) -> p a b", a=2), sn, ALU.mult))
                    vec.tensor_tensor(y, y, x, ALU.add).then_inc(S["rotated"], 1)

                def decayed(hh):
                    b = hh % 2
                    vec.wait_ge(S["score"], hh + 1)
                    vec.wait_ge(S["ssd_y"], HEADS) if hh < 2 else vec.wait_ge(S["ret_done"], hh - 1)
                    dec = C("decay", hh * 3 * P, 3 * P)
                    for j in range(NT):
                        vec.tensor_tensor(headm[:, b, j * T:(j + 1) * T], ps[:, 6 + b, j * T:(j + 1) * T],
                                          dec[:, (1 - j) * P:(1 - j) * P + T], ALU.mult).then_inc(S["decayed"], 1)

                mark(vec.tensor_scalar(dskip[:, :], dskip[:, :], 0.25, None, ALU.mult))
                seg(0)
                seg(1)
                head_mat(0)
                head_mat(1)
                seg(2)
                head_mat(2)
                seg(3)
                ratio()
                head_mat(3)
                rotate(0)
                seg(4)
                n = gelu_and_inputs()
                ssd_sum(0)
                head_mat(4)
                rotate(1)
                seg(5)
                ssd_sum(1)
                head_mat(5)
                rotate(2)
                recurrences(n)
                ssd_sum(2)
                for hh in range(HEADS):
                    decayed(hh)
                vec.wait_ge(S["g_tanh"], 1)
                link(vec.scalar_tensor_tensor(gz[:, 0:3, :], th[:, 4:7, :], 1.0, gz[:, 0:3, :], ALU.add, ALU.mult))
                vec.wait_ge(S["z_tanh"], 1)
                link(vec.scalar_tensor_tensor(gz[:, 3:6, :], th[:, 0:3, :], 1.0, gz[:, 3:6, :], ALU.add, ALU.mult))
                vec.tensor_tensor(oT[:, 3:6, :], oT[:, 3:6, :], gz[:, 3:6, :], ALU.mult).then_inc(S["ssd_sum"], 1)
                vec.wait_ge(S["ret_sd"], 1)
                link(vec.reciprocal(sd, sd))
                link(vec.scalar_tensor_tensor(sd, sd, 0.5, gz[:, 0:3, :], ALU.mult, ALU.mult))
                vec.tensor_tensor(oT[:, 0:3, :], oT[:, 0:3, :], sd, ALU.mult).then_inc(S["mix_ready"], 1)
                vec.wait_ge(S["ssd_sd"], 1)
                link(vec.reciprocal(ssd, ssd))
                for c in range(3):
                    vec.scalar_tensor_tensor(oT[:, 3 + c, :], oT[:, 3 + c, :], col("ssd_norm", c), ssd[:, c, :],
                                             ALU.mult, ALU.mult).then_inc(S["mix_ready"], 1)
                for n in range(4):
                    vec.wait_ge(S["mixed"], n + 1)
                    tt, half = n // 2, n % 2
                    hs = h[:, tt, half * 512:(half + 1) * 512]
                    vec.tensor_tensor(hs, hs, ps[:, 4 + n, :], ALU.add).then_inc(S["mixed_added"], 1)

            @block.tensor
            def _(pe):
                pe.transpose(ps[:, 4, 0:N_ROWS], prow[:, :], ident[0:N_ROWS, 0:N_ROWS]).then_inc(S["rows_turned"], 1)
                norm_pe(pe, 0, xn, 0)
                normed_T_ready(pe, 0)
                pe.wait_ge(S["params_cols"], 1)
                landed = set()

                def unit(u):
                    if u not in landed:
                        landed.add(u)
                        pe.wait_ge(full[PRE_SLOT[u]], 16 * sum(PRE_SLOT[v] == PRE_SLOT[u] for v in range(u + 1)))
                    return ring[:, PRE_SLOT[u], :].rearrange("p (k n) -> p k n", k=NK)

                def bank_free(n):
                    if n >= 2:
                        pe.wait_ge(S["proj_evac"], n - 1)
                    if n == 5:
                        pe.wait_ge(S["dt_raw"], 2)

                def job(n):
                    u, c0, blocks, rows = JOBS[n]
                    w = unit(u)
                    bank_free(n)
                    for b in range(blocks):
                        m = rows if b == blocks - 1 else P
                        for k in range(NK):
                            ins = pe.matmul(ps[0:m, 4 + n % 2, b * T:(b + 1) * T], w[:, k, c0 + b * P:c0 + b * P + m],
                                            xnT[:, k, :], start=(k == 0), stop=(k == NK - 1))
                    ins.then_inc(S["proj"], 1)

                def job_v(tt):
                    n = 9 + tt
                    bank_free(n)
                    for u, c0, m, o in ((4, 256, 256, 0), (5, 0, 128, 256)):
                        w = unit(u)
                        for k in range(NK):
                            ins = pe.matmul(ps[:, 4 + n % 2, o:o + m], xnT[:, k, tt * P:(tt + 1) * P],
                                            w[:, k, c0:c0 + m], start=(k == 0), stop=(k == NK - 1))
                    ins.then_inc(S["proj"], 1)

                def seg_rows(hh):
                    if hh >= 2:
                        pe.wait_ge(S["seg_arg"], hh - 1)
                    elif hh == 0:
                        pe.wait_ge(S["cols_sb"], 1)
                    pe.matmul(ps[:, 6 + hh % 2, :], C("pick_head", hh * P, P)[0:HEADS],
                              dtr[0:HEADS, 2].rearrange("p a b -> p (a b)"), start=True, stop=True
                              ).then_inc(S["seg_rows"], 1)

                def ssd_y(hh):
                    c, lo = hh // 2, (hh % 2) * HD
                    pe.wait_ge(S["head_mat"], hh + 1)
                    if hh in (0, 2):
                        pe.wait_ge(S["gate_tanh"], 8)
                    if hh == 4:
                        pe.wait_ge(S["z_gate"], 1)
                    for j in range(NT):
                        ins = pe.matmul(ps[lo:lo + HD, c % 2, 0:T], xstok[:, j, hh * HD:(hh + 1) * HD],
                                        headm[:, hh % 2, j * T:(j + 1) * T], start=(j == 0), stop=(j == NT - 1))
                    ins.then_inc(S["ssd_y"], 1)

                def rot(c):
                    pe.wait_ge(S["proj_evac"], 7 + c)
                    if c == 0:
                        pe.wait_ge(S["cb_sb"], 2)
                    if c == 2:
                        pe.wait_ge(S["rotated"], 1)
                    for b in range(2):
                        ins = pe.matmul(ps[:, 2 + c % 2, b * T:(b + 1) * T], C("rot"), qk[:, 2 * c + b, :],
                                        start=True, stop=True)
                    ins.then_inc(S["rot"], 1)

                def lru_gates(n):
                    r, c = n // 2, n % 2
                    pe.wait_ge(S["xs_tok"], 2) if n < 2 else pe.wait_ge(S["gate_tanh"], 2 * (n - 1))
                    for gate in range(2):
                        ins = pe.matmul(ps[:, n % 2, gate * T:(gate + 1) * T], lruw[:, r, gate, c, :],
                                        yc[:, 7 + c, :], start=True, stop=True)
                    ins.then_inc(S["lru_gates"], 1)

                def score(hh):
                    c, lo = hh // 2, (hh % 2) * HD
                    if hh == 0:
                        pe.wait_ge(S["rotated"], 3)
                        pe.wait_ge(S["seg_arg"], HEADS)
                    if hh >= 2:
                        pe.wait_ge(S["decayed"], 2 * (hh - 1))
                    for j in range(NT):
                        ins = pe.matmul(ps[:, 6 + hh % 2, j * T:(j + 1) * T], qkr[lo:lo + HD, 3 + c, j * P:(j + 1) * P],
                                        qkr[lo:lo + HD, c, :], start=True, stop=True)
                    ins.then_inc(S["score"], 1)

                def ret_sum(hh):
                    c, lo = hh // 2, (hh % 2) * HD
                    pe.wait_ge(S["decayed"], 2 * hh + 2)
                    if hh == 0:
                        pe.wait_ge(S["proj_evac"], 11)
                    if hh == 4:
                        pe.wait_ge(S["ret_copy"], 1)
                    for j in range(NT):
                        ins = pe.matmul(ps[lo:lo + HD, 2 + c % 2, 0:T], vtok[:, j, hh * HD:(hh + 1) * HD],
                                        headm[:, hh % 2, j * T:(j + 1) * T], start=(j == 0), stop=(j == NT - 1))
                    ins.then_inc(S["ret_done"], 1)

                for n in range(5):
                    job(n)
                pe.wait_ge(consts_in, 48)
                pe.wait_ge(S["silu"], 3)
                for tt in range(NT):
                    for c in range(3):
                        ins = pe.transpose(ps[:, tt, c * P:(c + 1) * P], yc[:, c, tt * P:(tt + 1) * P], ident)
                    ins.then_inc(S["xs_turned"], 1)
                job(5)
                pe.wait_ge(S["silu"], 7)
                for g in range(2):
                    for j in range(NT):
                        ins = pe.matmul(ps[:, 2 + g, j * T:(j + 1) * T], yc[:, 3 + g, j * P:(j + 1) * P],
                                        yc[:, 5 + g, :], start=True, stop=True)
                    ins.then_inc(S["cb"], 1)
                pe.wait_ge(S["conv"], NCONV)
                lru_gates(0)
                lru_gates(1)
                pe.wait_ge(S["cum_rows"], 2)
                pe.wait_ge(S["dt_rows"], 1)
                for q in range(4):
                    for tt in range(NT):
                        ins = pe.transpose(ps[:, 6, (2 * q + tt) * HEADS:(2 * q + tt + 1) * HEADS],
                                           dtr[0:HEADS, 2 + q // 2, q % 2, tt * P:(tt + 1) * P],
                                           ident[0:HEADS, 0:HEADS])
                ins.then_inc(S["dt_cols"], 1)
                seg_rows(0)
                seg_rows(1)
                job(6)
                lru_gates(2)
                lru_gates(3)
                seg_rows(2)
                ssd_y(0)
                job(7)
                ssd_y(1)
                seg_rows(3)
                rot(0)
                job(8)
                seg_rows(4)
                ssd_y(2)
                rot(1)
                job_v(0)
                seg_rows(5)
                ssd_y(3)
                rot(2)
                job_v(1)
                ssd_y(4)
                ssd_y(5)
                job(11)
                score(0)
                score(1)
                job(12)
                ret_sum(0)
                score(2)
                ret_sum(1)
                score(3)
                job(13)
                for hh in range(2, HEADS):
                    ret_sum(hh)
                    if hh + 2 < HEADS:
                        score(hh + 2)
                job(14)
                pe.wait_ge(S["ret_sq"], 1)
                pe.wait_ge(S["z_gate"], 3)
                for c in range(3):
                    ins = pe.matmul(ret_means[:, c, :], C("head_mean"), sq[:, c, :], start=True, stop=True)
                ins.then_inc(S["ret_mean"], 1)

                def out_proj(chunks, first, last):
                    for n in range(4):
                        tt, half = n // 2, n % 2
                        for c in chunks:
                            w = ring[:, PRE_SLOT[7 + c // 4], :].rearrange("p (c n) -> p c n", c=4)
                            unit(7 + c // 4)
                            ins = pe.matmul(ps[:, 4 + n, :], oT[:, c, tt * P:(tt + 1) * P],
                                            w[:, c % 4, half * 512:(half + 1) * 512],
                                            start=(first and c == chunks[0]), stop=(last and c == chunks[-1]))
                        if last:
                            ins.then_inc(S["mixed"], 1)

                pe.wait_ge(S["proj_evac"], 15)
                pe.wait_ge(S["mix_ready"], 1)
                out_proj((6, 7), True, False)
                pe.wait_ge(S["ssd_sq"], 1)
                gm = C("group_mean")
                lo, hi = slice(0, HD), slice(HD, P)
                m = [ssd_means[:, c, :] for c in range(3)]
                pe.matmul(m[0], gm, ssq[:, 0, :], start=True, stop=False)
                pe.matmul(m[0], gm[lo], ssq[lo, 1, :], start=False, stop=True)
                pe.matmul(m[1][lo], gm[:, lo], ssq[:, 0, :], start=True, stop=False)
                pe.matmul(m[1][lo], gm[lo, lo], ssq[lo, 1, :], start=False, stop=True)
                pe.matmul(m[1][hi], gm[:, lo], ssq[:, 2, :], start=True, stop=False)
                pe.matmul(m[1][hi], gm[hi, lo], ssq[hi, 1, :], start=False, stop=True)
                pe.matmul(m[2], gm, ssq[:, 2, :], start=True, stop=False)
                pe.matmul(m[2], gm[hi], ssq[hi, 1, :], start=False, stop=True).then_inc(S["ssd_mean"], 1)
                pe.wait_ge(S["mix_ready"], 2)
                out_proj((0, 1, 2), False, False)
                pe.wait_ge(S["mix_ready"], 5)
                out_proj((3, 4, 5), False, True)

    def attention(layer):
        wkv_v = a["ca_wkv"].rearrange("l (p k) n -> l p k n", k=NK)
        wq_v = a["ca_wq"].rearrange("l (p k) n -> l p k n", k=NK)
        wo_v = a["ca_wo"].rearrange("l (c p) n -> l p c n", p=P)
        with nc.Block() as block:
            @block.sync
            def _(sp):
                sp.dma_start(mem_sb, mem_v).then_inc(S["mem_in"], 16)
                free = {15: (S["kv"], 2), 16: (S["kv"], 4)}
                for u in range(9, 17):
                    if u in free:
                        sp.wait_ge(*free[u])
                    s = PRE_SLOT[u]
                    if u < 15:
                        w, c = (wkv_v, 512 * (u - 9)) if u < 13 else (wq_v, 512 * (u - 13))
                        dst = ring[:, s, :].rearrange("p (k n) -> p k n", k=NK)
                        src = w[bass.ds(layer, 1), :, :, c:c + 512].rearrange("l p k n -> p (l k) n")
                    else:
                        c = 4 * (u - 15)
                        dst = ring[:, s, :].rearrange("p (c n) -> p c n", c=4)
                        src = wo_v[bass.ds(layer, 1), :, c:c + 4, :].rearrange("l p c n -> p (l c) n")
                    sp.dma_start(dst, src).then_inc(full[s], 16)
                ready = ((S["kv"], 6), (S["kv"], 8), (S["q_proj"], 2), (S["q_proj"], 4), (S["att_out"], 4), (S["att_out"], 4))
                for e in range(2):
                    expert_loads(sp, layer * NE + e, e, lambda i: sp.wait_ge(*ready[3 * e + i]))

            @block.scalar
            def _(act):
                act.wait_ge(S["mem_in"], 16)
                norm_act(act, 1, mem_sb, memn, memT, 4)
                norm_act(act, 2, h, xn, xnT, 4)
                for n in range(0, 8, 2):
                    act.wait_ge(S["kv"], n + 1)
                    dst = kT[:, 2 * n:2 * n + 2, :] if n < 4 else vm[:, n % 2, (n // 2 - 2) * 512:(n // 2 - 1) * 512]
                    src = ps[:, n % 4, :]
                    if n < 4:
                        src = src.rearrange("p (a b) -> p a b", a=2)
                    act.activation(dst, src, ACT.Copy).then_inc(S["kv_evac"], 1)
                for n in range(0, 4, 2):
                    act.wait_ge(S["q_proj"], n + 1)
                    act.activation(qT[:, 2 * n:2 * n + 2, :], ps[:, n, :].rearrange("p (a b) -> p a b", a=2),
                                   ACT.Copy, scale=1.0 / 16.0).then_inc(S["q_evac"], 1)
                for hd in range(CA_HEADS):
                    act.wait_ge(S["att_max"], hd + 1)
                    for st in range(NT):
                        act.activation(prob[:, hd, st, :], ps[:, 4 + hd, st * T:(st + 1) * T], ACT.Exp,
                                       bias=att_stat[:, 0, hd, st:st + 1],
                                       accum_out=att_stat[:, 1, hd, st:st + 1]).then_inc(S["att_exp"], 1)
                for hd in range(0, CA_HEADS, 2):
                    act.wait_ge(S["att_turned"], hd + 1)
                    act.activation(probT[:, hd], ps[:, hd, :].rearrange("p (a b) -> p a b", a=2), ACT.Copy
                                   ).then_inc(S["att_pt"], 1)
                for hd in range(0, CA_HEADS, 2):
                    act.wait_ge(S["att_o"], hd + 1)
                    act.activation(attT[:, 2 * hd:2 * hd + 2, :], ps[:, 4 + hd, :].rearrange("p (a b) -> p a b", a=2),
                                   ACT.Copy).then_inc(S["att_oevac"], 1)

            @block.vector
            def _(vec):
                vec.wait_ge(S["mem_in"], 16)
                norm_vec(vec, 1, mem_sb, memn, memT, 4)
                norm_vec(vec, 2, h, xn, xnT, 4)
                for n in range(1, 8, 2):
                    vec.wait_ge(S["kv"], n + 1)
                    dst = kT[:, 2 * n:2 * n + 2, :] if n < 4 else vm[:, n % 2, (n // 2 - 2) * 512:(n // 2 - 1) * 512]
                    src = ps[:, n % 4, :]
                    if n < 4:
                        src = src.rearrange("p (a b) -> p a b", a=2)
                    vec.tensor_copy(dst, src).then_inc(S["kv_evac_vec"], 1)
                for n in range(1, 4, 2):
                    vec.wait_ge(S["q_proj"], n + 1)
                    vec.tensor_scalar(qT[:, 2 * n:2 * n + 2, :], ps[:, n, :].rearrange("p (a b) -> p a b", a=2),
                                      1.0 / 16.0, None, ALU.mult).then_inc(S["q_evac_vec"], 1)
                for hd in range(CA_HEADS):
                    vec.wait_ge(S["att_score"], hd + 1)
                    vec.tensor_reduce(att_stat[:, 0, hd, :], ps[:, 4 + hd, :].rearrange("p (a b) -> p a b", a=2),
                                      AX_X, ALU.max, negate=True).then_inc(S["att_max"], 1)
                mark, link = chained(vec, S["att_step"])
                for hd in range(CA_HEADS):
                    vec.wait_ge(S["att_exp"], 2 * hd + 2)
                    link(vec.reciprocal(att_stat[:, 2, hd, :], att_stat[:, 1, hd, :]))
                    for st in range(NT):
                        vec.tensor_scalar(prob[:, hd, st, :], prob[:, hd, st, :], att_stat[:, 2, hd, st:st + 1],
                                          None, ALU.mult).then_inc(S["att_prob"], 1)
                for hd in range(1, CA_HEADS, 2):
                    vec.wait_ge(S["att_turned"], hd + 1)
                    vec.tensor_copy(probT[:, hd], ps[:, hd, :].rearrange("p (a b) -> p a b", a=2)
                                    ).then_inc(S["att_pt_vec"], 1)
                for hd in range(1, CA_HEADS, 2):
                    vec.wait_ge(S["att_o"], hd + 1)
                    vec.tensor_copy(attT[:, 2 * hd:2 * hd + 2, :],
                                    ps[:, 4 + hd, :].rearrange("p (a b) -> p a b", a=2)).then_inc(S["att_oevac_vec"], 1)
                for n in range(4):
                    vec.wait_ge(S["att_out"], n + 1)
                    hs = h[:, n // 2, (n % 2) * 512:(n % 2 + 1) * 512]
                    vec.tensor_tensor(hs, hs, ps[:, n, :], ALU.add).then_inc(S["att_added"], 1)

            @block.tensor
            def _(pe):
                def unit(u):
                    pe.wait_ge(full[PRE_SLOT[u]], 16 * sum(PRE_SLOT[v] == PRE_SLOT[u] for v in range(u + 1)))
                    return ring[:, PRE_SLOT[u], :]

                norm_pe(pe, 1, memn, 4)
                normed_T_ready(pe, 1)
                norm_pe(pe, 2, xn, 4)
                for n in range(4):
                    w = unit(9 + n // 2).rearrange("p (k n) -> p k n", k=NK)
                    for b in range(2):
                        c0 = ((2 * n + b) % 4) * P
                        for k in range(NK):
                            ins = pe.matmul(ps[:, n, b * T:(b + 1) * T], w[:, k, c0:c0 + P], memT[:, k, :],
                                            start=(k == 0), stop=(k == NK - 1))
                    ins.then_inc(S["kv"], 1)
                for n in range(4, 8):
                    w = unit(9 + n // 2).rearrange("p (k n) -> p k n", k=NK)
                    pe.wait_ge(S["kv_evac"] if n % 2 == 0 else S["kv_evac_vec"], n // 2 - 1)
                    for k in range(NK):
                        ins = pe.matmul(ps[:, n % 4, :], memT[:, k, (n % 2) * P:(n % 2 + 1) * P], w[:, k, :],
                                        start=(k == 0), stop=(k == NK - 1))
                    ins.then_inc(S["kv"], 1)
                normed_T_ready(pe, 2)
                for n in range(4):
                    w = unit(13 + n // 2).rearrange("p (k n) -> p k n", k=NK)
                    pe.wait_ge(S["kv_evac"] if n % 2 == 0 else S["kv_evac_vec"], n // 2 + 3)
                    for b in range(2):
                        c0 = ((2 * n + b) % 4) * P
                        for k in range(NK):
                            ins = pe.matmul(ps[:, n, b * T:(b + 1) * T], w[:, k, c0:c0 + P], xnT[:, k, :],
                                            start=(k == 0), stop=(k == NK - 1))
                    ins.then_inc(S["q_proj"], 1)
                for hd in range(CA_HEADS):
                    pe.wait_ge(S["q_evac"] if hd % 2 == 0 else S["q_evac_vec"], hd // 2 + 1)
                    for st in range(NT):
                        for c in range(2):
                            ins = pe.matmul(ps[:, 4 + hd, st * T:(st + 1) * T],
                                            qT[:, 2 * hd + c, st * P:(st + 1) * P], kT[:, 2 * hd + c, :],
                                            start=(c == 0), stop=(c == 1))
                    ins.then_inc(S["att_score"], 1)
                for hd in range(CA_HEADS):
                    pe.wait_ge(S["att_prob"], 2 * hd + 2)
                    for mt in range(NT):
                        for st in range(NT):
                            ins = pe.transpose(ps[:, hd, mt * T + st * P:mt * T + (st + 1) * P],
                                               prob[:, hd, st, mt * P:(mt + 1) * P], ident)
                    ins.then_inc(S["att_turned"], 1)
                for hd in range(CA_HEADS):
                    pe.wait_ge(S["att_pt"] if hd % 2 == 0 else S["att_pt_vec"], hd // 2 + 1)
                    for c in range(2):
                        for mt in range(NT):
                            o = hd * 2 * P + c * P
                            ins = pe.matmul(ps[:, 4 + hd, c * T:(c + 1) * T], vm[:, mt, o:o + P],
                                            probT[:, hd, mt, :], start=(mt == 0), stop=(mt == 1))
                    ins.then_inc(S["att_o"], 1)
                pe.wait_ge(S["att_oevac"], 2)
                pe.wait_ge(S["att_oevac_vec"], 2)
                wo = [unit(15 + i).rearrange("p (c n) -> p c n", c=4) for i in range(2)]
                for n in range(4):
                    for c in range(NK):
                        ins = pe.matmul(ps[:, n, :], attT[:, c, (n // 2) * P:(n // 2 + 1) * P],
                                        wo[c // 4][:, c % 4, (n % 2) * 512:(n % 2 + 1) * 512],
                                        start=(c == 0), stop=(c == NK - 1))
                    ins.then_inc(S["att_out"], 1)

    w1_v = a["moe_w1"].rearrange("l e (p k) f -> (l e) p k f", k=NK)
    w3_v = a["moe_w3"].rearrange("l e (p k) f -> (l e) p k f", k=NK)
    w2_v = a["moe_w2"].rearrange("l e (half p b) d -> (l e) p half b d", half=2, b=2)

    def expert_unit(par, i):
        return (EXPERT_SLOT0 + 3 * par + i) % RING

    def expert_loads(sp, which, par, wait_free):
        for i in range(3):
            wait_free(i)
            s = expert_unit(par, i)
            if i < 2:
                dst = ring[:, s, :].rearrange("p (w k n) -> p w k n", w=2, k=4)
                for w, v in enumerate((w1_v, w3_v)):
                    src = v[bass.ds(which, 1), :, 4 * i:4 * i + 4, :].rearrange("e p k f -> p (e k) f")
                    sp.dma_start(dst[:, w], src).then_inc(xfull[s], 16)
            else:
                dst = ring[:, s, :].rearrange("p (half b d) -> p half b d", half=2, b=2)
                for half in range(2):
                    src = w2_v[bass.ds(which, 1), :, half, :, :].rearrange("e p b d -> p (e b) d")
                    sp.dma_start(dst[:, half], src).then_inc(xfull[s], 16)

    def hidden_matmuls(pe, par, i, lhs, bank):
        w = ring[:, expert_unit(par, i), :].rearrange("p (w k n) -> p w k n", w=2, k=4)
        for k in range(4):
            for j in range(4):
                ins = pe.matmul(ps[CAP * j:CAP * (j + 1), bank, 0:T], lhs(4 * i + k),
                                w[:, j // 2, k, (j % 2) * T:(j % 2 + 1) * T], start=(i == 0 and k == 0),
                                stop=(i == 1 and k == 3))
        return ins

    def down_matmuls(pe, par, hT, bank):
        w = ring[:, expert_unit(par, 2), :].rearrange("p (f d) -> p f d", f=4)
        for f in range(4):
            for j in range(4):
                ins = pe.matmul(ps[CAP * j:CAP * (j + 1), bank, 0:T], hT[:, f % 2, (f // 2) * CAP:(f // 2 + 1) * CAP],
                                w[:, f, j * T:(j + 1) * T], start=(f == 0), stop=(f == 3))
        return ins

    def router(layer):
        def gathered(k):
            return ps[:, k // 2, (k % 2) * TURN:(k % 2 + 1) * TURN].rearrange("p (q s) -> p q s", q=2)

        with nc.Block() as block:
            @block.scalar
            def _(act):
                norm_act(act, 3, h, xn, xnT, 0)
                act.wait_ge(S["logits_sb"], 1)
                act.activation(r_ge, r_ge, ACT.Exp).then_inc(S["group_exp"], 1)
                act.wait_ge(S["gate_exp"], 1)
                act.activation(r_m2, r_m2, ACT.Exp).then_inc(S["gate_exp"], 1)
                for k in (0, 1, 4, 5):
                    act.wait_ge(S["gather"], k // 2 + 1)
                    act.activation(stage[:, :, k, :], gathered(k), ACT.Copy, scale=gains[:, 3, k:k + 1]
                                   ).then_inc(S["gather_act"], 1)

            @block.vector
            def _(vec):
                norm_vec(vec, 3, h, xn, xnT, 0)
                mark, link = chained(vec, S["route_step"])
                vec.wait_ge(S["logits"], 1)
                lg = r_lg
                for tt in range(NT):
                    n = mark(vec.tensor_tensor(lg[:, tt, :], ps[:, 4 + tt, 0:GROUPS + NE], bge[:, :], ALU.add))
                link(vec.tensor_scalar(r_iota, C("iota", 0, PER_GROUP), -64.0, None, ALU.add))

                def over(x, n):
                    return x.unsqueeze(2).to_broadcast([P, NT, n])

                def first_max(x, mx_, one, n):
                    iota = r_iota[:, 0:n].unsqueeze(1).to_broadcast([P, NT, n])
                    link(vec.tensor_reduce(mx_, x, AX_X, ALU.max))
                    link(vec.tensor_tensor(one, x, over(mx_, n), ALU.is_equal))
                    link(vec.tensor_tensor(one, one, iota, ALU.mult))
                    link(vec.tensor_reduce(r_min, one, AX_X, ALU.min))
                    link(vec.tensor_tensor(one, iota, over(r_min, n), ALU.is_equal))

                first_max(lg[:, :, 0:GROUPS], r_gm, r_og, GROUPS)
                vec.tensor_tensor(r_ge, lg[:, :, 0:GROUPS], over(r_gm, GROUPS), ALU.subtract).then_inc(S["logits_sb"], 1)
                l4 = lg[:, :, GROUPS:].rearrange("p t (g e) -> p t g e", g=GROUPS)
                for tt in range(NT):
                    og = r_og[:, tt, :].unsqueeze(2).to_broadcast([P, GROUPS, PER_GROUP])
                    link(vec.tensor_tensor(r_t4[:, tt], l4[:, tt], og, ALU.mult))
                    link(vec.tensor_reduce(r_el[:, tt, :], r_t4[:, tt].rearrange("p g e -> p e g"), AX_X, ALU.add))
                first_max(r_el, r_m1, r_o1, PER_GROUP)
                link(vec.scalar_tensor_tensor(r_el, r_o1, -1e30, r_el, ALU.mult, ALU.add))
                first_max(r_el, r_m2, r_o2, PER_GROUP)
                vec.tensor_tensor(r_m2, r_m2, r_m1, ALU.subtract).then_inc(S["gate_exp"], 1)
                vec.wait_ge(S["group_exp"], 1)
                link(vec.tensor_reduce(r_gm, r_ge, AX_X, ALU.add))
                vec.wait_ge(S["gate_exp"], 2)
                link(vec.tensor_scalar(r_m1, r_m2, 1.0, None, ALU.add))
                link(vec.tensor_tensor(r_gm, r_gm, r_m1, ALU.mult))
                link(vec.reciprocal(slotc[:, :, 2], r_gm))
                link(vec.tensor_tensor(slotc[:, :, 3], slotc[:, :, 2], r_m2, ALU.mult))
                for tt in range(NT):
                    og = r_og[:, tt, :].unsqueeze(2).to_broadcast([P, GROUPS, PER_GROUP])
                    for o, e in ((r_o1, r_e1), (r_o2, r_e2)):
                        ob = o[:, tt, :].unsqueeze(1).to_broadcast([P, GROUPS, PER_GROUP])
                        link(vec.tensor_tensor(e[:, tt].rearrange("p (g e) -> p g e", g=GROUPS), og, ob, ALU.mult))
                vec.tensor_tensor(r_ea, r_e1, r_e2, ALU.add).then_inc(S["routed"], 1)
                vec.wait_ge(S["rank_mm"], 1)
                link(vec.tensor_copy(r_cnt, ps[:, 6, 2 * NE:3 * NE]))
                link(vec.tensor_scalar(r_nov, r_cnt, float(CAP), None, ALU.is_gt))
                for m in range(2, T // CAP):
                    link(vec.scalar_tensor_tensor(r_nov, r_cnt, float(CAP * m), r_nov, ALU.is_gt, ALU.add))
                one = C("ones", 0, NE)
                link(vec.tensor_tensor_scan(ov_table[:, 0:NE], one, r_nov, 0.0, ALU.mult, ALU.add))
                link(vec.tensor_copy(ov_int[:, 0:1], ov_table[:, NE - 1:NE]))
                link(vec.tensor_tensor(r_nov, ov_table[:, 0:NE], r_nov, ALU.subtract))
                link(vec.scalar_tensor_tensor(r_nov, r_nov, float(CAP), C("first_slot"), ALU.mult, ALU.subtract))
                link(vec.tensor_scalar(r_nov, r_nov, float(SLOTS - CAP), None, ALU.add))
                rank = ps[:, 6, 0:2 * NE].rearrange("p (t e) -> p t e", t=NT)
                for tt in range(NT):
                    link(vec.scalar_tensor_tensor(r_sv[:, tt, :], rank[:, tt, :], float(CAP), r_nov, ALU.is_ge,
                                                  ALU.mult))
                    link(vec.tensor_tensor(r_sv[:, tt, :], r_sv[:, tt, :], rank[:, tt, :], ALU.add))
                    link(vec.tensor_tensor(r_sv[:, tt, :], r_sv[:, tt, :], C("first_slot"), ALU.add))
                for i, e in enumerate((r_e1, r_e2)):
                    link(vec.tensor_tensor(e, e, r_sv, ALU.mult))
                    link(vec.tensor_reduce(slotc[:, :, i], e, AX_X, ALU.add))
                for tt in range(NT):
                    mark(vec.tensor_scalar(sel[:, tt, :], C("iota", 0, TURN), slotc[:, tt, 0:1], None, ALU.is_equal))
                link(vec.tensor_scalar(slot_left, slotc[:, :, 0:2], -float(TURN), None, ALU.add))
                for tt in range(NT):
                    vec.scalar_tensor_tensor(sel[:, tt, :], C("iota", 0, TURN), slotc[:, tt, 1:2], sel[:, tt, :],
                                             ALU.is_equal, ALU.add).then_inc(S["sel"], 1)
                for tt in range(NT):
                    for q in range(4):
                        ins = vec.tensor_scalar(diag[:, tt, q, :], ident, slotc[:, tt, q:q + 1], None, ALU.mult)
                        ins.then_inc(S["diag"], 1)
                for tt in range(NT):
                    vec.wait_ge(S["diag_mm"], tt + 1)
                    vec.tensor_copy(rows4[:, :, tt * P:(tt + 1) * P], ps[:, 4 + tt, :].rearrange("p (q s) -> p q s", q=4)
                                    ).then_inc(S["bcast"], 1)
                vec.tensor_copy(slot_id[:, :], C("part")).then_inc(S["bcast"], 1)
                vec.memset(ov_at[:, 0:1], float(SLOTS)).then_inc(S["bcast"], 1)
                vec.memset(ov_at[:, 1:2], 0.0).then_inc(S["bcast"], 1)
                for k in (2, 3, 6, 7):
                    vec.wait_ge(S["gather"], k // 2 + 1)
                    vec.tensor_scalar(stage[:, :, k, :], gathered(k), gains[:, 3, k:k + 1], None, ALU.mult
                                      ).then_inc(S["gather_vec"], 1)

            @block.tensor
            def _(pe):
                norm_pe(pe, 3, xn, 0)
                normed_T_ready(pe, 3)
                for tt in range(NT):
                    for k in range(NK):
                        ins = pe.matmul(ps[:, 4 + tt, 0:GROUPS + NE], xnT[:, k, tt * P:(tt + 1) * P], wge[:, k, :],
                                        start=(k == 0), stop=(k == NK - 1))
                ins.then_inc(S["logits"], 1)
                pe.wait_ge(S["routed"], 1)
                pe.matmul(ps[:, 6, 0:NE], C("before"), r_ea[:, 0, :], start=True, stop=True)
                pe.matmul(ps[:, 6, NE:2 * NE], C("ones"), r_ea[:, 0, :], start=True, stop=False)
                pe.matmul(ps[:, 6, NE:2 * NE], C("before"), r_ea[:, 1, :], start=False, stop=True)
                pe.matmul(ps[:, 6, 2 * NE:3 * NE], C("ones"), r_ea[:, 0, :], start=True, stop=False)
                pe.matmul(ps[:, 6, 2 * NE:3 * NE], C("ones"), r_ea[:, 1, :], start=False, stop=True
                          ).then_inc(S["rank_mm"], 1)
                pe.wait_ge(S["sel"], 2)
                for k in range(NK):
                    for tt in range(NT):
                        ins = pe.matmul(ps[:, k // 2, (k % 2) * TURN:(k % 2 + 1) * TURN], xn[:, tt, k::NK], sel[:, tt, :],
                                        start=(tt == 0), stop=(tt == NT - 1))
                    if k % 2:
                        ins.then_inc(S["gather"], 1)
                for tt in range(NT):
                    pe.wait_ge(S["diag"], 4 * tt + 4)
                    pe.matmul(ps[:, 4 + tt, :], C("ones"), diag[:, tt].rearrange("p q s -> p (q s)"), start=True,
                              stop=True).then_inc(S["diag_mm"], 1)

    def experts(layer):
        H0, C0, A0 = 16, 8, 2
        G0, ST0 = 4, 2
        turns = SLOTS // TURN
        GATHER_AT = (2, 3, 4, 5)
        with nc.Block() as block:
            @block.sync
            def _(sp):
                with sp.Fori(0, NE // 2 - 1) as it:
                    for par in range(2):
                        e = 2 * it + par

                        def wait_free(i):
                            if i < 2:
                                sp.wait_ge(S["x_hidden"], sp.snap(2 * e + i + 1 + H0))
                            else:
                                sp.wait_ge(S["x_y"], sp.snap(e + 1))

                        expert_loads(sp, layer * NE + e + 2, par, wait_free)
                with sp.If(layer < DEPTH - 1):
                    following = nc.s_assert_within(layer + 1, 1, DEPTH - 1, skip_runtime_bounds_check_because=
                                                   "this branch is taken where layer is below DEPTH - 1")
                    with nc.allow_non_contiguous_dma(reason="a few bytes"):
                        for dst, src in mixer_param_loads(following):
                            sp.dma_start(dst, src).then_inc(next_params, 16)
                    sp.wait_ge(next_params, sp.snap(MIX_PARAMS * (layer + 2)))
                    for u in range(EARLY):
                        assert PRE_SLOT[u] == expert_unit(1, u)
                        sp.wait_ge(S["x_hidden"], 2 * NE - 1 + u + H0) if u < 2 else sp.wait_ge(S["x_y"], NE)
                        w_in_load(sp, following, u, next_unit[u])
                with sp.Else():
                    pass

            @block.gpsimd
            def _(pool):
                pool.sem_inc(S["x_stage"], ST0)
                with pool.Fori(0, turns - 1) as it:
                    for q in range(2):
                        pool.wait_ge(S["x_gather_act"], pool.snap(4 * it + 4 + G0))
                        pool.wait_ge(S["x_hidden"], pool.snap(16 * it + 8 * q + 8 + H0))
                        pool.sem_inc(S["x_stage_free"], 1)
                        pool.tensor_copy(stage[:, q], nextT[:, :, q * P:(q + 1) * P]).then_inc(S["x_stage"], 1)

            @block.scalar
            def _(act):
                act.sem_inc(S["x_yact"], A0)
                act.sem_inc(S["x_gather_act"], G0)
                with act.Fori(0, turns) as it:
                    for r in range(8):
                        q, b = r // 4, r % 2
                        act.wait_ge(S["x_hidden"], act.snap(16 * it + 2 * r + 2 + H0))
                        act.activation(gated[0:64, b, :], ps[0:64, b, 0:T], ACT.Tanh, scale=0.5).then_inc(S["x_tanh"], 1)
                        act.wait_ge(S["x_hT"], act.snap(8 * it + r + 1))
                        act.activation(hTs[:, b], ps[:, 2, 0:4 * CAP].rearrange("p (a b) -> p a b", a=2), ACT.Copy
                                       ).then_inc(S["x_hTsb"], 1)
                        if r in GATHER_AT:
                            i = GATHER_AT.index(r)
                            act.wait_ge(S["x_gather"], act.snap(4 * it + i + 1 + G0))
                            if i == 0:
                                act.wait_ge(S["x_stage"], act.snap(2 * it + ST0))
                            for c in range(2):
                                k = 2 * i + c
                                ins = act.activation(nextT[:, k, :], ps[:, 3, c * TURN:(c + 1) * TURN], ACT.Copy,
                                                     scale=gains[:, 3, k:k + 1])
                            ins.then_inc(S["x_gather_act"], 1)
                        act.wait_ge(S["x_y"], act.snap(8 * it + r + 1))
                        if r % 4 == 0:
                            act.wait_ge(S["x_scat"], act.snap(8 * it + 4 * q + 4))
                        lo = CAP * (r % 4)
                        for j in range(2):
                            ins = act.activation(ysb[lo:lo + CAP, q, j * T:(j + 1) * T],
                                                 ps[CAP * j:CAP * (j + 1), 4 + b, 0:T], ACT.Copy)
                        ins.then_inc(S["x_yact"], 1)

            @block.vector
            def _(vec):
                vec.sem_inc(S["x_h"], A0)
                vec.sem_inc(S["x_yvec"], A0)
                vec.sem_inc(S["x_added"], A0)
                with vec.Fori(0, turns) as it:
                    for r in range(8):
                        q, b = r // 4, r % 2
                        if r % 4 == 0:
                            vec.wait_ge(S["x_scat"], vec.snap(8 * it + 4 * q + 4))
                            step = 4 * q
                            vec.scalar_tensor_tensor(selT[:, q, :], rows4[:, 0, :], slot_id[:, 0:1], rows4[:, 2, :],
                                                     ALU.is_equal, ALU.mult).then_inc(S["x_vec"], 1)
                            vec.scalar_tensor_tensor(rows_t, rows4[:, 1, :], slot_id[:, 0:1], rows4[:, 3, :],
                                                     ALU.is_equal, ALU.mult).then_inc(S["x_vec"], 1)
                            vec.wait_ge(S["x_vec"], vec.snap(6 * it + 3 * q + 2))
                            vec.tensor_tensor(selT[:, q, :], selT[:, q, :], rows_t, ALU.add).then_inc(S["x_selT"], 1)
                            vec.tensor_scalar(slot_id[:, :], slot_id[:, :], float(P), None, ALU.add
                                              ).then_inc(S["x_vec"], 1)
                            vec.wait_ge(S["x_vec"], vec.snap(6 * it + 3 * q + 3))
                            vec.wait_ge(S["x_selT"], vec.snap(2 * it + q + 1))
                        if r == 1:
                            vec.wait_ge(S["x_gather"], vec.snap(4 * it + G0))
                            for tt in range(NT):
                                vec.tensor_scalar(sel[:, tt, :], C("iota", 0, TURN), slot_left[:, tt, 0:1], None,
                                                  ALU.is_equal).then_inc(S["x_sel"], 1)
                            vec.wait_ge(S["x_sel"], vec.snap(5 * it + 2))
                            for tt in range(NT):
                                vec.scalar_tensor_tensor(sel[:, tt, :], C("iota", 0, TURN), slot_left[:, tt, 1:2],
                                                         sel[:, tt, :], ALU.is_equal, ALU.add).then_inc(S["x_sel"], 1)
                            vec.wait_ge(S["x_sel"], vec.snap(5 * it + 4))
                            vec.tensor_scalar(slot_left, slot_left, -float(TURN), None, ALU.add
                                              ).then_inc(S["x_sel"], 1)
                            vec.wait_ge(S["x_sel"], vec.snap(5 * it + 5))
                        vec.wait_ge(S["x_tanh"], vec.snap(8 * it + r + 1))
                        vec.scalar_tensor_tensor(gated[64:128, b, :], gated[0:64, b, :], 1.0, ps[0:64, b, 0:T],
                                                 ALU.add, ALU.mult).then_inc(S["x_gated"], 1)
                        vec.wait_ge(S["x_gated"], vec.snap(8 * it + r + 1))
                        vec.scalar_tensor_tensor(hsb[64:128, b, :], gated[64:128, b, :], 0.5, ps[64:128, b, 0:T],
                                                 ALU.mult, ALU.mult).then_inc(S["x_h"], 1)
                        vec.wait_ge(S["x_y"], vec.snap(8 * it + r + 1))
                        lo = CAP * (r % 4)
                        for j in range(2, 4):
                            ins = vec.tensor_copy(ysb[lo:lo + CAP, q, j * T:(j + 1) * T],
                                                  ps[CAP * j:CAP * (j + 1), 4 + b, 0:T])
                        ins.then_inc(S["x_yvec"], 1)
                        if r % 4 == 3:
                            for n in range(4):
                                vec.wait_ge(S["x_scat"], vec.snap(8 * it + 4 * q + n + 1 + C0))
                                hs = h[:, n // 2, (n % 2) * 512:(n % 2 + 1) * 512]
                                vec.tensor_tensor(hs, hs, ps[:, 6 + n % 2, :], ALU.add).then_inc(S["x_added"], 1)

            @block.tensor
            def _(pe):
                pe.sem_inc(S["x_hidden"], H0)
                pe.sem_inc(S["x_scat"], C0)
                pe.sem_inc(S["x_gather"], G0)
                with pe.Fori(0, turns) as it:
                    for r in range(8):
                        q, b, par = r // 4, r % 2, r % 2
                        if r % 4 == 0:
                            pe.wait_ge(S["x_stage"], pe.snap(2 * it + q - 1 + ST0))
                        pe.wait_ge(S["x_h"], pe.snap(8 * it + r + A0 - 1))
                        for i in range(2):
                            pe.wait_ge(xfull[expert_unit(par, i)], pe.snap(128 * it + 32 * (r // 2 + 1)))
                            hidden_matmuls(pe, par, i, lambda k: stage[:, q, k, CAP * (r % 4):CAP * (r % 4 + 1)], b
                                           ).then_inc(S["x_hidden"], 1)
                        if r in GATHER_AT:
                            i = GATHER_AT.index(r)
                            pe.wait_ge(S["x_sel"], pe.snap(5 * it + 4))
                            pe.wait_ge(S["x_gather_act"], pe.snap(4 * it + i + G0))
                            for c in range(2):
                                for tt in range(NT):
                                    ins = pe.matmul(ps[:, 3, c * TURN:(c + 1) * TURN], xn[:, tt, 2 * i + c::NK],
                                                    sel[:, tt, :], start=(tt == 0), stop=(tt == NT - 1))
                            ins.then_inc(S["x_gather"], 1)
                        pe.wait_ge(S["x_h"], pe.snap(8 * it + r + A0 + 1))
                        for f in range(2):
                            ins = pe.matmul(ps[:, 2, f * 64:(f + 1) * 64], hsb[64:128, b, f::2],
                                            ident[64:128, 64:128], start=True, stop=True)
                        ins.then_inc(S["x_hT"], 1)
                        pe.wait_ge(S["x_hTsb"], pe.snap(8 * it + r + 1))
                        pe.wait_ge(S["x_yact"], pe.snap(8 * it + r + A0 - 1))
                        pe.wait_ge(S["x_yvec"], pe.snap(8 * it + r + A0 - 1))
                        pe.wait_ge(xfull[expert_unit(par, 2)], pe.snap(128 * it + 32 * (r // 2 + 1)))
                        down_matmuls(pe, par, hTs[:, b], 4 + b).then_inc(S["x_y"], 1)
                        if r % 4 == 3:
                            pe.wait_ge(S["x_yact"], pe.snap(8 * it + r + A0 + 1))
                            pe.wait_ge(S["x_yvec"], pe.snap(8 * it + r + A0 + 1))
                            pe.wait_ge(S["x_selT"], pe.snap(2 * it + q + 1))
                            for n in range(4):
                                tt, half = n // 2, n % 2
                                pe.wait_ge(S["x_added"], pe.snap(8 * it + 4 * q + n + A0 - 1))
                                pe.matmul(ps[:, 6 + n % 2, :], selT[:, q, tt * P:(tt + 1) * P],
                                          ysb[:, q, half * 512:(half + 1) * 512], start=True, stop=True
                                          ).then_inc(S["x_scat"], 1)

    def overflow(layer):
        with nc.Block() as block:
            @block.sync
            def _(sp):
                sp.wait_ge(S["ov_w"], 1)
                e = sp.value_load(ov_int[0:1, 1:2], min_val=0, max_val=NE - 1)
                expert_loads(sp, layer * NE + e, 0, lambda i: None)

            @block.scalar
            def _(act):
                act.wait_ge(S["x_hidden"], 2)
                act.activation(gated[0:64, 0, :], ps[0:64, 1, 0:T], ACT.Tanh, scale=0.5).then_inc(S["x_tanh"], 1)
                act.wait_ge(S["x_hT"], 1)
                act.activation(hTs[:, 0], ps[:, 2, 0:4 * CAP].rearrange("p (a b) -> p a b", a=2), ACT.Copy
                               ).then_inc(S["x_hTsb"], 1)

            @block.vector
            def _(vec):
                mark, link = chained(vec, S["ov_step"])
                link(vec.tensor_scalar(ov_f, ov_table[:, 0:NE], ov_at[:, 1:2], None, ALU.is_le))
                link(vec.tensor_reduce(ov_at[:, 2:3], ov_f, AX_X, ALU.add))
                vec.tensor_copy(ov_int[:, 1:2], ov_at[:, 2:3]).then_inc(S["ov_w"], 1)
                for tt in range(NT):
                    link(vec.tensor_scalar(ov_s, C("iota", 0, CAP), ov_at[:, 0:1], slotc[:, tt, 0:1], ALU.add,
                                           ALU.is_equal))
                    link(vec.tensor_scalar(ov_sel[:, tt, :], C("iota", 0, CAP), ov_at[:, 0:1], slotc[:, tt, 1:2],
                                           ALU.add, ALU.is_equal))
                    vec.tensor_tensor(ov_sel[:, tt, :], ov_sel[:, tt, :], ov_s, ALU.add).then_inc(S["ov_sel"], 1)
                    vec.wait_ge(S["ov_sel"], tt + 1)
                link(vec.tensor_tensor(ov_at[:, 3:4], C("part"), ov_at[:, 0:1], ALU.add))
                link(vec.scalar_tensor_tensor(selT[:, 0, :], rows4[:, 0, :], ov_at[:, 3:4], rows4[:, 2, :],
                                              ALU.is_equal, ALU.mult))
                link(vec.scalar_tensor_tensor(rows_t, rows4[:, 1, :], ov_at[:, 3:4], rows4[:, 3, :],
                                              ALU.is_equal, ALU.mult))
                vec.tensor_tensor(selT[:, 0, :], selT[:, 0, :], rows_t, ALU.add).then_inc(S["x_selT"], 1)
                vec.wait_ge(S["ov_x"], 1)
                vec.tensor_tensor(ov_x, ps[:, 0, 0:NK * CAP].rearrange("p (k s) -> p k s", k=NK),
                                  gains[:, 3, :].unsqueeze(2).to_broadcast([P, NK, CAP]), ALU.mult
                                  ).then_inc(S["ov_xT"], 1)
                vec.wait_ge(S["x_tanh"], 1)
                vec.scalar_tensor_tensor(gated[64:128, 0, :], gated[0:64, 0, :], 1.0, ps[0:64, 1, 0:T],
                                         ALU.add, ALU.mult).then_inc(S["x_gated"], 1)
                vec.wait_ge(S["x_gated"], 1)
                vec.scalar_tensor_tensor(hsb[64:128, 0, :], gated[64:128, 0, :], 0.5, ps[64:128, 1, 0:T],
                                         ALU.mult, ALU.mult).then_inc(S["x_h"], 1)
                vec.wait_ge(S["x_y"], 1)
                for j in range(4):
                    vec.tensor_copy(ysb[0:CAP, 0, j * T:(j + 1) * T], ps[CAP * j:CAP * (j + 1), 4, 0:T]
                                    ).then_inc(S["x_yvec"], 1)
                for n in range(4):
                    vec.wait_ge(S["x_scat"], n + 1)
                    hs = h[:, n // 2, (n % 2) * 512:(n % 2 + 1) * 512]
                    vec.tensor_tensor(hs, hs, ps[:, 6 + n % 2, :], ALU.add).then_inc(S["x_added"], 1)
                link(vec.tensor_scalar(ov_at[:, 0:1], ov_at[:, 0:1], float(CAP), None, ALU.add))
                link(vec.tensor_scalar(ov_at[:, 1:2], ov_at[:, 1:2], 1.0, None, ALU.add))

            @block.tensor
            def _(pe):
                pe.wait_ge(S["ov_sel"], 2)
                for k in range(NK):
                    for tt in range(NT):
                        ins = pe.matmul(ps[:, 0, k * CAP:(k + 1) * CAP], xn[:, tt, k::NK], ov_sel[:, tt, :],
                                        start=(tt == 0), stop=(tt == NT - 1))
                ins.then_inc(S["ov_x"], 1)
                pe.wait_ge(S["ov_xT"], 1)
                for i in range(2):
                    pe.wait_ge(xfull[expert_unit(0, i)], 32)
                    hidden_matmuls(pe, 0, i, lambda k: ov_x[:, k, :], 1).then_inc(S["x_hidden"], 1)
                pe.wait_ge(S["x_h"], 1)
                for f in range(2):
                    ins = pe.matmul(ps[:, 2, f * 64:(f + 1) * 64], hsb[64:128, 0, f::2], ident[64:128, 64:128],
                                    start=True, stop=True)
                ins.then_inc(S["x_hT"], 1)
                pe.wait_ge(S["x_hTsb"], 1)
                pe.wait_ge(xfull[expert_unit(0, 2)], 32)
                down_matmuls(pe, 0, hTs[:, 0], 4).then_inc(S["x_y"], 1)
                pe.wait_ge(S["x_yvec"], 4)
                pe.wait_ge(S["x_selT"], 1)
                for n in range(4):
                    tt, half = n // 2, n % 2
                    if n >= 2:
                        pe.wait_ge(S["x_added"], n - 1)
                    pe.matmul(ps[:, 6 + n % 2, :], selT[0:CAP, 0, tt * P:(tt + 1) * P],
                              ysb[0:CAP, 0, half * 512:(half + 1) * 512], start=True, stop=True).then_inc(S["x_scat"], 1)

    with nc.Fori(0, DEPTH) as layer:
        mixer(layer)
        attention(layer)
        router(layer)
        experts(layer)
        nc.sync.sem_clear(layer_sems)
        nc.all_engine_barrier()
        overflow_blocks = nc.values_load(ov_int[0:1, 0:1], min_val=0, max_val=OV_BLOCKS)
        with nc.If(overflow_blocks > 0):
            with nc.Fori(0, overflow_blocks):
                overflow(layer)
                nc.sync.sem_clear(layer_sems)
                nc.all_engine_barrier()
        with nc.Else():
            pass

    with nc.Block() as block:
        @block.sync
        def _(sp):
            sp.dma_start(ysb[:, 0, :], a["g_final"].rearrange("(o d) -> o d", o=1).to_broadcast([P, D])
                         ).then_inc(consts_in, 16)
            sp.wait_ge(S["mixed"], NT)
            sp.dma_start(out_v, xn[:, :, :]).then_inc(consts_in, 16)
            sp.wait_ge(consts_in, 80)

        @block.scalar
        def _(act):
            for tt in range(NT):
                act.activation(xn[:, tt, :], h[:, tt, :], ACT.Square, accum_out=stat[:, 0, tt, 0:1]
                               ).then_inc(S["squared"], 1)
            act.wait_ge(S["variance"], 1)
            act.activation(stat[:, 0, :, 2], stat[:, 0, :, 1], ACT.Sqrt).then_inc(S["deviation"], 1)

        @block.vector
        def _(vec):
            vec.wait_ge(S["squared"], NT)
            vec.tensor_scalar(stat[:, 0, :, 1], stat[:, 0, :, 0], 1.0 / D, EPS, ALU.mult, ALU.add
                              ).then_inc(S["variance"], 1)
            vec.wait_ge(S["deviation"], 1)
            vec.reciprocal(stat[:, 0, :, 3], stat[:, 0, :, 2]).then_inc(S["inverse"], 1)
            vec.wait_ge(S["inverse"], 1)
            vec.wait_ge(consts_in, 64)
            for tt in range(NT):
                vec.scalar_tensor_tensor(xn[:, tt, :], h[:, tt, :], stat[:, 0, tt, 3:4], ysb[:, 0, :], ALU.mult,
                                         ALU.mult).then_inc(S["mixed"], 1)
    ctx.close()


INPUTS = ("x mem g_mix w_in w_out ssd_conv_w ssd_conv_b ssd_dt_bias ssd_a_log ssd_d ssd_norm lru_conv_w lru_conv_b "
          "lru_lambda lru_wa lru_ba lru_wx lru_bx g_ca g_mem ca_wq ca_wkv ca_wo g_moe moe_wg moe_bg moe_we moe_be "
          "moe_w1 moe_w3 moe_w2 g_final").split()


def kernel(**inputs):
    import concourse.bacc as bacc
    from concourse.bass_utils import run_bass_kernel_spmd

    nc = bacc.Bacc("TRN2", target_bir_lowering=False, num_devices=1)
    arrays = {f"in_{n}": np.ascontiguousarray(inputs[n]) for n in INPUTS}
    arrays["in_const"] = constants()
    aps = {n[3:]: nc.dram_tensor(n, v.shape, mybir.dt.from_np(v.dtype), kind="ExternalInput").ap()
           for n, v in arrays.items()}
    out = nc.dram_tensor("out_0", inputs["x"].shape, F32, kind="ExternalOutput").ap()
    build_trunk(nc, aps, out)
    r = run_bass_kernel_spmd(nc, [arrays], core_ids=[0])
    return r.results[0]["out_0"]
```

```python
import math
from contextlib import ExitStack

import numpy as np
import concourse.bass as bass
from concourse import mybir

F32 = mybir.dt.float32
I32 = mybir.dt.int32
ALU = mybir.AluOpType
ACT = mybir.ActivationFunctionType
AX_X = mybir.AxisListType.X

P = 128
D = 1024
T = 256
NT = T // P
NK = D // P
DEPTH = 2
EPS = 1e-6
RET_W, SSD_W, LRU_W = 384, 384, 256
EARLY = 3
PARAM_LOADS = (1, 8, 12)
HEADS = 6
HD = 64
XBC = SSD_W + 2 * 2 * 128
D_IN = 4 * RET_W + SSD_W + XBC + HEADS + 2 * LRU_W
NCONV = (XBC + LRU_W) // P
CW = 4
PAD = 2
CA_HEADS = 4
GROUPS, PER_GROUP = 4, 8
NE = GROUPS * PER_GROUP
F = 512
CAP = 32
QUAD = P // CAP
OV_BLOCKS = 16
SLOTS = NE * CAP
TURN = 2 * P
RING = 6
UNIT = 4096

CONST = {}
_at = 0
for _name, _n in (("ident", P), ("rot", P), ("cos", T), ("sin", T), ("decay", HEADS * 3 * P), ("causal", NT * T),
                  ("head_mean", P), ("group_mean", P), ("before", P), ("ones", P), ("iota", F), ("part", 1),
                  ("first_slot", NE), ("pick_head", HEADS * P)):
    CONST[_name] = (_at, _at + _n)
    _at += _n
N_CONST = _at

ROWS = {}
_at = 0
for _name, _n in (("conv_w", CW * 7), ("conv_b", 7), ("lru_conv_w", CW * 2), ("lru_conv_b", 2), ("lam", 4),
                  ("ba", 4), ("bx", 4), ("ssd_norm", 3)):
    ROWS[_name] = (_at, _n)
    _at += _n
N_ROWS = _at

O_Q, O_K, O_V, O_G, O_Z, O_X = 0, 384, 768, 1152, 1536, 1920
O_DT = O_X + XBC
O_XR = O_DT + HEADS
W_IN_UNITS = ((O_X, 512), (O_X + 512, 390), (O_XR, 512), (O_Q, 512), (512, 512), (1024, 512), (O_Z, 384))
JOBS = ((0, 0, 2, P), (0, 256, 2, P), (1, 0, 2, P), (1, 256, 2, HEADS), (2, 0, 2, P), (2, 256, 2, P),
        (3, 0, 2, P), (3, 256, 2, P), (4, 0, 2, P), None, None, (5, 128, 2, P), (5, 384, 1, P),
        (6, 0, 2, P), (6, 256, 1, P))
PRE_SLOT = (0, 1, 2, 3, 0, 1, 2, 3, 0, 1, 2, 3, 4, 5, 0, 1, 2)
EXPERT_SLOT = (3, 4, 5, 0, 6, 7, 1, 2)
AROUND = len(EXPERT_SLOT)


def constants():
    c = np.zeros((P, N_CONST), np.float64)

    def put(name, a):
        lo, hi = CONST[name]
        c[:a.shape[0], lo:hi] = a

    p = np.arange(P)
    put("ident", np.eye(P))
    rot = np.zeros((P, P))
    for b in (0, HD):
        for d in range(HD // 2):
            rot[b + HD // 2 + d, b + d] = -1.0
            rot[b + d, b + HD // 2 + d] = 1.0
    put("rot", rot)
    inv = (10000.0 ** (-np.arange(HD // 2, dtype=np.float32) / np.float32(HD // 2))).astype(np.float32)
    ang = (np.arange(T, dtype=np.float32)[None, :] * inv[p % (HD // 2)][:, None]).astype(np.float32)
    put("cos", np.cos(ang.astype(np.float64)))
    put("sin", np.sin(ang.astype(np.float64)))
    band = np.arange(3 * P)[None, :] - P - p[:, None]
    put("decay", np.concatenate([HD ** -0.5 * (1.0 - 2.0 ** (-5.0 - h)) ** np.abs(band) for h in range(HEADS)], 1))
    t = np.arange(T)
    put("causal", np.concatenate([(t[None, :] >= P * j + p[:, None]).astype(float) for j in range(NT)], 1))
    put("head_mean", (p[:, None] // HD == p[None, :] // HD) / float(HD))
    put("group_mean", np.full((P, P), 1.0 / (SSD_W // 2)))
    put("before", (p[:, None] < p[None, :]).astype(float))
    put("ones", np.ones((P, P)))
    put("iota", np.tile(np.arange(F), (P, 1)))
    put("part", p[:, None])
    put("first_slot", np.tile(np.arange(NE) * CAP, (P, 1)))
    put("pick_head", np.concatenate([np.tile((np.arange(HEADS) == h)[:, None], (1, P)) for h in range(HEADS)], 1))
    return c.astype(np.float32)


SEMS = """params gain_in rows_in mix_params_in rows_turned params_cols mem_in
squared variance deviation inverse normed_act normed_vec turned turned_act turned_vec
proj proj_evac dt_raw conv tanh_conv silu xs_turned xs_tok
soft_abs soft_exp soft_ln dt_rows cum_rows dt_cols cols_sb cb cb_sb
lru_gates gate_tanh lru_coef lru_decay lru_open lru_ratio lru_root
seg_rows seg_fwd seg_arg seg_exp dt_mix cb_dt head_mat ssd_y ssd_sum z_tanh z_gate ssd_sq ssd_mean ssd_sd
rot rotated score decayed ret_done ret_copy g_tanh ret_sq ret_mean ret_sd mix_ready lru_gelu_a lru_gelu_t
mixed mixed_added kv kv_evac kv_evac_vec q_proj q_evac q_evac_vec att_score att_max att_exp att_prob att_turned att_pt att_pt_vec att_o att_oevac att_oevac_vec
att_out att_added logits logits_sb group_exp gate_exp rank_mm routed diag diag_mm bcast sel gather gather_act gather_vec
act_step vec_step ov_w ov_step
x_hidden x_tanh x_gated x_h x_hT x_hTsb x_y x_yact x_yvec x_selT x_scat x_added x_vec x_sel x_gather x_gather_act att_step route_step ov_sel ov_x ov_xT""".split()


def build_trunk(nc, a, out):
    ctx = ExitStack()
    consts_in = ctx.enter_context(nc.semaphore("consts_in"))
    next_params = [ctx.enter_context(nc.semaphore(f"next_params_{i}")) for i in range(len(PARAM_LOADS))]
    next_unit = [ctx.enter_context(nc.semaphore(f"next_unit_{u}")) for u in range(EARLY)]
    S = {n: ctx.enter_context(nc.semaphore(n)) for n in SEMS}
    full = [ctx.enter_context(nc.semaphore(f"unit_landed_{s}")) for s in range(RING)]
    xfull = [ctx.enter_context(nc.semaphore(f"expert_landed_{s}")) for s in range(AROUND)]
    last_sem = ctx.enter_context(nc.semaphore("last_of_a_layer"))
    layer_sems = range(S["params"].num, last_sem.num + 1)
    assert len(layer_sems) == len(SEMS) + RING + AROUND + 1

    def sb(name, shape, dt=F32):
        return ctx.enter_context(nc.sbuf_tensor(name, shape, dt))

    ring = sb("ring", [P, RING, UNIT])
    h = sb("h", [P, NT, D])
    xn = sb("xn", [P, NT, D])
    xnT = sb("xnT", [P, NK, T])
    K = sb("const", [P, N_CONST])
    gains = sb("gains", [P, 4, NK])
    prow = sb("prow", [N_ROWS, P])
    pcol = sb("pcol", [P, N_ROWS])
    dtp = sb("dtp", [HEADS, 2, 3])
    dskip = sb("dskip", [P, 3])
    lruw = sb("lruw", [P, 2, 2, 2, P])
    lrup = sb("lrup", [P, 4, 4])
    halfb = sb("halfb", [P, 8])
    wge = sb("wge", [P, NK, GROUPS + NE])
    bge = sb("bge", [P, GROUPS + NE])
    stat = sb("stat", [P, 4, NT, 4])
    ov_table = sb("ov_table", [P, 3 * NE])
    ov_int = sb("ov_int", [P, 2], I32)
    ov_at = sb("ov_at", [P, 4])
    slotc = sb("slotc", [P, NT, 4])
    slot_id = sb("slot_id", [P, 1])
    slot_left = sb("slot_left", [P, NT, 2])[:, :, :]
    eps = sb("eps", [P, 1])
    sqrt_junk = sb("sqrt_junk", [P, 1])
    arena = sb("arena", [P, 14848])
    ps = ctx.enter_context(nc.psum_tensor("ps", [P, 8, 512], F32))

    def C(name, lo=0, n=None):
        b, e = CONST[name]
        return K[:, b + lo:(b + lo + n) if n else e]

    ident = C("ident")

    def col(name, i):
        return pcol[:, ROWS[name][0] + i:ROWS[name][0] + i + 1]

    class Carve:
        def __init__(self):
            self.used = 0

        def __call__(self, *shape):
            n = math.prod(shape)
            lo, self.used = self.used, self.used + n
            assert self.used <= 14848, self.used
            v = arena[:, lo:lo + n]
            names = "abc"[:len(shape)]
            if len(shape) == 1:
                return v
            return v.rearrange(f"p ({' '.join(names)}) -> p {' '.join(names)}", **dict(zip(names, shape)))

    mx = Carve()
    spare = ring[:, 4:6, :].rearrange("p s n -> p (s n)")
    xc = mx(NCONV, 260)
    th = mx(7, T)
    qk = mx(6, T)
    qkr = mx(6, T)
    vtok = mx(NT, RET_W)
    gz = mx(6, T)
    gt = mx(2, T)
    MEMN = mx.used
    cbs = mx(2, 2 * T)
    lru_a = mx(4, T)
    yc = spare[:, 0:NCONV * T].rearrange("p (a b) -> p a b", b=T)
    o1 = NCONV * T
    headm = spare[:, o1:o1 + 1024].rearrange("p (a b) -> p a b", a=2)
    cbd = spare[:, o1 + 1024:o1 + 2048].rearrange("p (a b) -> p a b", a=2)
    o2 = o1 + 2048
    lru = spare[:, o2:o2 + 3072].rearrange("p (a b) -> p a b", b=T)
    o3 = o2 + 3072
    xstok = spare[:, o3:o3 + NT * SSD_W].rearrange("p (a b) -> p a b", a=NT)
    assert o3 + NT * SSD_W <= 2 * UNIT
    MEMT = mx.used
    dtr = mx(5, 2, T)
    cols = mx(8, HEADS)
    dt_diff = mx(NT, HEADS)
    oT = xn.rearrange("p a b -> p (a b)").rearrange("p (a b) -> p a b", b=T)
    xcf = xc.rearrange("p a b -> p (a b)")
    seg_f = xcf[:, 0:1024].rearrange("p (a b) -> p a b", a=2)
    seg_b = xcf[:, 1024:2048].rearrange("p (a b) -> p a b", a=2)
    seg_e = th.rearrange("p a b -> p (a b)")[:, 0:1024].rearrange("p (a b) -> p a b", a=2)

    sq = xcf[:, 0:768].rearrange("p (a b) -> p a b", b=T)
    sd = xcf[:, 768:1536].rearrange("p (a b) -> p a b", b=T)
    ssq = spare[:, o3:o3 + 768].rearrange("p (a b) -> p a b", b=T)
    ssd = spare[:, o1 + 1024:o1 + 1792].rearrange("p (a b) -> p a b", b=T)

    def means(bank):
        return ps[:, bank:bank + 2, :].rearrange("p a b -> p (a b)")[:, 0:768].rearrange("p (a b) -> p a b", b=T)

    ret_means, ssd_means = means(0), means(2)

    at = Carve()
    kT = at(NK, T)
    vm = at(NT, D)
    qT = at(NK, T)
    prob = at(CA_HEADS, NT, T)
    probT = at(CA_HEADS, NT, T)
    attT = qT
    assert at.used <= MEMT
    memT = arena[:, MEMT:MEMT + NK * T].rearrange("p (a b) -> p a b", a=NK)
    att_stat = at(3, CA_HEADS, NT)
    mem_sb = spare[:, o2:o2 + NT * D].rearrange("p (a b) -> p a b", a=NT)
    memn = arena[:, MEMN:MEMN + NT * D].rearrange("p (a b) -> p a b", a=NT)

    mo = Carve()
    tables = mo(2048)
    sel = mo(NT, P)
    rows4 = mo(4, T)
    ysb = mo(D)
    gated = mo(2, T)
    hsb = mo(2, T)
    hTs = mo(2, 2, 2 * CAP)
    selT = mo(2, T)
    diag = tables[:, 0:2 * 4 * P].rearrange("p (a q s) -> p a q s", a=NT, q=4)
    rt = tables[:, 2 * 4 * P:]
    r_used = [0]

    def small(*shape):
        n = math.prod(shape)
        v = rt[:, r_used[0]:r_used[0] + n]
        r_used[0] += n
        return v if len(shape) == 1 else v.rearrange("p (a b) -> p a b", a=shape[0])

    r_lg, r_iota = small(NT, GROUPS + NE), small(NE)
    r_gm, r_min, r_m1, r_m2 = small(NT), small(NT), small(NT), small(NT)
    r_og, r_ge, r_el = small(NT, GROUPS), small(NT, GROUPS), small(NT, NE)
    r_e1, r_e2, r_ea, r_sv = small(NT, NE), small(NT, NE), small(NT, NE), small(NT, NE)
    r_in, r_a1, r_a2, r_first = small(NT, NE), small(NT, NE), small(NT, NE), small(NT, 2)
    r_nov, r_more = small(NE), small(NE, T // CAP - 1)
    rows_t = mo(T)
    tail0 = 14848 - 2 * UNIT
    assert mo.used <= tail0
    ov_x = tables[:, 0:NK * CAP].rearrange("p (k s) -> p k s", k=NK)
    ov_f, ov_s = tables[:, 256:256 + NE], tables[:, 256 + NE:256 + NE + CAP]
    ov_sel = tables[:, 512:512 + NT * CAP].rearrange("p (t s) -> p t s", t=NT)
    stage = xnT.rearrange("p a b -> p (a b)").rearrange("p (q k s) -> p q k s", q=2, k=NK)

    x_v = a["x"].rearrange("b (tt p) d -> p (b tt) d", p=P)
    mem_v = a["mem"].rearrange("b (tt p) d -> p (b tt) d", p=P)
    out_v = out.rearrange("b (tt p) d -> p (b tt) d", p=P)


    def chained(eng, sem):
        count = [0]

        def mark(ins):
            count[0] += 1
            ins.then_inc(sem, 1)
            return count[0]

        def link(ins):
            eng.wait_ge(sem, mark(ins))

        return mark, link

    def norm_squares(act, n, src, dst, tile_ready=None):
        for tt in range(NT):
            if tile_ready is not None:
                act.wait_ge(tile_ready, 2 * tt + 2)
            act.activation(dst[:, tt, :], src[:, tt, :], ACT.Square,
                           accum_out=stat[:, n, tt, 0:1]).then_inc(S["squared"], 1)

    def turned_chunk(k, bank0, banks):
        return ps[:, bank0 + k // 2 % banks, (k % 2) * T:(k % 2 + 1) * T]

    def norm_act(act, n, src, dst):
        act.wait_ge(S["variance"], n + 1)
        act.activation(stat[:, n, :, 2], stat[:, n, :, 1], ACT.Sqrt).then_inc(S["deviation"], 1)
        act.wait_ge(S["inverse"], n + 1)
        act.activation(dst[:, 0, :], src[:, 0, :], ACT.Copy, scale=stat[:, n, 0, 3:4]).then_inc(S["normed_act"], 1)

    def turned_act(act, n, dstT, bank0, banks=4, chunks=(0, 1, 4, 5)):
        for k in chunks:
            act.wait_ge(S["turned"], 4 * n + k // 2 + 1)
            act.activation(dstT[:, k, :], turned_chunk(k, bank0, banks), ACT.Copy,
                           scale=gains[:, n, k:k + 1]).then_inc(S["turned_act"], 1)

    def norm_scale_vec(vec, n):
        vec.wait_ge(S["squared"], 2 * (n + 1))
        vec.tensor_scalar(stat[:, n, :, 1], stat[:, n, :, 0], 1.0 / D, EPS, ALU.mult, ALU.add).then_inc(S["variance"], 1)
        vec.wait_ge(S["deviation"], n + 1)
        vec.reciprocal(stat[:, n, :, 3], stat[:, n, :, 2]).then_inc(S["inverse"], 1)
        vec.wait_ge(S["inverse"], n + 1)

    def norm_rows_vec(vec, n, src, dst):
        vec.tensor_scalar(dst[:, 1, :], src[:, 1, :], stat[:, n, 1, 3:4], None, ALU.mult).then_inc(S["normed_vec"], 1)

    def norm_vec(vec, n, src, dst):
        norm_scale_vec(vec, n)
        norm_rows_vec(vec, n, src, dst)

    def turned_vec(vec, n, dstT, bank0, banks=4, chunks=(2, 3, 6, 7)):
        for k in chunks:
            vec.wait_ge(S["turned"], 4 * n + k // 2 + 1)
            vec.tensor_scalar(dstT[:, k, :], turned_chunk(k, bank0, banks), gains[:, n, k:k + 1], None,
                              ALU.mult).then_inc(S["turned_vec"], 1)

    def norm_pe(pe, n, dst, bank0, banks=4, chunks=range(NK)):
        pe.wait_ge(S["normed_act"], n + 1)
        pe.wait_ge(S["normed_vec"], n + 1)
        for k in chunks:
            for tt in range(NT):
                ins = pe.transpose(turned_chunk(k, bank0, banks)[:, tt * P:(tt + 1) * P], dst[:, tt, k::NK], ident)
            if k % 2:
                ins.then_inc(S["turned"], 1)

    def normed_T_ready(pe, n):
        pe.wait_ge(S["turned_act"], 4 * (n + 1))
        pe.wait_ge(S["turned_vec"], 4 * (n + 1))

    w_in_v = a["w_in"].rearrange("l (p k) n -> l p k n", k=NK)

    def mixer_param_loads(layer):
        def of(name):
            return a[name][bass.ds(layer, 1)]

        def rows(name, src):
            r, n = ROWS[name]
            return prow[r:r + n, :], src

        loads = [(gains[:, 0, :], of("g_mix").rearrange("l (p k) -> p (l k)", k=NK)),
                 rows("conv_w", of("ssd_conv_w").rearrange("l i (c p) -> (l i c) p", p=P)),
                 rows("conv_b", of("ssd_conv_b").rearrange("l (c p) -> (l c) p", p=P)),
                 rows("lru_conv_w", of("lru_conv_w").rearrange("l i (c p) -> (l i c) p", p=P)),
                 rows("lru_conv_b", of("lru_conv_b").rearrange("l (c p) -> (l c) p", p=P)),
                 rows("lam", of("lru_lambda").rearrange("l r (c p) -> (l r c) p", p=P)),
                 rows("ba", of("lru_ba").rearrange("l r (c p) -> (l r c) p", p=P)),
                 rows("bx", of("lru_bx").rearrange("l r (c p) -> (l r c) p", p=P)),
                 rows("ssd_norm", of("ssd_norm").rearrange("l (c p) -> (l c) p", p=P)),
                 (dtp[:, :, 0], of("ssd_dt_bias").rearrange("l r h -> h (l r)")),
                 (dtp[:, :, 1], of("ssd_a_log").rearrange("l r h -> h (l r)"))]
        for half in range(2):
            src = of("ssd_d").rearrange("l (c two) -> (l two) c", two=2)[half:half + 1, :]
            loads.append((dskip[half * HD:(half + 1) * HD, :], src.to_broadcast([HD, 3])))
            for gate, name in enumerate(("lru_wa", "lru_wx")):
                for r in range(2):
                    src = of(name)[:, r].rearrange("l (c two) i j -> (l two) i c j", two=2)[half]
                    loads.append((lruw[half * HD:(half + 1) * HD, r, gate, :, half * HD:(half + 1) * HD], src))
        assert len(loads) == sum(PARAM_LOADS)
        return loads

    def issue_params(sp, layer, part):
        lo = sum(PARAM_LOADS[0:part])
        with nc.allow_non_contiguous_dma(reason="a few bytes"):
            for dst, src in mixer_param_loads(layer)[lo:lo + PARAM_LOADS[part]]:
                sp.dma_start(dst, src).then_inc(next_params[part], 16)

    def w_in_load(sp, layer, u, sem):
        c0, n = W_IN_UNITS[u]
        dst = ring[:, PRE_SLOT[u], :].rearrange("p (k n) -> p k n", k=NK)[:, :, 0:n]
        sp.dma_start(dst, w_in_v[bass.ds(layer, 1), :, :, c0:c0 + n].rearrange("l p k n -> p (l k) n")
                     ).then_inc(sem, 16)

    def sqrt_table(act):
        act.activation(sqrt_junk[:, :], eps[:, :], ACT.Sqrt)

    with nc.Block() as block:
        @block.sync
        def _(sp):
            sp.dma_start(h[:, :, :], x_v).then_inc(consts_in, 16)
            sp.dma_start(ident, a["const"][:, 0:P]).then_inc(consts_in, 16)
            sp.wait_ge(consts_in, 32)

        @block.gpsimd
        def _(pool):
            pool.memset(eps[:, :], EPS)
            pool.memset(lruw[:, :, :, :, :], 0.0)

    wkv_v = a["ca_wkv"].rearrange("l (p k) n -> l p k n", k=NK)

    def kv_load(sp, layer, u):
        s, c = PRE_SLOT[u], 512 * (u - 9)
        sp.dma_start(ring[:, s, :].rearrange("p (k n) -> p k n", k=NK),
                     wkv_v[bass.ds(layer, 1), :, :, c:c + 512].rearrange("l p k n -> p (l k) n")).then_inc(full[s], 16)

    def one_layer(layer):
        def of(name):
            return a[name][bass.ds(layer, 1)]

        w_out_v = a["w_out"].rearrange("l (c p) n -> l p c n", p=P)
        with nc.Block() as block:
            @block.sync
            def _(sp):
                def pass_params(part, there):
                    sp.wait_ge(next_params[part], sp.snap(16 * PARAM_LOADS[part] * (layer + 1)))
                    sp.sem_inc(S[there], 1)

                def pass_unit(u):
                    sp.wait_ge(next_unit[u], sp.snap(16 * layer + 16))
                    sp.sem_inc(full[PRE_SLOT[u]], 16)

                with sp.If(layer < 1):
                    issue_params(sp, 0, 0)
                    w_in_load(sp, 0, 0, next_unit[0])
                    issue_params(sp, 0, 1)
                    w_in_load(sp, 0, 1, next_unit[1])
                with sp.Else():
                    pass
                pass_params(0, "gain_in")
                pass_unit(0)
                pass_params(1, "rows_in")
                with sp.If(layer < 1):
                    sp.dma_start(K[:, P:], a["const"][:, P:]).then_inc(consts_in, 16)
                    w_in_load(sp, 0, 2, next_unit[2])
                    issue_params(sp, 0, 2)
                with sp.Else():
                    pass
                pass_unit(1)
                w_in_load(sp, layer, EARLY, full[PRE_SLOT[EARLY]])
                pass_unit(2)
                pass_params(2, "mix_params_in")

                def param(dst, src):
                    sp.dma_start(dst, src).then_inc(S["params"], 16)

                with nc.allow_non_contiguous_dma(reason="a few bytes"):
                    for n, g in ((1, "g_mem"), (2, "g_ca"), (3, "g_moe")):
                        param(gains[:, n, :], of(g).rearrange("l (p k) -> p (l k)", k=NK))
                    param(wge[:, :, 0:GROUPS], of("moe_wg").rearrange("l (p k) n -> p (l k) n", k=NK))
                    param(wge[:, :, GROUPS:], of("moe_we").rearrange("l (p k) n -> p (l k) n", k=NK))
                    param(bge[:, 0:GROUPS], of("moe_bg").to_broadcast([P, GROUPS]))
                    param(bge[:, GROUPS:], of("moe_be").to_broadcast([P, NE]))
                free = {4: (S["proj"], 2), 5: (S["proj"], 4), 6: (S["proj"], 6), 7: (S["proj"], 8), 8: (S["proj"], 11)}
                for u in range(EARLY + 1, 9):
                    sp.wait_ge(*free[u])
                    s = PRE_SLOT[u]
                    if u < 7:
                        w_in_load(sp, layer, u, full[s])
                    else:
                        c = 4 * (u - 7)
                        dst = ring[:, s, :].rearrange("p (c n) -> p c n", c=4)
                        src = w_out_v[bass.ds(layer, 1), :, c:c + 4, :].rearrange("l p c n -> p (l c) n")
                        sp.dma_start(dst, src).then_inc(full[s], 16)
                    if u == 7:
                        sp.wait_ge(S["mix_ready"], 1)
                        sp.dma_start(mem_sb, mem_v).then_inc(S["mem_in"], 16)
                sp.wait_ge(S["params"], 16 * 7)
                for u, after in ((9, 13), (10, 15)):
                    sp.wait_ge(S["proj"], after)
                    kv_load(sp, layer, u)
                attention_loads(sp, layer)

            @block.gpsimd
            def _(pool):
                pool.wait_ge(consts_in, 48)
                for hh in range(HEADS):
                    b = hh % 2
                    pool.wait_ge(S["cols_sb"], 1)
                    if hh >= 2:
                        pool.wait_ge(S["head_mat"], hh - 1)
                    for j in range(NT):
                        pool.tensor_scalar(cbd[:, b, j * T:(j + 1) * T], C("causal", j * T, T),
                                           dt_diff[:, j, hh:hh + 1], cols[:, 6 + j, hh:hh + 1],
                                           ALU.mult, ALU.add).then_inc(S["dt_mix"], 1)
                    pool.wait_ge(S["dt_mix"], 2 * hh + 2)
                    pool.wait_ge(S["cb_sb"], hh // 3 + 1)
                    pool.tensor_tensor(cbd[:, b, :], cbd[:, b, :], cbs[:, hh // 3, :], ALU.mult).then_inc(S["cb_dt"], 1)
            @block.scalar
            def _(act):
                sqrt_table(act)
                norm_squares(act, 0, h, xn)
                norm_act(act, 0, h, xn)
                act.wait_ge(S["gain_in"], 1)
                turned_act(act, 0, xnT, 0)

                def evac(n, dst):
                    act.wait_ge(S["proj"], n + 1)
                    blocks = 1 if len(dst.shape) == 2 else dst.shape[1]
                    src = ps[:, 4 + n % 2, 0:math.prod(dst.shape[1:])]
                    if blocks > 1:
                        src = src.rearrange("p (a b) -> p a b", a=blocks)
                    act.activation(dst, src, ACT.Copy).then_inc(S["proj_evac"], 1)

                def tanh_conv(b):
                    act.wait_ge(S["conv"], b + 1)
                    act.activation(th[:, b, :], yc[:, b, :], ACT.Tanh, scale=0.5).then_inc(S["tanh_conv"], 1)

                for n in range(4):
                    if n == 3:
                        act.wait_ge(S["proj"], 4)
                        act.activation(xc[:, 6, PAD:PAD + T], ps[:, 5, 0:T], ACT.Copy).then_inc(S["proj_evac"], 1)
                    else:
                        evac(n, xc[:, 2 * n:2 * n + 2, PAD:PAD + T])
                    if n == 0:
                        act.wait_ge(S["soft_abs"], 1)
                        act.activation(lrup[:, :, 1], lrup[:, :, 0], ACT.Exp, scale=-1.0).then_inc(S["soft_exp"], 1)
                        act.wait_ge(S["soft_exp"], 1)
                        act.activation(lrup[:, :, 2], lrup[:, :, 1], ACT.Ln, bias=1.0).then_inc(S["soft_ln"], 1)
                    else:
                        tanh_conv(2 * n - 2)
                        tanh_conv(2 * n - 1)
                evac(4, xc[:, 7:9, PAD:PAD + T])
                tanh_conv(6)
                act.wait_ge(S["mix_params_in"], 1)
                act.activation(dtp[:, :, 2], dtp[:, :, 1], ACT.Exp).then_inc(S["act_step"], 1)
                act.wait_ge(S["soft_abs"], 2)
                act.activation(dtr[0:HEADS, 2], dtr[0:HEADS, 1], ACT.Exp, scale=-1.0).then_inc(S["soft_exp"], 1)
                act.wait_ge(S["soft_exp"], 2)
                act.activation(dtr[0:HEADS, 3], dtr[0:HEADS, 2], ACT.Ln, bias=1.0).then_inc(S["soft_ln"], 1)
                for tt in range(NT):
                    act.wait_ge(S["xs_turned"], tt + 1)
                    act.activation(xstok[:, tt, :], ps[:, tt, 0:SSD_W], ACT.Copy).then_inc(S["xs_tok"], 1)
                evac(5, gt)

                def gate_tanh(n):
                    act.wait_ge(S["lru_gates"], n + 1)
                    act.wait_ge(S["lru_coef"], 1)
                    for gate in range(2):
                        act.activation(lru[:, 4 * gate + n, :], ps[:, n % 2, gate * T:(gate + 1) * T], ACT.Tanh,
                                       scale=0.5, bias=halfb[:, 4 * gate + n:4 * gate + n + 1]
                                       ).then_inc(S["gate_tanh"], 1)

                def seg_fwd(hh):
                    b = hh % 2
                    act.wait_ge(S["seg_rows"], hh + 1)
                    act.wait_ge(S["cols_sb"], 1)
                    act.wait_ge(S["conv"], NCONV)
                    if hh >= 2:
                        act.wait_ge(S["seg_arg"], hh - 1)
                    for j in range(NT):
                        act.activation(seg_f[:, b, j * T:(j + 1) * T], ps[:, 6 + b, 0:T], ACT.Relu, scale=-1.0,
                                       bias=cols[:, j, hh:hh + 1]).then_inc(S["seg_fwd"], 1)

                def seg_exp(hh):
                    b = hh % 2
                    act.wait_ge(S["seg_arg"], hh + 1)
                    act.wait_ge(S["silu"], 7)
                    if hh >= 2:
                        act.wait_ge(S["head_mat"], hh - 1)
                    act.activation(seg_e[:, b, :], seg_b[:, b, :], ACT.Exp).then_inc(S["seg_exp"], 1)

                gate_tanh(0)
                gate_tanh(1)
                seg_fwd(0)
                seg_fwd(1)
                seg_exp(0)
                seg_exp(1)
                evac(6, qk[:, 0:2, :])
                gate_tanh(2)
                gate_tanh(3)
                seg_fwd(2)
                for n in range(4):
                    act.wait_ge(S["gate_tanh"], 2 * n + 2)
                    act.activation(lru_a[:, n, :], lru[:, n, :], ACT.Exp, scale=lrup[:, n, 3:4],
                                   bias=lrup[:, n, 3:4]).then_inc(S["lru_decay"], 1)
                seg_exp(2)
                for n in range(4):
                    act.wait_ge(S["lru_decay"], n + 1)
                    act.activation(lru[:, n, :], lru[:, n, :], ACT.Tanh, scale=lrup[:, n, 0:1],
                                   bias=lrup[:, n, 0:1]).then_inc(S["lru_open"], 1)
                evac(7, qk[:, 2:4, :])
                seg_fwd(3)
                seg_exp(3)
                evac(8, qk[:, 4:6, :])
                seg_fwd(4)
                seg_exp(4)
                evac(9, vtok[:, 0, :])
                seg_fwd(5)
                seg_exp(5)
                act.wait_ge(S["lru_ratio"], 1)
                act.activation(lru[:, 8:12, :], lru[:, 8:12, :], ACT.Sqrt, scale=0.5).then_inc(S["lru_root"], 1)
                act.wait_ge(S["lru_gelu_a"], 1)
                act.activation(lru[:, 0:2, :], lru[:, 0:2, :], ACT.Tanh, scale=math.sqrt(2.0 / math.pi)
                               ).then_inc(S["lru_gelu_t"], 1)
                evac(10, vtok[:, 1, :])
                evac(11, gz[:, 0:2, :])
                evac(12, gz[:, 2, :])
                act.wait_ge(S["proj_evac"], 13)
                act.activation(th[:, 4:7, :], gz[:, 0:3, :], ACT.Tanh, scale=0.5).then_inc(S["g_tanh"], 1)
                act.wait_ge(S["mem_in"], 16)
                act.wait_ge(S["cb_dt"], HEADS)
                act.wait_ge(S["mix_ready"], 1)
                norm_squares(act, 1, mem_sb, memn)
                norm_act(act, 1, mem_sb, memn)
                evac(13, gz[:, 3:5, :])
                act.wait_ge(S["params"], 16 * 7)
                turned_act(act, 1, memT, 0, 2, (0, 1))

                def ret_copy(c):
                    act.wait_ge(S["ret_done"], 2 * c + 2)
                    act.activation(oT[:, c, :], ps[:, 2 + c % 2, 0:T], ACT.Copy).then_inc(S["ret_copy"], 1)

                for c in range(3):
                    ret_copy(c)
                act.wait_ge(S["ret_copy"], 3)
                act.activation(sq, oT[:, 0:3, :], ACT.Square).then_inc(S["ret_sq"], 1)
                evac(14, gz[:, 5, :])
                turned_act(act, 1, memT, 0, 2, (4, 5))
                act.wait_ge(S["proj_evac"], 15)
                act.wait_ge(S["head_mat"], HEADS)
                act.activation(th[:, 0:3, :], gz[:, 3:6, :], ACT.Tanh, scale=0.5).then_inc(S["z_tanh"], 1)
                act.wait_ge(S["ret_mean"], 1)
                act.activation(sd, ret_means, ACT.Sqrt, bias=eps[:, 0:1]).then_inc(S["ret_sd"], 1)
                act.wait_ge(S["ssd_sum"], 1)
                act.activation(ssq, oT[:, 3:6, :], ACT.Square).then_inc(S["ssd_sq"], 1)
                act.wait_ge(S["ssd_mean"], 1)
                act.activation(ssd, ssd_means, ACT.Sqrt, bias=eps[:, 0:1]).then_inc(S["ssd_sd"], 1)
                attention_act(act)

            @block.vector
            def _(vec):
                mark, link = chained(vec, S["vec_step"])
                mark(vec.memset(xc[:, :, 0:PAD], 0.0))
                link(vec.memset(xc[:, :, PAD + T:260], 0.0))
                norm_vec(vec, 0, h, xn)
                vec.wait_ge(S["gain_in"], 1)
                turned_vec(vec, 0, xnT, 0)
                vec.wait_ge(S["rows_turned"], 1)
                vec.tensor_copy(pcol[:, :], ps[:, 6, 0:N_ROWS]).then_inc(S["params_cols"], 1)
                vec.wait_ge(S["params_cols"], 1)
                lam = pcol[:, ROWS["lam"][0]:ROWS["lam"][0] + 4]
                vec.scalar_tensor_tensor(lrup[:, :, 0], lam, -1.0, lam, ALU.mult, ALU.max).then_inc(S["soft_abs"], 1)
                b0 = ROWS["ba"][0]
                mark(vec.tensor_scalar(halfb[:, :], pcol[:, b0:b0 + 8], 0.5, None, ALU.mult))
                vec.wait_ge(S["soft_ln"], 1)
                link(vec.tensor_scalar(lrup[:, :, 1], lam, -1.0, 0.0, ALU.mult, ALU.max))
                link(vec.tensor_tensor(lrup[:, :, 2], lrup[:, :, 1], lrup[:, :, 2], ALU.add))
                mark(vec.tensor_scalar(lrup[:, :, 0], lrup[:, :, 2], 4.0, None, ALU.mult))
                vec.tensor_scalar(lrup[:, :, 3], lrup[:, :, 2], -4.0, None, ALU.mult).then_inc(S["lru_coef"], 1)

                def conv(b):
                    w, bias = ("conv_w", col("conv_b", b)) if b < 7 else ("lru_conv_w", col("lru_conv_b", b - 7))
                    nb, i = (7, b) if b < 7 else (2, b - 7)
                    vec.wait_ge(S["proj_evac"], (b // 2 + 1) if b < 7 else 5)
                    link(vec.tensor_scalar(yc[:, b, :], xc[:, b, 0:T], col(w, i), bias, ALU.mult, ALU.add))
                    for tap in range(1, CW):
                        ins = vec.scalar_tensor_tensor(yc[:, b, :], xc[:, b, tap:tap + T], col(w, tap * nb + i),
                                                       yc[:, b, :], ALU.mult, ALU.add)
                        if tap < CW - 1:
                            link(ins)
                    ins.then_inc(S["conv"], 1)

                def silu(b):
                    vec.wait_ge(S["tanh_conv"], b + 1)
                    vec.scalar_tensor_tensor(yc[:, b, :], th[:, b, :], 1.0, yc[:, b, :], ALU.add, ALU.mult
                                             ).then_inc(S["silu"], 1)

                for b in range(7):
                    conv(b)
                    if b % 2 and b >= 3:
                        silu(b - 3)
                        silu(b - 2)
                vec.wait_ge(S["proj"], 4)
                vec.wait_ge(S["mix_params_in"], 1)
                for r in range(2):
                    vec.tensor_scalar(dtr[0:HEADS, 0, r, :], ps[0:HEADS, 5, T:2 * T], dtp[:, r, 0:1], None,
                                      ALU.add).then_inc(S["dt_raw"], 1)
                vec.wait_ge(S["dt_raw"], 2)
                vec.scalar_tensor_tensor(dtr[0:HEADS, 1], dtr[0:HEADS, 0], -1.0, dtr[0:HEADS, 0], ALU.mult, ALU.max
                                         ).then_inc(S["soft_abs"], 1)
                silu(4)
                silu(5)
                conv(7)
                conv(8)
                silu(6)
                vec.wait_ge(S["soft_ln"], 2)
                vec.wait_ge(S["act_step"], 1)
                link(vec.scalar_tensor_tensor(dtr[0:HEADS, 4], dtr[0:HEADS, 0], 0.0, dtr[0:HEADS, 3], ALU.max,
                                              ALU.add))
                for r in range(2):
                    n = mark(vec.tensor_scalar(dtr[0:HEADS, 1, r, :], dtr[0:HEADS, 4, r, :], dtp[:, r, 2:3], -1.0,
                                               ALU.mult, ALU.mult))
                vec.tensor_scalar(dtr[0:HEADS, 3], dtr[0:HEADS, 4], 0.0625, None, ALU.mult).then_inc(S["dt_rows"], 1)
                vec.wait_ge(S["vec_step"], n)
                vec.wait_ge(consts_in, 48)
                one = C("ones", 0, 1)[0:HEADS].to_broadcast([HEADS, T])
                vec.tensor_tensor_scan(dtr[0:HEADS, 2, 0, :], one, dtr[0:HEADS, 1, 0, :], 0.0, ALU.mult, ALU.add
                                       ).then_inc(S["cum_rows"], 1)
                vec.tensor_tensor_scan(dtr[0:HEADS, 2, 1, ::-1], one, dtr[0:HEADS, 1, 1, ::-1], 0.0,
                                       ALU.mult, ALU.add).then_inc(S["cum_rows"], 1)
                for g in range(2):
                    vec.wait_ge(S["cb"], g + 1)
                    vec.tensor_copy(cbs[:, g, :], ps[:, 2 + g, :]).then_inc(S["cb_sb"], 1)
                vec.wait_ge(S["dt_cols"], 1)
                link(vec.tensor_copy(cols[:, :, :], ps[:, 6, 0:8 * HEADS].rearrange("p (a b) -> p a b", a=8)))
                vec.tensor_tensor(dt_diff, cols[:, 4:6, :], cols[:, 6:8, :], ALU.subtract).then_inc(S["cols_sb"], 1)

                def seg(hh):
                    b = hh % 2
                    vec.wait_ge(S["seg_fwd"], 2 * hh + 2)
                    if hh >= 2:
                        vec.wait_ge(S["seg_exp"], hh - 1)
                    for j in range(NT):
                        n = mark(vec.tensor_scalar(seg_b[:, b, j * T:(j + 1) * T], ps[:, 6 + b, T:2 * T],
                                                   cols[:, 2 + j, hh:hh + 1], 0.0, ALU.subtract, ALU.min))
                    vec.wait_ge(S["vec_step"], n)
                    vec.tensor_tensor(seg_b[:, b, :], seg_b[:, b, :], seg_f[:, b, :], ALU.subtract
                                      ).then_inc(S["seg_arg"], 1)

                def head_mat(hh):
                    b = hh % 2
                    vec.wait_ge(S["seg_exp"], hh + 1)
                    vec.wait_ge(S["cb_dt"], hh + 1)
                    if hh >= 2:
                        vec.wait_ge(S["ssd_y"], hh - 1)
                    vec.tensor_tensor(headm[:, b, :], seg_e[:, b, :], cbd[:, b, :], ALU.mult).then_inc(S["head_mat"], 1)

                def ratio():
                    vec.wait_ge(S["lru_open"], 4)
                    link(vec.tensor_scalar(lru[:, 8:12, :], lru[:, 0:4, :], 1.0, None, ALU.add))
                    link(vec.reciprocal(lru[:, 8:12, :], lru[:, 8:12, :]))
                    vec.tensor_tensor(lru[:, 8:12, :], lru[:, 8:12, :], lru[:, 0:4, :], ALU.mult
                                      ).then_inc(S["lru_ratio"], 1)
                    vec.wait_ge(S["lru_ratio"], 1)

                def gelu_and_inputs():
                    link(vec.tensor_tensor(lru[:, 0:2, :], gt[:, :, :], gt[:, :, :], ALU.mult))
                    link(vec.tensor_scalar(lru[:, 0:2, :], lru[:, 0:2, :], 0.044715, 1.0, ALU.mult, ALU.add))
                    vec.tensor_tensor(lru[:, 0:2, :], lru[:, 0:2, :], gt[:, :, :], ALU.mult
                                      ).then_inc(S["lru_gelu_a"], 1)
                    for r in range(2):
                        n = mark(vec.scalar_tensor_tensor(lru[:, 4 + 2 * r:6 + 2 * r, :],
                                                          lru[:, 4 + 2 * r:6 + 2 * r, :], 1.0, yc[:, 7:9, :],
                                                          ALU.add, ALU.mult))
                    return n

                def recurrences(n):
                    vec.wait_ge(S["vec_step"], n)
                    vec.wait_ge(S["lru_root"], 1)
                    link(vec.tensor_tensor(lru[:, 4:8, :], lru[:, 4:8, :], lru[:, 8:12, :], ALU.mult))
                    for c in range(2):
                        mark(vec.tensor_tensor_scan(lru[:, 8 + c, :], lru_a[:, c, :], lru[:, 4 + c, :], 0.0,
                                                    ALU.mult, ALU.add))
                        n = mark(vec.tensor_tensor_scan(lru[:, 10 + c, ::-1], lru_a[:, 2 + c, ::-1],
                                                        lru[:, 6 + c, ::-1], 0.0, ALU.mult, ALU.add))
                    vec.wait_ge(S["lru_gelu_t"], 1)
                    mark(vec.scalar_tensor_tensor(lru[:, 0:2, :], lru[:, 0:2, :], 1.0, gt[:, :, :], ALU.add, ALU.mult))
                    vec.wait_ge(S["vec_step"], n)
                    link(vec.tensor_tensor(lru[:, 8:10, :], lru[:, 8:10, :], lru[:, 10:12, :], ALU.add))
                    vec.scalar_tensor_tensor(oT[:, 6:8, :], lru[:, 8:10, :], 0.5, lru[:, 0:2, :], ALU.mult, ALU.mult
                                             ).then_inc(S["mix_ready"], 1)

                def ssd_sum(c):
                    vec.wait_ge(S["ssd_y"], 2 * c + 2)
                    link(vec.scalar_tensor_tensor(oT[:, 3 + c, :], yc[:, c, :], dskip[:, c:c + 1],
                                                  ps[:, c % 2, 0:T], ALU.mult, ALU.add))
                    vec.sem_inc(S["z_gate"], 1)

                def rotate(c):
                    x, y = qk[:, 2 * c:2 * c + 2, :], qkr[:, 2 * c:2 * c + 2, :]
                    vec.wait_ge(S["rot"], c + 1)
                    cs = C("cos").unsqueeze(1).to_broadcast([P, 2, T])
                    sn = C("sin").unsqueeze(1).to_broadcast([P, 2, T])
                    mark(vec.tensor_tensor(x, x, cs, ALU.mult))
                    link(vec.tensor_tensor(y, ps[:, 2 + c % 2, :].rearrange("p (a b) -> p a b", a=2), sn, ALU.mult))
                    vec.tensor_tensor(y, y, x, ALU.add).then_inc(S["rotated"], 1)

                def decayed(hh):
                    b = hh % 2
                    vec.wait_ge(S["score"], hh + 1)
                    vec.wait_ge(S["ssd_y"], HEADS) if hh < 2 else vec.wait_ge(S["ret_done"], hh - 1)
                    dec = C("decay", hh * 3 * P, 3 * P)
                    for j in range(NT):
                        vec.tensor_tensor(headm[:, b, j * T:(j + 1) * T], ps[:, 6 + b, j * T:(j + 1) * T],
                                          dec[:, (1 - j) * P:(1 - j) * P + T], ALU.mult).then_inc(S["decayed"], 1)

                mark(vec.tensor_scalar(dskip[:, :], dskip[:, :], 0.25, None, ALU.mult))
                seg(0)
                seg(1)
                head_mat(0)
                head_mat(1)
                seg(2)
                head_mat(2)
                seg(3)
                ratio()
                head_mat(3)
                rotate(0)
                seg(4)
                n = gelu_and_inputs()
                ssd_sum(0)
                head_mat(4)
                rotate(1)
                seg(5)
                ssd_sum(1)
                head_mat(5)
                rotate(2)
                recurrences(n)
                ssd_sum(2)
                for hh in range(HEADS):
                    decayed(hh)
                    if hh == 3:
                        norm_vec(vec, 1, mem_sb, memn)
                        vec.wait_ge(S["params"], 16 * 7)
                        turned_vec(vec, 1, memT, 0, 2, (2, 3))
                vec.wait_ge(S["g_tanh"], 1)
                link(vec.scalar_tensor_tensor(gz[:, 0:3, :], th[:, 4:7, :], 1.0, gz[:, 0:3, :], ALU.add, ALU.mult))
                turned_vec(vec, 1, memT, 0, 2, (6, 7))
                vec.wait_ge(S["z_tanh"], 1)
                link(vec.scalar_tensor_tensor(gz[:, 3:6, :], th[:, 0:3, :], 1.0, gz[:, 3:6, :], ALU.add, ALU.mult))
                vec.tensor_tensor(oT[:, 3:6, :], oT[:, 3:6, :], gz[:, 3:6, :], ALU.mult).then_inc(S["ssd_sum"], 1)
                vec.wait_ge(S["ret_sd"], 1)
                link(vec.reciprocal(sd, sd))
                link(vec.scalar_tensor_tensor(sd, sd, 0.5, gz[:, 0:3, :], ALU.mult, ALU.mult))
                vec.tensor_tensor(oT[:, 0:3, :], oT[:, 0:3, :], sd, ALU.mult).then_inc(S["mix_ready"], 1)
                vec.wait_ge(S["ssd_sd"], 1)
                link(vec.reciprocal(ssd, ssd))
                for c in range(3):
                    vec.scalar_tensor_tensor(oT[:, 3 + c, :], oT[:, 3 + c, :], col("ssd_norm", c), ssd[:, c, :],
                                             ALU.mult, ALU.mult).then_inc(S["mix_ready"], 1)
                for n in range(4):
                    vec.wait_ge(S["mixed"], n + 1)
                    tt, half = n // 2, n % 2
                    hs = h[:, tt, half * 512:(half + 1) * 512]
                    vec.tensor_tensor(hs, hs, ps[:, 4 + n, :], ALU.add).then_inc(S["mixed_added"], 1)
                attention_vec(vec)

            @block.tensor
            def _(pe):
                norm_pe(pe, 0, xn, 0)
                normed_T_ready(pe, 0)
                landed = set()

                def unit(u):
                    if u not in landed:
                        landed.add(u)
                        pe.wait_ge(full[PRE_SLOT[u]], 16 * sum(PRE_SLOT[v] == PRE_SLOT[u] for v in range(u + 1)))
                    return ring[:, PRE_SLOT[u], :].rearrange("p (k n) -> p k n", k=NK)

                def bank_free(n):
                    if n >= 2:
                        pe.wait_ge(S["proj_evac"], n - 1)
                    if n == 5:
                        pe.wait_ge(S["dt_raw"], 2)

                def job(n):
                    u, c0, blocks, rows = JOBS[n]
                    w = unit(u)
                    bank_free(n)
                    for b in range(blocks):
                        m = rows if b == blocks - 1 else P
                        for k in range(NK):
                            ins = pe.matmul(ps[0:m, 4 + n % 2, b * T:(b + 1) * T], w[:, k, c0 + b * P:c0 + b * P + m],
                                            xnT[:, k, :], start=(k == 0), stop=(k == NK - 1))
                    ins.then_inc(S["proj"], 1)

                def job_v(tt):
                    n = 9 + tt
                    bank_free(n)
                    for u, c0, m, o in ((4, 256, 256, 0), (5, 0, 128, 256)):
                        w = unit(u)
                        for k in range(NK):
                            ins = pe.matmul(ps[:, 4 + n % 2, o:o + m], xnT[:, k, tt * P:(tt + 1) * P],
                                            w[:, k, c0:c0 + m], start=(k == 0), stop=(k == NK - 1))
                    ins.then_inc(S["proj"], 1)

                def seg_rows(hh):
                    if hh >= 2:
                        pe.wait_ge(S["seg_arg"], hh - 1)
                    elif hh == 0:
                        pe.wait_ge(S["cols_sb"], 1)
                    pe.matmul(ps[:, 6 + hh % 2, :], C("pick_head", hh * P, P)[0:HEADS],
                              dtr[0:HEADS, 2].rearrange("p a b -> p (a b)"), start=True, stop=True
                              ).then_inc(S["seg_rows"], 1)

                def ssd_y(hh):
                    c, lo = hh // 2, (hh % 2) * HD
                    pe.wait_ge(S["head_mat"], hh + 1)
                    if hh in (0, 2):
                        pe.wait_ge(S["gate_tanh"], 8)
                    if hh == 4:
                        pe.wait_ge(S["z_gate"], 1)
                    for j in range(NT):
                        ins = pe.matmul(ps[lo:lo + HD, c % 2, 0:T], xstok[:, j, hh * HD:(hh + 1) * HD],
                                        headm[:, hh % 2, j * T:(j + 1) * T], start=(j == 0), stop=(j == NT - 1))
                    ins.then_inc(S["ssd_y"], 1)

                def rot(c):
                    pe.wait_ge(S["proj_evac"], 7 + c)
                    if c == 0:
                        pe.wait_ge(S["cb_sb"], 2)
                    if c == 2:
                        pe.wait_ge(S["rotated"], 1)
                    for b in range(2):
                        ins = pe.matmul(ps[:, 2 + c % 2, b * T:(b + 1) * T], C("rot"), qk[:, 2 * c + b, :],
                                        start=True, stop=True)
                    ins.then_inc(S["rot"], 1)

                def lru_gates(n):
                    r, c = n // 2, n % 2
                    pe.wait_ge(S["xs_tok"], 2) if n < 2 else pe.wait_ge(S["gate_tanh"], 2 * (n - 1))
                    for gate in range(2):
                        ins = pe.matmul(ps[:, n % 2, gate * T:(gate + 1) * T], lruw[:, r, gate, c, :],
                                        yc[:, 7 + c, :], start=True, stop=True)
                    ins.then_inc(S["lru_gates"], 1)

                def score(hh):
                    c, lo = hh // 2, (hh % 2) * HD
                    if hh == 0:
                        pe.wait_ge(S["rotated"], 3)
                        pe.wait_ge(S["seg_arg"], HEADS)
                    if hh >= 2:
                        pe.wait_ge(S["decayed"], 2 * (hh - 1))
                    for j in range(NT):
                        ins = pe.matmul(ps[:, 6 + hh % 2, j * T:(j + 1) * T], qkr[lo:lo + HD, 3 + c, j * P:(j + 1) * P],
                                        qkr[lo:lo + HD, c, :], start=True, stop=True)
                    ins.then_inc(S["score"], 1)

                def ret_sum(hh):
                    c, lo = hh // 2, (hh % 2) * HD
                    pe.wait_ge(S["decayed"], 2 * hh + 2)
                    if hh == 0:
                        pe.wait_ge(S["proj_evac"], 11)
                    if hh == 4:
                        pe.wait_ge(S["ret_copy"], 1)
                    for j in range(NT):
                        ins = pe.matmul(ps[lo:lo + HD, 2 + c % 2, 0:T], vtok[:, j, hh * HD:(hh + 1) * HD],
                                        headm[:, hh % 2, j * T:(j + 1) * T], start=(j == 0), stop=(j == NT - 1))
                    ins.then_inc(S["ret_done"], 1)

                job(0)
                pe.wait_ge(S["rows_in"], 1)
                pe.transpose(ps[:, 6, 0:N_ROWS], prow[:, :], ident[0:N_ROWS, 0:N_ROWS]).then_inc(S["rows_turned"], 1)
                for n in range(1, 5):
                    job(n)
                pe.wait_ge(consts_in, 48)
                pe.wait_ge(S["silu"], 3)
                for tt in range(NT):
                    for c in range(3):
                        ins = pe.transpose(ps[:, tt, c * P:(c + 1) * P], yc[:, c, tt * P:(tt + 1) * P], ident)
                    ins.then_inc(S["xs_turned"], 1)
                job(5)
                pe.wait_ge(S["silu"], 7)
                for g in range(2):
                    for j in range(NT):
                        ins = pe.matmul(ps[:, 2 + g, j * T:(j + 1) * T], yc[:, 3 + g, j * P:(j + 1) * P],
                                        yc[:, 5 + g, :], start=True, stop=True)
                    ins.then_inc(S["cb"], 1)
                pe.wait_ge(S["conv"], NCONV)
                pe.wait_ge(S["mix_params_in"], 1)
                lru_gates(0)
                lru_gates(1)
                pe.wait_ge(S["cum_rows"], 2)
                pe.wait_ge(S["dt_rows"], 1)
                for q in range(4):
                    for tt in range(NT):
                        ins = pe.transpose(ps[:, 6, (2 * q + tt) * HEADS:(2 * q + tt + 1) * HEADS],
                                           dtr[0:HEADS, 2 + q // 2, q % 2, tt * P:(tt + 1) * P],
                                           ident[0:HEADS, 0:HEADS])
                ins.then_inc(S["dt_cols"], 1)
                seg_rows(0)
                seg_rows(1)
                job(6)
                lru_gates(2)
                lru_gates(3)
                seg_rows(2)
                ssd_y(0)
                job(7)
                ssd_y(1)
                seg_rows(3)
                rot(0)
                job(8)
                seg_rows(4)
                ssd_y(2)
                rot(1)
                job_v(0)
                seg_rows(5)
                ssd_y(3)
                rot(2)
                job_v(1)
                ssd_y(4)
                ssd_y(5)
                job(11)
                score(0)
                score(1)
                job(12)
                ret_sum(0)
                score(2)
                ret_sum(1)
                score(3)
                job(13)
                pe.wait_ge(S["z_gate"], 3)
                norm_pe(pe, 1, memn, 0, 2, range(0, 4))
                for hh in range(2, HEADS):
                    ret_sum(hh)
                    if hh + 2 < HEADS:
                        score(hh + 2)
                job(14)
                pe.wait_ge(S["turned_act"], 4 + 2)
                pe.wait_ge(S["turned_vec"], 4 + 2)
                norm_pe(pe, 1, memn, 0, 2, range(4, NK))
                pe.wait_ge(S["ret_sq"], 1)
                normed_T_ready(pe, 1)
                for c in range(3):
                    ins = pe.matmul(ret_means[:, c, :], C("head_mean"), sq[:, c, :], start=True, stop=True)
                ins.then_inc(S["ret_mean"], 1)

                def out_proj(chunks, first, last):
                    for n in range(4):
                        tt, half = n // 2, n % 2
                        for c in chunks:
                            w = ring[:, PRE_SLOT[7 + c // 4], :].rearrange("p (c n) -> p c n", c=4)
                            unit(7 + c // 4)
                            ins = pe.matmul(ps[:, 4 + n, :], oT[:, c, tt * P:(tt + 1) * P],
                                            w[:, c % 4, half * 512:(half + 1) * 512],
                                            start=(first and c == chunks[0]), stop=(last and c == chunks[-1]))
                        if last:
                            ins.then_inc(S["mixed"], 1)

                pe.wait_ge(S["proj_evac"], 15)
                pe.wait_ge(S["mix_ready"], 1)
                out_proj((6, 7), True, False)
                pe.wait_ge(S["ssd_sq"], 1)
                gm = C("group_mean")
                lo, hi = slice(0, HD), slice(HD, P)
                m = [ssd_means[:, c, :] for c in range(3)]
                pe.matmul(m[0], gm, ssq[:, 0, :], start=True, stop=False)
                pe.matmul(m[0], gm[lo], ssq[lo, 1, :], start=False, stop=True)
                pe.matmul(m[1][lo], gm[:, lo], ssq[:, 0, :], start=True, stop=False)
                pe.matmul(m[1][lo], gm[lo, lo], ssq[lo, 1, :], start=False, stop=True)
                pe.matmul(m[1][hi], gm[:, lo], ssq[:, 2, :], start=True, stop=False)
                pe.matmul(m[1][hi], gm[hi, lo], ssq[hi, 1, :], start=False, stop=True)
                pe.matmul(m[2], gm, ssq[:, 2, :], start=True, stop=False)
                pe.matmul(m[2], gm[hi], ssq[hi, 1, :], start=False, stop=True).then_inc(S["ssd_mean"], 1)
                pe.wait_ge(S["mix_ready"], 2)
                out_proj((0, 1, 2), False, False)
                pe.wait_ge(S["mix_ready"], 5)
                out_proj((3, 4, 5), False, True)
                attention_pe(pe)

    wq_v = a["ca_wq"].rearrange("l (p k) n -> l p k n", k=NK)
    wo_v = a["ca_wo"].rearrange("l (c p) n -> l p c n", p=P)

    def attention_loads(sp, layer):
        sp.wait_ge(S["mixed"], 4)
        free = {15: (S["kv"], 2), 16: (S["kv"], 4)}
        for u in range(11, 17):
            if u in free:
                sp.wait_ge(*free[u])
            s = PRE_SLOT[u]
            if u < 13:
                kv_load(sp, layer, u)
                continue
            if u < 15:
                c = 512 * (u - 13)
                dst = ring[:, s, :].rearrange("p (k n) -> p k n", k=NK)
                src = wq_v[bass.ds(layer, 1), :, :, c:c + 512].rearrange("l p k n -> p (l k) n")
            else:
                c = 4 * (u - 15)
                dst = ring[:, s, :].rearrange("p (c n) -> p c n", c=4)
                src = wo_v[bass.ds(layer, 1), :, c:c + 4, :].rearrange("l p c n -> p (l c) n")
            sp.dma_start(dst, src).then_inc(full[s], 16)
        ready = ((S["kv"], 6), (S["kv"], 8), (S["q_proj"], 2), (S["q_proj"], 4), (S["att_o"], 4), (S["att_o"], 4),
                 (S["att_out"], 4), (S["att_out"], 4))
        for m in range(AROUND):
            sp.wait_ge(*ready[m])
            expert_load(sp, layer * NE + m // 3, m % 3, EXPERT_SLOT[m])
        experts_loads(sp, layer)

    def attention_act(act):
        act.wait_ge(S["mixed_added"], 4)
        norm_squares(act, 2, h, xn)
        norm_act(act, 2, h, xn)
        turned_act(act, 2, xnT, 4)
        for n in range(0, 8, 2):
            act.wait_ge(S["kv"], n + 1)
            dst = kT[:, 2 * n:2 * n + 2, :] if n < 4 else vm[:, n % 2, (n // 2 - 2) * 512:(n // 2 - 1) * 512]
            src = ps[:, n % 4, :]
            if n < 4:
                src = src.rearrange("p (a b) -> p a b", a=2)
            act.activation(dst, src, ACT.Copy).then_inc(S["kv_evac"], 1)

        def q_evac(n):
            act.wait_ge(S["q_proj"], n + 1)
            act.activation(qT[:, 2 * n:2 * n + 2, :], ps[:, n, :].rearrange("p (a b) -> p a b", a=2),
                           ACT.Copy, scale=1.0 / 16.0).then_inc(S["q_evac"], 1)

        def att_exp(hd):
            act.wait_ge(S["att_max"], hd + 1)
            for st in range(NT):
                act.activation(prob[:, hd, st, :], ps[:, 4 + hd, st * T:(st + 1) * T], ACT.Exp,
                               bias=att_stat[:, 0, hd, st:st + 1],
                               accum_out=att_stat[:, 1, hd, st:st + 1]).then_inc(S["att_exp"], 1)

        q_evac(0)
        att_exp(0)
        q_evac(2)
        att_exp(1)
        att_exp(2)

        def att_pt(hd):
            act.wait_ge(S["att_turned"], hd + 1)
            act.activation(probT[:, hd], ps[:, hd, :].rearrange("p (a b) -> p a b", a=2), ACT.Copy
                           ).then_inc(S["att_pt"], 1)

        att_pt(0)
        att_exp(3)
        att_pt(2)
        for hd in range(0, CA_HEADS, 2):
            act.wait_ge(S["att_o"], hd + 1)
            act.activation(attT[:, 2 * hd:2 * hd + 2, :], ps[:, 4 + hd, :].rearrange("p (a b) -> p a b", a=2),
                           ACT.Copy).then_inc(S["att_oevac"], 1)
        sqrt_table(act)
        norm_squares(act, 3, h, xn, S["att_added"])
        router_act(act)
        experts_act(act)

    def attention_vec(vec):
        norm_vec(vec, 2, h, xn)
        turned_vec(vec, 2, xnT, 4)
        for n in range(1, 8, 2):
            vec.wait_ge(S["kv"], n + 1)
            dst = kT[:, 2 * n:2 * n + 2, :] if n < 4 else vm[:, n % 2, (n // 2 - 2) * 512:(n // 2 - 1) * 512]
            src = ps[:, n % 4, :]
            if n < 4:
                src = src.rearrange("p (a b) -> p a b", a=2)
            vec.tensor_copy(dst, src).then_inc(S["kv_evac_vec"], 1)
        mark, link = chained(vec, S["att_step"])

        def q_evac(n):
            vec.wait_ge(S["q_proj"], n + 1)
            vec.tensor_scalar(qT[:, 2 * n:2 * n + 2, :], ps[:, n, :].rearrange("p (a b) -> p a b", a=2),
                              1.0 / 16.0, None, ALU.mult).then_inc(S["q_evac_vec"], 1)

        def att_max(hd):
            vec.wait_ge(S["att_score"], hd + 1)
            vec.tensor_reduce(att_stat[:, 0, hd, :], ps[:, 4 + hd, :].rearrange("p (a b) -> p a b", a=2),
                              AX_X, ALU.max, negate=True).then_inc(S["att_max"], 1)

        def att_prob(hd):
            vec.wait_ge(S["att_exp"], 2 * hd + 2)
            link(vec.reciprocal(att_stat[:, 2, hd, :], att_stat[:, 1, hd, :]))
            for st in range(NT):
                vec.tensor_scalar(prob[:, hd, st, :], prob[:, hd, st, :], att_stat[:, 2, hd, st:st + 1],
                                  None, ALU.mult).then_inc(S["att_prob"], 1)

        q_evac(1)
        att_max(0)
        att_prob(0)
        att_max(1)
        att_prob(1)
        q_evac(3)
        att_max(2)
        att_prob(2)
        att_max(3)

        def att_pt(hd):
            vec.wait_ge(S["att_turned"], hd + 1)
            vec.tensor_copy(probT[:, hd], ps[:, hd, :].rearrange("p (a b) -> p a b", a=2)
                            ).then_inc(S["att_pt_vec"], 1)

        att_pt(1)
        att_prob(3)
        att_pt(3)
        for hd in range(1, CA_HEADS, 2):
            vec.wait_ge(S["att_o"], hd + 1)
            vec.tensor_copy(attT[:, 2 * hd:2 * hd + 2, :],
                            ps[:, 4 + hd, :].rearrange("p (a b) -> p a b", a=2)).then_inc(S["att_oevac_vec"], 1)
        for n in range(4):
            vec.wait_ge(S["att_out"], n + 1)
            hs = h[:, n // 2, (n % 2) * 512:(n % 2 + 1) * 512]
            vec.tensor_tensor(hs, hs, ps[:, n, :], ALU.add).then_inc(S["att_added"], 1)
            if n >= 2:
                raw_evac(vec, n - 2)
        router_vec(vec)
        experts_vec(vec)

    def attention_pe(pe):
        def unit(u):
            pe.wait_ge(full[PRE_SLOT[u]], 16 * sum(PRE_SLOT[v] == PRE_SLOT[u] for v in range(u + 1)))
            return ring[:, PRE_SLOT[u], :]

        for n in range(4):
            if n == 2:
                norm_pe(pe, 2, xn, 4)
            w = unit(9 + n // 2).rearrange("p (k n) -> p k n", k=NK)
            for b in range(2):
                c0 = ((2 * n + b) % 4) * P
                for k in range(NK):
                    ins = pe.matmul(ps[:, n, b * T:(b + 1) * T], w[:, k, c0:c0 + P], memT[:, k, :],
                                    start=(k == 0), stop=(k == NK - 1))
            ins.then_inc(S["kv"], 1)
        for n in range(4, 8):
            w = unit(9 + n // 2).rearrange("p (k n) -> p k n", k=NK)
            pe.wait_ge(S["kv_evac"] if n % 2 == 0 else S["kv_evac_vec"], n // 2 - 1)
            for k in range(NK):
                ins = pe.matmul(ps[:, n % 4, :], memT[:, k, (n % 2) * P:(n % 2 + 1) * P], w[:, k, :],
                                start=(k == 0), stop=(k == NK - 1))
            ins.then_inc(S["kv"], 1)
        normed_T_ready(pe, 2)

        def q_job(n):
            w = unit(13 + n // 2).rearrange("p (k n) -> p k n", k=NK)
            pe.wait_ge(S["kv_evac"] if n % 2 == 0 else S["kv_evac_vec"], n // 2 + 3)
            for b in range(2):
                c0 = ((2 * n + b) % 4) * P
                for k in range(NK):
                    ins = pe.matmul(ps[:, n, b * T:(b + 1) * T], w[:, k, c0:c0 + P], xnT[:, k, :],
                                    start=(k == 0), stop=(k == NK - 1))
            ins.then_inc(S["q_proj"], 1)

        def att_score(hd):
            pe.wait_ge(S["q_evac"] if hd % 2 == 0 else S["q_evac_vec"], hd // 2 + 1)
            for st in range(NT):
                for c in range(2):
                    ins = pe.matmul(ps[:, 4 + hd, st * T:(st + 1) * T],
                                    qT[:, 2 * hd + c, st * P:(st + 1) * P], kT[:, 2 * hd + c, :],
                                    start=(c == 0), stop=(c == 1))
            ins.then_inc(S["att_score"], 1)

        def att_turned(hd):
            pe.wait_ge(S["att_prob"], 2 * hd + 2)
            for mt in range(NT):
                for st in range(NT):
                    ins = pe.transpose(ps[:, hd, mt * T + st * P:mt * T + (st + 1) * P],
                                       prob[:, hd, st, mt * P:(mt + 1) * P], ident)
            ins.then_inc(S["att_turned"], 1)

        def att_o(hd):
            pe.wait_ge(S["att_pt"] if hd % 2 == 0 else S["att_pt_vec"], hd // 2 + 1)
            for c in range(2):
                for mt in range(NT):
                    o = hd * 2 * P + c * P
                    ins = pe.matmul(ps[:, 4 + hd, c * T:(c + 1) * T], vm[:, mt, o:o + P],
                                    probT[:, hd, mt, :], start=(mt == 0), stop=(mt == 1))
            ins.then_inc(S["att_o"], 1)

        q_job(0)
        q_job(1)
        att_score(0)
        q_job(2)
        att_score(1)
        q_job(3)
        att_score(2)
        att_turned(0)
        att_score(3)
        att_turned(1)
        att_turned(2)
        att_o(0)
        att_o(1)
        att_turned(3)
        att_o(2)
        att_o(3)
        wo = [unit(15 + i).rearrange("p (c n) -> p c n", c=4) for i in range(2)]
        for n in range(4):
            for c in range(NK):
                if n == 0 and c % 2 == 0:
                    pe.wait_ge(S["att_oevac"] if c % 4 == 0 else S["att_oevac_vec"], c // 4 + 1)
                ins = pe.matmul(ps[:, n, :], attT[:, c, (n // 2) * P:(n // 2 + 1) * P],
                                wo[c // 4][:, c % 4, (n % 2) * 512:(n % 2 + 1) * 512],
                                start=(c == 0), stop=(c == NK - 1))
            ins.then_inc(S["att_out"], 1)
            if n == 2:
                turn_raw(pe, 0)
        logits(pe, 0)
        turn_raw(pe, 1)
        logits(pe, 1)
        router_pe(pe)
        experts_pe(pe)

    w1_v = a["moe_w1"].rearrange("l e (p k) f -> (l e) p k f", k=NK)
    w3_v = a["moe_w3"].rearrange("l e (p k) f -> (l e) p k f", k=NK)
    w2_v = a["moe_w2"].rearrange("l e (half p b) d -> (l e) p half b d", half=2, b=2)

    def expert_slot(r, i):
        return EXPERT_SLOT[(3 * r + i) % AROUND]

    def slot(s):
        return ring[:, s, :] if s < RING else arena[:, tail0 + (s - RING) * UNIT:tail0 + (s - RING + 1) * UNIT]

    def expert_load(sp, which, i, s):
        if i < 2:
            dst = slot(s).rearrange("p (w k n) -> p w k n", w=2, k=4)
            for w, v in enumerate((w1_v, w3_v)):
                src = v[bass.ds(which, 1), :, 4 * i:4 * i + 4, :].rearrange("e p k f -> p (e k) f")
                sp.dma_start(dst[:, w], src).then_inc(xfull[s], 16)
        else:
            dst = slot(s).rearrange("p (half b d) -> p half b d", half=2, b=2)
            for half in range(2):
                src = w2_v[bass.ds(which, 1), :, half, :, :].rearrange("e p b d -> p (e b) d")
                sp.dma_start(dst[:, half], src).then_inc(xfull[s], 16)

    def unit_landed(pe, it, r, i):
        m = 3 * r + i
        pe.wait_ge(xfull[EXPERT_SLOT[m % AROUND]], pe.snap(96 * it + 32 * (m // AROUND + 1)))

    def hidden_matmuls(pe, s, i, lhs, bank):
        w = slot(s).rearrange("p (w k n) -> p w k n", w=2, k=4)
        for k in range(4):
            for j in range(4):
                ins = pe.matmul(ps[CAP * j:CAP * (j + 1), bank, 0:T], lhs(4 * i + k),
                                w[:, j // 2, k, (j % 2) * T:(j % 2 + 1) * T], start=(i == 0 and k == 0),
                                stop=(i == 1 and k == 3))
        return ins

    def down_matmuls(pe, s, hT, bank):
        w = slot(s).rearrange("p (f d) -> p f d", f=4)
        for f in range(4):
            for j in range(4):
                ins = pe.matmul(ps[CAP * j:CAP * (j + 1), bank, 0:T], hT[:, f % 2, (f // 2) * CAP:(f // 2 + 1) * CAP],
                                w[:, f, j * T:(j + 1) * T], start=(f == 0), stop=(f == 3))
        return ins

    def gathered(bank):
        return ps[:, bank, :].rearrange("p (k s) -> p k s", k=4)

    def gather(pe, bank, half):
        for k in range(4):
            for tt in range(NT):
                ins = pe.matmul(gathered(bank)[:, k, :], xn[:, tt, 4 * half + k::NK], sel[:, tt, :],
                                start=(tt == 0), stop=(tt == NT - 1))
        return ins

    def gather_evac_act(act, bank, half, q):
        for k in range(4):
            ins = act.activation(stage[:, q, 4 * half + k, :], gathered(bank)[:, k, :], ACT.Copy,
                                 scale=gains[:, 3, 4 * half + k:4 * half + k + 1])
        return ins

    def raw_T(tt, half):
        return ps[:, 4 + 2 * tt + half, :].rearrange("p (k t) -> p k t", k=4)

    def turn_raw(pe, tt):
        pe.wait_ge(S["att_added"], 2 * tt + 2)
        for k in range(NK):
            ins = pe.transpose(raw_T(tt, k // 4)[:, k % 4, :], h[:, tt, k::NK], ident)
            if k % 4 == 3:
                ins.then_inc(S["turned"], 1)

    def raw_evac(vec, tt):
        for half in range(2):
            vec.wait_ge(S["turned"], 12 + 2 * tt + half + 1)
            ks = slice(4 * half, 4 * half + 4)
            vec.tensor_tensor(xnT[:, ks, tt * P:(tt + 1) * P], raw_T(tt, half),
                              gains[:, 3, ks].unsqueeze(2).to_broadcast([P, 4, P]), ALU.mult
                              ).then_inc(S["turned_vec"], 1)

    def logits(pe, tt):
        for k in range(NK):
            if k % 4 == 0:
                pe.wait_ge(S["turned_vec"], 12 + 2 * tt + k // 4 + 1)
            ins = pe.matmul(ps[:, tt, 0:GROUPS + NE], xnT[:, k, tt * P:(tt + 1) * P], wge[:, k, :],
                            start=(k == 0), stop=(k == NK - 1))
        ins.then_inc(S["logits"], 1)

    def router_act(act):
        norm_act(act, 3, h, xn)
        act.wait_ge(S["logits_sb"], 1)
        act.activation(r_ge, r_ge, ACT.Exp).then_inc(S["group_exp"], 1)
        act.wait_ge(S["gate_exp"], 1)
        act.activation(r_m2, r_m2, ACT.Exp).then_inc(S["gate_exp"], 1)
        act.wait_ge(S["gather"], 1)
        gather_evac_act(act, 0, 0, 0).then_inc(S["gather_act"], 1)

    def router_vec(vec):
        mark, link = chained(vec, S["route_step"])
        mark(vec.tensor_scalar(r_iota, C("iota", 0, NE), -64.0, None, ALU.add))
        norm_scale_vec(vec, 3)
        lg = r_lg
        for tt in range(NT):
            vec.wait_ge(S["logits"], tt + 1)
            n = mark(vec.scalar_tensor_tensor(lg[:, tt, :], ps[:, tt, 0:GROUPS + NE], stat[:, 3, tt, 3:4], bge[:, :],
                                              ALU.mult, ALU.add))
        vec.wait_ge(S["route_step"], n)

        def over(x, n):
            return x.unsqueeze(2).to_broadcast([P, NT, n])

        def first_max(x, mx_, one, n):
            iota = r_iota[:, 0:n].unsqueeze(1).to_broadcast([P, NT, n])
            link(vec.tensor_reduce(mx_, x, AX_X, ALU.max))
            link(vec.tensor_tensor(one, x, over(mx_, n), ALU.is_equal))
            link(vec.tensor_tensor(one, one, iota, ALU.mult))
            link(vec.tensor_reduce(r_min, one, AX_X, ALU.min))
            link(vec.tensor_tensor(one, iota, over(r_min, n), ALU.is_equal))

        first_max(lg[:, :, 0:GROUPS], r_gm, r_og, GROUPS)
        vec.tensor_tensor(r_ge, lg[:, :, 0:GROUPS], over(r_gm, GROUPS), ALU.subtract).then_inc(S["logits_sb"], 1)
        link(vec.tensor_scalar(r_og, r_og, -1.0, 1e30, ALU.add, ALU.mult))
        for tt in range(NT):
            og = r_og[:, tt, :].unsqueeze(2).to_broadcast([P, GROUPS, PER_GROUP])
            n = mark(vec.tensor_tensor(r_el[:, tt, :].rearrange("p (g e) -> p g e", g=GROUPS),
                                       lg[:, tt, GROUPS:].rearrange("p (g e) -> p g e", g=GROUPS), og, ALU.add))
        vec.wait_ge(S["route_step"], n)
        first_max(r_el, r_m1, r_e1, NE)
        link(vec.scalar_tensor_tensor(r_el, r_e1, -1e30, r_el, ALU.mult, ALU.add))
        first_max(r_el, r_m2, r_e2, NE)
        vec.tensor_tensor(r_ea, r_e1, r_e2, ALU.add).then_inc(S["routed"], 1)
        vec.tensor_tensor(r_m2, r_m2, r_m1, ALU.subtract).then_inc(S["gate_exp"], 1)
        norm_rows_vec(vec, 3, h, xn)
        vec.wait_ge(S["group_exp"], 1)
        link(vec.tensor_reduce(r_gm, r_ge, AX_X, ALU.add))
        vec.wait_ge(S["gate_exp"], 2)
        link(vec.tensor_scalar(r_m1, r_m2, 1.0, None, ALU.add))
        link(vec.tensor_tensor(r_gm, r_gm, r_m1, ALU.mult))
        link(vec.reciprocal(slotc[:, :, 2], r_gm))
        link(vec.tensor_tensor(slotc[:, :, 3], slotc[:, :, 2], r_m2, ALU.mult))
        vec.wait_ge(S["rank_mm"], 1)
        rank = ps[:, 6, 0:2 * NE].rearrange("p (t e) -> p t e", t=NT)
        first_slot = C("first_slot").unsqueeze(1).to_broadcast([P, NT, NE])

        def slots_of(sv, one1, one2, dst):
            for e, one in ((r_e1, one1), (r_e2, one2)):
                n = mark(vec.tensor_tensor(one, e, sv, ALU.mult))
            vec.wait_ge(S["route_step"], n)
            for i, one in enumerate((one1, one2)):
                n = mark(vec.tensor_reduce(dst[:, :, i], one, AX_X, ALU.add))
            vec.wait_ge(S["route_step"], n)

        mark(vec.tensor_scalar(r_sv, rank, float(CAP), 4.0 * SLOTS, ALU.is_ge, ALU.mult))
        link(vec.tensor_tensor(r_in, rank, first_slot, ALU.add))
        link(vec.tensor_tensor(r_sv, r_sv, r_in, ALU.add))
        slots_of(r_sv, r_a1, r_a2, r_first)
        for tt in range(NT):
            n = mark(vec.tensor_scalar(sel[:, tt, :], C("iota", 0, P), r_first[:, tt, 0:1], None, ALU.is_equal))
        vec.wait_ge(S["route_step"], n)
        for tt in range(NT):
            vec.scalar_tensor_tensor(sel[:, tt, :], C("iota", 0, P), r_first[:, tt, 1:2], sel[:, tt, :],
                                     ALU.is_equal, ALU.add).then_inc(S["sel"], 1)
        vec.wait_ge(S["rank_mm"], 2)
        cnt = ps[:, 7, 0:NE].unsqueeze(2).to_broadcast([P, NE, T // CAP - 1])
        steps = C("first_slot", 1, T // CAP - 1).unsqueeze(1).to_broadcast([P, NE, T // CAP - 1])
        link(vec.tensor_tensor(r_more, cnt, steps, ALU.is_gt))
        link(vec.tensor_reduce(r_nov, r_more, AX_X, ALU.add))
        link(vec.tensor_tensor_scan(ov_table[:, 0:NE], C("ones", 0, NE), r_nov, 0.0, ALU.mult, ALU.add))
        link(vec.tensor_tensor(r_nov, ov_table[:, 0:NE], r_nov, ALU.subtract))
        link(vec.scalar_tensor_tensor(r_nov, r_nov, float(CAP), C("first_slot"), ALU.mult, ALU.subtract))
        link(vec.tensor_scalar(r_nov, r_nov, float(SLOTS - CAP), None, ALU.add))
        link(vec.scalar_tensor_tensor(r_sv, rank, float(CAP), r_nov.unsqueeze(1).to_broadcast([P, NT, NE]),
                                      ALU.is_ge, ALU.mult))
        link(vec.tensor_tensor(r_sv, r_sv, r_in, ALU.add))
        slots_of(r_sv, r_a1, r_a2, slotc)
        mark(vec.tensor_scalar(slot_left, slotc[:, :, 0:2], -float(P), None, ALU.add))
        for tt in range(NT):
            for q in range(4):
                ins = vec.tensor_scalar(diag[:, tt, q, :], ident, slotc[:, tt, q:q + 1], None, ALU.mult)
                ins.then_inc(S["diag"], 1)
        mark(vec.tensor_copy(ov_int[:, 0:1], ov_table[:, NE - 1:NE]))
        vec.wait_ge(S["gather"], 2)
        vec.tensor_tensor(stage[:, 0, 4:8, :], gathered(1), gains[:, 3, 4:8].unsqueeze(2).to_broadcast([P, 4, P]),
                          ALU.mult).then_inc(S["gather_vec"], 1)

    def router_pe(pe):
        pe.wait_ge(S["routed"], 1)
        pe.matmul(ps[:, 6, 0:NE], C("before"), r_ea[:, 0, :], start=True, stop=True)
        pe.matmul(ps[:, 6, NE:2 * NE], C("ones"), r_ea[:, 0, :], start=True, stop=False)
        pe.matmul(ps[:, 6, NE:2 * NE], C("before"), r_ea[:, 1, :], start=False, stop=True).then_inc(S["rank_mm"], 1)
        pe.matmul(ps[:, 7, 0:NE], C("ones"), r_ea[:, 0, :], start=True, stop=False)
        pe.matmul(ps[:, 7, 0:NE], C("ones"), r_ea[:, 1, :], start=False, stop=True).then_inc(S["rank_mm"], 1)
        pe.wait_ge(S["sel"], 2)
        pe.wait_ge(S["normed_act"], 4)
        pe.wait_ge(S["normed_vec"], 4)
        for half in range(2):
            gather(pe, half, half).then_inc(S["gather"], 1)
        for tt in range(NT):
            pe.wait_ge(S["diag"], 4 * tt + 4)
            pe.matmul(ps[:, 4 + tt, :], C("ones"), diag[:, tt].rearrange("p q s -> p (q s)"), start=True,
                      stop=True).then_inc(S["diag_mm"], 1)

    H0, C0, A0 = 16, 8, 2
    G0 = 2
    turns = SLOTS // TURN
    GATHER_AT = (1, 2)

    def experts_loads(sp, layer):
        def load_behind(turn, m, value):
            r, i = m // 3, m % 3
            if i < 2:
                sp.wait_ge(S["x_hidden"], value(16 * turn + 2 * r + i + 1 + H0))
            else:
                sp.wait_ge(S["x_y"], value(8 * turn + r + 1))
            n = m + AROUND
            expert_load(sp, layer * NE + 8 * turn + n // 3, n % 3, EXPERT_SLOT[n % AROUND])

        with sp.Fori(0, turns - 1) as it:
            for m in range(3 * 8):
                load_behind(it, m, sp.snap)
        for m in range(3 * 8 - AROUND):
            load_behind(turns - 1, m, int)
        with sp.If(layer < DEPTH - 1):
            following = nc.s_assert_within(layer + 1, 1, DEPTH - 1, skip_runtime_bounds_check_because=
                                           "this branch is taken where layer is below DEPTH - 1")
            for part in range(len(PARAM_LOADS)):
                issue_params(sp, following, part)
            for u in range(EARLY):
                m = 3 * 8 - AROUND + EXPERT_SLOT.index(PRE_SLOT[u])
                r, i = NE - 8 + m // 3, m % 3
                sp.wait_ge(S["x_hidden"], 2 * r + i + 1 + H0) if i < 2 else sp.wait_ge(S["x_y"], r + 1)
                w_in_load(sp, following, u, next_unit[u])
        with sp.Else():
            pass

    def experts_act(act):
        act.sem_inc(S["x_yact"], A0)
        act.sem_inc(S["x_gather_act"], G0)
        with act.Fori(0, turns) as it:
            for r in range(8):
                q, b = r // 4, r % 2
                act.wait_ge(S["x_hidden"], act.snap(16 * it + 2 * r + 2 + H0))
                act.activation(gated[0:64, b, :], ps[0:64, b, 0:T], ACT.Tanh, scale=0.5).then_inc(S["x_tanh"], 1)
                act.wait_ge(S["x_hT"], act.snap(8 * it + r + 1))
                act.activation(hTs[:, b], ps[:, 2, 0:4 * CAP].rearrange("p (a b) -> p a b", a=2), ACT.Copy
                               ).then_inc(S["x_hTsb"], 1)
                if r % 4 in GATHER_AT:
                    i = GATHER_AT.index(r % 4)
                    act.wait_ge(S["x_gather"], act.snap(4 * it + 2 * q + i + 1 + G0))
                    gather_evac_act(act, 3, i, 1 - q).then_inc(S["x_gather_act"], 1)
                act.wait_ge(S["x_y"], act.snap(8 * it + r + 1))
                if r % 4 == 0:
                    act.wait_ge(S["x_scat"], act.snap(8 * it + 4 * q + C0))
                lo = CAP * (r % 4)
                for j in range(2):
                    ins = act.activation(ysb[lo:lo + CAP, j * T:(j + 1) * T],
                                         ps[CAP * j:CAP * (j + 1), 4 + b, 0:T], ACT.Copy)
                ins.then_inc(S["x_yact"], 1)

    def experts_vec(vec):
        vec.sem_inc(S["x_h"], A0)
        vec.sem_inc(S["x_yvec"], A0)
        vec.sem_inc(S["x_added"], A0)
        for tt in range(NT):
            vec.wait_ge(S["diag_mm"], tt + 1)
            vec.tensor_copy(rows4[:, :, tt * P:(tt + 1) * P], ps[:, 4 + tt, :].rearrange("p (q s) -> p q s", q=4)
                            ).then_inc(S["bcast"], 1)
        vec.tensor_copy(slot_id[:, :], C("part")).then_inc(S["bcast"], 1)
        vec.memset(ov_at[:, 0:1], float(SLOTS)).then_inc(S["bcast"], 1)
        vec.memset(ov_at[:, 1:2], 0.0).then_inc(S["bcast"], 1)
        vec.wait_ge(S["bcast"], NT + 3)
        with vec.Fori(0, turns) as it:
            for r in range(8):
                q, b = r // 4, r % 2
                if r % 4 == 0:
                    vec.wait_ge(S["x_scat"], vec.snap(8 * it + 4 * q + 4))
                    vec.scalar_tensor_tensor(selT[:, q, :], rows4[:, 0, :], slot_id[:, 0:1], rows4[:, 2, :],
                                             ALU.is_equal, ALU.mult).then_inc(S["x_vec"], 1)
                    vec.scalar_tensor_tensor(rows_t, rows4[:, 1, :], slot_id[:, 0:1], rows4[:, 3, :],
                                             ALU.is_equal, ALU.mult).then_inc(S["x_vec"], 1)
                    vec.wait_ge(S["x_vec"], vec.snap(6 * it + 3 * q + 2))
                    vec.tensor_tensor(selT[:, q, :], selT[:, q, :], rows_t, ALU.add).then_inc(S["x_selT"], 1)
                    vec.tensor_scalar(slot_id[:, :], slot_id[:, :], float(P), None, ALU.add
                                      ).then_inc(S["x_vec"], 1)
                    vec.wait_ge(S["x_vec"], vec.snap(6 * it + 3 * q + 3))
                    vec.wait_ge(S["x_selT"], vec.snap(2 * it + q + 1))
                if r % 4 == 0:
                    vec.wait_ge(S["x_gather"], vec.snap(4 * it + 2 * q + G0))
                    for tt in range(NT):
                        vec.tensor_scalar(sel[:, tt, :], C("iota", 0, P), slot_left[:, tt, 0:1], None,
                                          ALU.is_equal).then_inc(S["x_sel"], 1)
                    vec.wait_ge(S["x_sel"], vec.snap(10 * it + 5 * q + 2))
                    for tt in range(NT):
                        vec.scalar_tensor_tensor(sel[:, tt, :], C("iota", 0, P), slot_left[:, tt, 1:2],
                                                 sel[:, tt, :], ALU.is_equal, ALU.add).then_inc(S["x_sel"], 1)
                    vec.wait_ge(S["x_sel"], vec.snap(10 * it + 5 * q + 4))
                    vec.tensor_scalar(slot_left, slot_left, -float(P), None, ALU.add).then_inc(S["x_sel"], 1)
                    vec.wait_ge(S["x_sel"], vec.snap(10 * it + 5 * q + 5))
                vec.wait_ge(S["x_tanh"], vec.snap(8 * it + r + 1))
                vec.scalar_tensor_tensor(gated[64:128, b, :], gated[0:64, b, :], 1.0, ps[0:64, b, 0:T],
                                         ALU.add, ALU.mult).then_inc(S["x_gated"], 1)
                vec.wait_ge(S["x_gated"], vec.snap(8 * it + r + 1))
                vec.scalar_tensor_tensor(hsb[64:128, b, :], gated[64:128, b, :], 0.5, ps[64:128, b, 0:T],
                                         ALU.mult, ALU.mult).then_inc(S["x_h"], 1)
                vec.wait_ge(S["x_y"], vec.snap(8 * it + r + 1))
                lo = CAP * (r % 4)
                for j in range(2, 4):
                    ins = vec.tensor_copy(ysb[lo:lo + CAP, j * T:(j + 1) * T],
                                          ps[CAP * j:CAP * (j + 1), 4 + b, 0:T])
                ins.then_inc(S["x_yvec"], 1)
                if r % 4 == 3:
                    for n in range(4):
                        vec.wait_ge(S["x_scat"], vec.snap(8 * it + 4 * q + n + 1 + C0))
                        hs = h[:, n // 2, (n % 2) * 512:(n % 2 + 1) * 512]
                        vec.tensor_tensor(hs, hs, ps[:, 6 + n % 2, :], ALU.add).then_inc(S["x_added"], 1)

    def experts_pe(pe):
        pe.sem_inc(S["x_hidden"], H0)
        pe.sem_inc(S["x_scat"], C0)
        pe.sem_inc(S["x_gather"], G0)
        pe.wait_ge(S["gather_act"], 1)
        pe.wait_ge(S["gather_vec"], 1)
        with pe.Fori(0, turns) as it:
            for r in range(8):
                q, b = r // 4, r % 2
                if r % 4 == 0:
                    pe.wait_ge(S["x_gather_act"], pe.snap(4 * it + 2 * q + G0))
                pe.wait_ge(S["x_h"], pe.snap(8 * it + r + A0 - 1))
                for i in range(2):
                    unit_landed(pe, it, r, i)
                    hidden_matmuls(pe, expert_slot(r, i), i, lambda k: stage[:, q, k, CAP * (r % 4):CAP * (r % 4 + 1)], b
                                   ).then_inc(S["x_hidden"], 1)
                if r % 4 in GATHER_AT:
                    i = GATHER_AT.index(r % 4)
                    pe.wait_ge(S["x_sel"], pe.snap(10 * it + 5 * q + 4))
                    pe.wait_ge(S["x_gather_act"], pe.snap(4 * it + 2 * q + i + G0))
                    gather(pe, 3, i).then_inc(S["x_gather"], 1)
                pe.wait_ge(S["x_h"], pe.snap(8 * it + r + A0 + 1))
                for f in range(2):
                    ins = pe.matmul(ps[:, 2, f * 64:(f + 1) * 64], hsb[64:128, b, f::2],
                                    ident[64:128, 64:128], start=True, stop=True)
                ins.then_inc(S["x_hT"], 1)
                pe.wait_ge(S["x_hTsb"], pe.snap(8 * it + r + 1))
                pe.wait_ge(S["x_yact"], pe.snap(8 * it + r + A0 - 1))
                pe.wait_ge(S["x_yvec"], pe.snap(8 * it + r + A0 - 1))
                unit_landed(pe, it, r, 2)
                down_matmuls(pe, expert_slot(r, 2), hTs[:, b], 4 + b).then_inc(S["x_y"], 1)
                if r % 4 == 3:
                    pe.wait_ge(S["x_yact"], pe.snap(8 * it + r + A0 + 1))
                    pe.wait_ge(S["x_yvec"], pe.snap(8 * it + r + A0 + 1))
                    pe.wait_ge(S["x_selT"], pe.snap(2 * it + q + 1))
                    for n in range(4):
                        tt, half = n // 2, n % 2
                        pe.wait_ge(S["x_added"], pe.snap(8 * it + 4 * q + n + A0 - 1))
                        pe.matmul(ps[:, 6 + n % 2, :], selT[:, q, tt * P:(tt + 1) * P],
                                  ysb[:, half * 512:(half + 1) * 512], start=True, stop=True
                                  ).then_inc(S["x_scat"], 1)

    def overflow(layer):
        with nc.Block() as block:
            @block.sync
            def _(sp):
                sp.wait_ge(S["ov_w"], 1)
                e = sp.value_load(ov_int[0:1, 1:2], min_val=0, max_val=NE - 1)
                for i in range(3):
                    expert_load(sp, layer * NE + e, i, expert_slot(0, i))

            @block.scalar
            def _(act):
                act.wait_ge(S["x_hidden"], 2)
                act.activation(gated[0:64, 0, :], ps[0:64, 1, 0:T], ACT.Tanh, scale=0.5).then_inc(S["x_tanh"], 1)
                act.wait_ge(S["x_hT"], 1)
                act.activation(hTs[:, 0], ps[:, 2, 0:4 * CAP].rearrange("p (a b) -> p a b", a=2), ACT.Copy
                               ).then_inc(S["x_hTsb"], 1)

            @block.vector
            def _(vec):
                mark, link = chained(vec, S["ov_step"])
                link(vec.tensor_scalar(ov_f, ov_table[:, 0:NE], ov_at[:, 1:2], None, ALU.is_le))
                link(vec.tensor_reduce(ov_at[:, 2:3], ov_f, AX_X, ALU.add))
                vec.tensor_copy(ov_int[:, 1:2], ov_at[:, 2:3]).then_inc(S["ov_w"], 1)
                for tt in range(NT):
                    link(vec.tensor_scalar(ov_s, C("iota", 0, CAP), ov_at[:, 0:1], slotc[:, tt, 0:1], ALU.add,
                                           ALU.is_equal))
                    link(vec.tensor_scalar(ov_sel[:, tt, :], C("iota", 0, CAP), ov_at[:, 0:1], slotc[:, tt, 1:2],
                                           ALU.add, ALU.is_equal))
                    vec.tensor_tensor(ov_sel[:, tt, :], ov_sel[:, tt, :], ov_s, ALU.add).then_inc(S["ov_sel"], 1)
                    vec.wait_ge(S["ov_sel"], tt + 1)
                link(vec.tensor_tensor(ov_at[:, 3:4], C("part"), ov_at[:, 0:1], ALU.add))
                link(vec.scalar_tensor_tensor(selT[:, 0, :], rows4[:, 0, :], ov_at[:, 3:4], rows4[:, 2, :],
                                              ALU.is_equal, ALU.mult))
                link(vec.scalar_tensor_tensor(rows_t, rows4[:, 1, :], ov_at[:, 3:4], rows4[:, 3, :],
                                              ALU.is_equal, ALU.mult))
                vec.tensor_tensor(selT[:, 0, :], selT[:, 0, :], rows_t, ALU.add).then_inc(S["x_selT"], 1)
                vec.wait_ge(S["ov_x"], 1)
                vec.tensor_tensor(ov_x, ps[:, 0, 0:NK * CAP].rearrange("p (k s) -> p k s", k=NK),
                                  gains[:, 3, :].unsqueeze(2).to_broadcast([P, NK, CAP]), ALU.mult
                                  ).then_inc(S["ov_xT"], 1)
                vec.wait_ge(S["x_tanh"], 1)
                vec.scalar_tensor_tensor(gated[64:128, 0, :], gated[0:64, 0, :], 1.0, ps[0:64, 1, 0:T],
                                         ALU.add, ALU.mult).then_inc(S["x_gated"], 1)
                vec.wait_ge(S["x_gated"], 1)
                vec.scalar_tensor_tensor(hsb[64:128, 0, :], gated[64:128, 0, :], 0.5, ps[64:128, 1, 0:T],
                                         ALU.mult, ALU.mult).then_inc(S["x_h"], 1)
                vec.wait_ge(S["x_y"], 1)
                for j in range(4):
                    vec.tensor_copy(ysb[0:CAP, j * T:(j + 1) * T], ps[CAP * j:CAP * (j + 1), 4, 0:T]
                                    ).then_inc(S["x_yvec"], 1)
                for n in range(4):
                    vec.wait_ge(S["x_scat"], n + 1)
                    hs = h[:, n // 2, (n % 2) * 512:(n % 2 + 1) * 512]
                    vec.tensor_tensor(hs, hs, ps[:, 6 + n % 2, :], ALU.add).then_inc(S["x_added"], 1)
                link(vec.tensor_scalar(ov_at[:, 0:1], ov_at[:, 0:1], float(CAP), None, ALU.add))
                link(vec.tensor_scalar(ov_at[:, 1:2], ov_at[:, 1:2], 1.0, None, ALU.add))

            @block.tensor
            def _(pe):
                pe.wait_ge(S["ov_sel"], 2)
                for k in range(NK):
                    for tt in range(NT):
                        ins = pe.matmul(ps[:, 0, k * CAP:(k + 1) * CAP], xn[:, tt, k::NK], ov_sel[:, tt, :],
                                        start=(tt == 0), stop=(tt == NT - 1))
                ins.then_inc(S["ov_x"], 1)
                pe.wait_ge(S["ov_xT"], 1)
                for i in range(2):
                    pe.wait_ge(xfull[expert_slot(0, i)], 32)
                    hidden_matmuls(pe, expert_slot(0, i), i, lambda k: ov_x[:, k, :], 1).then_inc(S["x_hidden"], 1)
                pe.wait_ge(S["x_h"], 1)
                for f in range(2):
                    ins = pe.matmul(ps[:, 2, f * 64:(f + 1) * 64], hsb[64:128, 0, f::2], ident[64:128, 64:128],
                                    start=True, stop=True)
                ins.then_inc(S["x_hT"], 1)
                pe.wait_ge(S["x_hTsb"], 1)
                pe.wait_ge(xfull[expert_slot(0, 2)], 32)
                down_matmuls(pe, expert_slot(0, 2), hTs[:, 0], 4).then_inc(S["x_y"], 1)
                pe.wait_ge(S["x_yvec"], 4)
                pe.wait_ge(S["x_selT"], 1)
                for n in range(4):
                    tt, half = n // 2, n % 2
                    if n >= 2:
                        pe.wait_ge(S["x_added"], n - 1)
                    pe.matmul(ps[:, 6 + n % 2, :], selT[0:CAP, 0, tt * P:(tt + 1) * P],
                              ysb[0:CAP, half * 512:(half + 1) * 512], start=True, stop=True).then_inc(S["x_scat"], 1)

    with nc.Fori(0, DEPTH) as layer:
        one_layer(layer)
        nc.sync.sem_clear(layer_sems)
        nc.all_engine_barrier()
        overflow_blocks = nc.values_load(ov_int[0:1, 0:1], min_val=0, max_val=OV_BLOCKS)
        with nc.If(overflow_blocks > 0):
            with nc.Fori(0, overflow_blocks):
                overflow(layer)
                nc.sync.sem_clear(layer_sems)
                nc.all_engine_barrier()
        with nc.Else():
            pass

    with nc.Block() as block:
        @block.sync
        def _(sp):
            sp.dma_start(ysb, a["g_final"].rearrange("(o d) -> o d", o=1).to_broadcast([P, D])
                         ).then_inc(consts_in, 16)
            for tt in range(NT):
                sp.wait_ge(S["mixed"], tt + 1)
                sp.dma_start(out_v[:, tt:tt + 1, :], xn[:, tt:tt + 1, :]).then_inc(consts_in, 16)
            sp.wait_ge(consts_in, 96)

        @block.scalar
        def _(act):
            sqrt_table(act)
            for tt in range(NT):
                act.activation(xn[:, tt, :], h[:, tt, :], ACT.Square, accum_out=stat[:, 0, tt, 0:1]
                               ).then_inc(S["squared"], 1)
            act.wait_ge(S["variance"], 1)
            act.activation(stat[:, 0, :, 2], stat[:, 0, :, 1], ACT.Sqrt).then_inc(S["deviation"], 1)

        @block.vector
        def _(vec):
            vec.wait_ge(S["squared"], NT)
            vec.tensor_scalar(stat[:, 0, :, 1], stat[:, 0, :, 0], 1.0 / D, EPS, ALU.mult, ALU.add
                              ).then_inc(S["variance"], 1)
            vec.wait_ge(S["deviation"], 1)
            vec.reciprocal(stat[:, 0, :, 3], stat[:, 0, :, 2]).then_inc(S["inverse"], 1)
            vec.wait_ge(S["inverse"], 1)
            vec.wait_ge(consts_in, 64)
            for tt in range(NT):
                vec.scalar_tensor_tensor(xn[:, tt, :], h[:, tt, :], stat[:, 0, tt, 3:4], ysb, ALU.mult,
                                         ALU.mult).then_inc(S["mixed"], 1)
    ctx.close()


INPUTS = ("x mem g_mix w_in w_out ssd_conv_w ssd_conv_b ssd_dt_bias ssd_a_log ssd_d ssd_norm lru_conv_w lru_conv_b "
          "lru_lambda lru_wa lru_ba lru_wx lru_bx g_ca g_mem ca_wq ca_wkv ca_wo g_moe moe_wg moe_bg moe_we moe_be "
          "moe_w1 moe_w3 moe_w2 g_final").split()


def kernel(**inputs):
    import concourse.bacc as bacc
    from concourse.bass_utils import run_bass_kernel_spmd

    nc = bacc.Bacc("TRN2", target_bir_lowering=False, num_devices=1)
    arrays = {f"in_{n}": np.ascontiguousarray(inputs[n]) for n in INPUTS}
    arrays["in_const"] = constants()
    aps = {n[3:]: nc.dram_tensor(n, v.shape, mybir.dt.from_np(v.dtype), kind="ExternalInput").ap()
           for n, v in arrays.items()}
    out = nc.dram_tensor("out_0", inputs["x"].shape, F32, kind="ExternalOutput").ap()
    build_trunk(nc, aps, out)
    r = run_bass_kernel_spmd(nc, [arrays], core_ids=[0])
    return r.results[0]["out_0"]
```
